# Optimizing a Trainium2 kernel written in Bass

```python
import math
import jax, jax.numpy as jnp
from jax import lax
import numpy as np

D_MODEL = 1024
BATCH = 1
SEQ = 256
DEPTH = 2
DEC_BATCH = 1
DEC_SEQ = 32
PAST_LEN = 256

CHUNK = 64
N_EVEN = (DEPTH + 1) // 2
N_ODD = DEPTH // 2
NORM_EPS = 1e-6
CONV_W = 4
DA = 512
NB_A = 8
DBLK_A = DA // NB_A
LRU_C = 8.0
HB = 8
DHB = 64
DB = HB * DHB
N_PREV_CHUNKS = 8
BAND_PAST = N_PREV_CHUNKS * CHUNK
MAX_REL = 128
HC = 8
DK = 128
DV = 128
DCK = HC * DK
DCV = HC * DV
N_QKV = 2 * DCK + DCV
DELTA_CHUNK = 64
N_EXPERTS = 64
TOP_K = 8
N_GROUPS = 8
TOPK_GROUPS = 4
D_EXPERT = 256
D_SHARED = 256
ROUTE_SCALE = 2.5
IN0 = 2 * DA + 3 * DB
IN1 = N_QKV + DCV + 2 * HC

kernel_name = 'hybrid_streaming_encoder_step'

def rmsnorm(x, g):
    xf = x.astype(jnp.float32)
    y = xf * lax.rsqrt(jnp.mean(xf * xf, axis=-1, keepdims=True) + NORM_EPS)
    return (y * g.astype(jnp.float32)).astype(x.dtype)

def l2norm(x):
    xf = x.astype(jnp.float32)
    return xf * lax.rsqrt(jnp.sum(xf * xf, axis=-1, keepdims=True) + NORM_EPS)

def causal_dwconv(x, w, buf):
    T = x.shape[1]
    xp = jnp.concatenate([buf.astype(x.dtype), x], axis=1)
    y = sum(xp[:, j:j + T] * w[j] for j in range(CONV_W))
    return y, xp[:, -(CONV_W - 1):]

def linear_scan(a, b, h0):
    b = b.at[:, 0].add(a[:, 0] * h0)
    def combine(l, r):
        return l[0] * r[0], r[0] * l[1] + r[1]
    _, h = lax.associative_scan(combine, (a, b), axis=1)
    return h

def rglru_branch(xa, ga, conv_w, conv_b, w_r, b_r, w_i, b_i, lam, conv_buf, h0):
    B, T, _ = xa.shape
    xc, new_buf = causal_dwconv(xa, conv_w, conv_buf)
    xc = xc + conv_b
    xb = xc.reshape(B, T, NB_A, DBLK_A)
    gate_r = jnp.einsum('btnd,nde->btne', xb, w_r).reshape(B, T, DA) + b_r
    gate_i = jnp.einsum('btnd,nde->btne', xb, w_i).reshape(B, T, DA) + b_i
    r = jax.nn.sigmoid(gate_r.astype(jnp.float32))
    i = jax.nn.sigmoid(gate_i.astype(jnp.float32))
    log_a = -LRU_C * r * jax.nn.softplus(-lam.astype(jnp.float32))
    a = jnp.exp(log_a)
    u = jnp.sqrt(-jnp.expm1(2.0 * log_a)) * (i * xc.astype(jnp.float32))
    h = linear_scan(a, u, h0.astype(jnp.float32))
    y = h.astype(xa.dtype) * jax.nn.gelu(ga)
    return y, new_buf, h[:, -1].astype(xa.dtype)

def rel_bias(table, q_pos, k_pos):
    rel = jnp.clip(q_pos[:, None] - k_pos[None, :], -MAX_REL, MAX_REL) + MAX_REL
    return jnp.take(table.astype(jnp.float32), rel, axis=1)

def band_attention_prompt(q, k, v, table):
    B, T = q.shape[:2]
    nC = T // CHUNK
    band = (N_PREV_CHUNKS + 1) * CHUNK
    pad = jnp.zeros((B, BAND_PAST, HB, DHB), k.dtype)
    kc = jnp.concatenate([pad, k], axis=1).reshape(B, nC + N_PREV_CHUNKS, CHUNK, HB, DHB)
    vc = jnp.concatenate([pad, v], axis=1).reshape(B, nC + N_PREV_CHUNKS, CHUNK, HB, DHB)
    idx = jnp.arange(nC)[:, None] + jnp.arange(N_PREV_CHUNKS + 1)[None, :]
    kb = kc[:, idx].reshape(B, nC, band, HB, DHB)
    vb = vc[:, idx].reshape(B, nC, band, HB, DHB)
    qc = q.reshape(B, nC, CHUNK, HB, DHB)
    s = jnp.einsum('bcqhd,bckhd->bhcqk', qc, kb).astype(jnp.float32) * DHB ** -0.5
    k_off = jnp.arange(band)
    bias = rel_bias(table, BAND_PAST + jnp.arange(CHUNK), k_off)
    valid = (jnp.arange(nC)[:, None] - N_PREV_CHUNKS) * CHUNK + k_off[None, :] >= 0
    s = jnp.where(valid[None, None, :, None, :], s + bias[None, :, None], -jnp.inf)
    p = jax.nn.softmax(s, axis=-1).astype(v.dtype)
    return jnp.einsum('bhcqk,bckhd->bcqhd', p, vb).reshape(B, T, HB, DHB)

def band_attention_sample(q, k, v, k_cache, v_cache, table):
    P_, T = k_cache.shape[1], q.shape[1]
    kk = jnp.concatenate([k_cache.astype(k.dtype), k], axis=1)
    vv = jnp.concatenate([v_cache.astype(v.dtype), v], axis=1)
    s = jnp.einsum('bqhd,bkhd->bhqk', q, kk).astype(jnp.float32) * DHB ** -0.5
    s = s + rel_bias(table, P_ + jnp.arange(T), jnp.arange(P_ + T))[None]
    p = jax.nn.softmax(s, axis=-1).astype(v.dtype)
    return jnp.einsum('bhqk,bkhd->bqhd', p, vv)

def chunk_gated_delta(q, k, v, g, beta, S0):
    B, T, H, _ = q.shape
    C = DELTA_CHUNK
    n = -(-T // C)
    pad = n * C - T
    def blocks(x):
        x = jnp.pad(x.astype(jnp.float32), [(0, 0), (0, pad)] + [(0, 0)] * (x.ndim - 2))
        x = x.reshape((B, n, C) + x.shape[2:])
        return jnp.moveaxis(jnp.moveaxis(x, 1, 0), 2, 3)
    q, k, v, g, beta = blocks(q), blocks(k), blocks(v), blocks(g), blocks(beta)
    G = jnp.cumsum(g, axis=-1)
    causal = jnp.tril(jnp.ones((C, C), bool))
    strict = jnp.tril(jnp.ones((C, C), bool), -1)
    diff = G[..., :, None] - G[..., None, :]
    L = jnp.where(causal, jnp.exp(jnp.where(causal, diff, 0.0)), 0.0)
    kb = k * beta[..., None]
    M = jnp.where(strict, jnp.einsum('nbhid,nbhjd->nbhij', kb, k) * L, 0.0) + jnp.eye(C, dtype=jnp.float32)
    rhs = jnp.concatenate([v * beta[..., None], kb * jnp.exp(G)[..., None]], axis=-1)
    X = lax.linalg.triangular_solve(M, rhs, left_side=True, lower=True, unit_diagonal=True)
    u, w = X[..., :DV], X[..., DV:]
    A_qk = jnp.einsum('nbhid,nbhjd->nbhij', q, k) * L
    q_dec = q * jnp.exp(G)[..., None]
    k_dec = k * jnp.exp(G[..., -1:] - G)[..., None]
    s_dec = jnp.exp(G[..., -1])
    def step(S, xs):
        u_c, w_c, q_c, a_c, k_c, d_c = xs
        v_new = u_c - jnp.einsum('bhck,bhkv->bhcv', w_c, S)
        o_c = jnp.einsum('bhck,bhkv->bhcv', q_c, S) + jnp.einsum('bhij,bhjv->bhiv', a_c, v_new)
        S = S * d_c[..., None, None] + jnp.einsum('bhck,bhcv->bhkv', k_c, v_new)
        return S, o_c
    S, o = lax.scan(step, S0.astype(jnp.float32), (u, w, q_dec, A_qk, k_dec, s_dec))
    o = jnp.moveaxis(jnp.moveaxis(o, 3, 2), 0, 1).reshape(B, n * C, H, DV)[:, :T]
    return o, S

def even_mixer(h, P, j, a_buf, a_h0, k_cache, v_cache):
    B, T, _ = h.shape
    proj = h @ P['w_in0'][j]
    xa, ga, q, k, v = jnp.split(proj, [DA, 2 * DA, 2 * DA + DB, 2 * DA + 2 * DB], axis=-1)
    ya, a_buf_new, a_h_new = rglru_branch(xa, ga, P['a_conv_w'][j], P['a_conv_b'][j], P['a_w_r'][j], P['a_b_r'][j],
                                          P['a_w_i'][j], P['a_b_i'][j], P['a_lambda'][j], a_buf, a_h0)
    q = q.reshape(B, T, HB, DHB)
    k = k.reshape(B, T, HB, DHB)
    v = v.reshape(B, T, HB, DHB)
    table = P['b_rel_bias'][j]
    if k_cache is None:
        yb = band_attention_prompt(q, k, v, table)
        keep = min(BAND_PAST, T)
        k_new, v_new = k[:, T - keep:], v[:, T - keep:]
    else:
        yb = band_attention_sample(q, k, v, k_cache, v_cache, table)
        k_new, v_new = k, v
    y = jnp.concatenate([ya, yb.reshape(B, T, DB)], axis=-1) @ P['w_out0'][j]
    return y, a_buf_new, a_h_new, k_new, v_new

def odd_mixer(h, P, j, c_buf, S0):
    B, T, _ = h.shape
    f32 = jnp.float32
    proj = h @ P['w_in1'][j]
    qkv, z, a_in, b_in = jnp.split(proj, [N_QKV, N_QKV + DCV, N_QKV + DCV + HC], axis=-1)
    qkv, new_buf = causal_dwconv(qkv, P['c_conv_w'][j], c_buf)
    qkv = jax.nn.silu(qkv)
    q, k, v = jnp.split(qkv, [DCK, 2 * DCK], axis=-1)
    q = l2norm(q.reshape(B, T, HC, DK)) * DK ** -0.5
    k = l2norm(k.reshape(B, T, HC, DK))
    v = v.reshape(B, T, HC, DV)
    g = -jnp.exp(P['c_A_log'][j].astype(f32)) * jax.nn.softplus(a_in.astype(f32) + P['c_dt_bias'][j].astype(f32))
    beta = jax.nn.sigmoid(b_in.astype(f32))
    o, S = chunk_gated_delta(q, k, v, g, beta, S0)
    o = rmsnorm(o, P['c_norm_g'][j]) * jax.nn.silu(z.reshape(B, T, HC, DV).astype(f32))
    y = o.reshape(B, T, DCV).astype(h.dtype) @ P['w_out1'][j]
    return y, new_buf, S.astype(h.dtype)

def moe(h, rw, rb, wg, wu, wd, sg, su, sd):
    B, T, D = h.shape
    xt = h.reshape(B * T, D)
    scores = jax.nn.sigmoid((xt @ rw).astype(jnp.float32))
    sel = scores + rb.astype(jnp.float32)
    grp = sel.reshape(-1, N_GROUPS, N_EXPERTS // N_GROUPS)
    grp_score = jnp.sum(lax.top_k(grp, 2)[0], axis=-1)
    _, gidx = lax.top_k(grp_score, TOPK_GROUPS)
    gmask = jnp.any(gidx[..., None] == jnp.arange(N_GROUPS), axis=-2)
    emask = jnp.repeat(gmask, N_EXPERTS // N_GROUPS, axis=-1)
    _, eidx = lax.top_k(jnp.where(emask, sel, -jnp.inf), TOP_K)
    wsel = jnp.take_along_axis(scores, eidx, axis=-1)
    wsel = wsel / jnp.sum(wsel, axis=-1, keepdims=True) * ROUTE_SCALE
    gates = jnp.sum(jax.nn.one_hot(eidx, N_EXPERTS, dtype=jnp.float32) * wsel[..., None], axis=1)
    def expert_step(acc, xs):
        g_w, u_w, d_w, gate = xs
        hid = jax.nn.silu(xt @ g_w) * (xt @ u_w)
        return acc + gate[:, None].astype(xt.dtype) * (hid @ d_w), None
    acc, _ = lax.scan(expert_step, jnp.zeros_like(xt), (wg, wu, wd, gates.T))
    shared = (jax.nn.silu(xt @ sg) * (xt @ su)) @ sd
    return (acc + shared).reshape(B, T, D)

def run_group(x, c, P, a_conv, a_h, b_k, b_v, c_conv, c_S):
    cond = jax.nn.silu(c)
    nb_k, nb_v, na_c, na_h, nc_c, nc_s = [], [], [], [], [], []
    for l in range(DEPTH):
        mod = cond @ P['w_mod'][l] + P['b_mod'][l]
        sh1, sc1, gt1, sh2, sc2, gt2 = jnp.split(mod[:, None, :], 6, axis=-1)
        h = rmsnorm(x, P['norm1_g'][l]) * (1 + sc1) + sh1
        j = l // 2
        if l % 2 == 0:
            y, ac, ah, bk, bv = even_mixer(h, P, j, a_conv[j], a_h[j],
                                           None if b_k is None else b_k[j], None if b_v is None else b_v[j])
            na_c.append(ac)
            na_h.append(ah)
            nb_k.append(bk)
            nb_v.append(bv)
        else:
            y, cc, cs = odd_mixer(h, P, j, c_conv[j], c_S[j])
            nc_c.append(cc)
            nc_s.append(cs)
        x = x + gt1 * y
        h = rmsnorm(x, P['norm2_g'][l]) * (1 + sc2) + sh2
        x = x + gt2 * moe(h, P['router_w'][l], P['router_bias'][l], P['e_w_gate'][l], P['e_w_up'][l],
                          P['e_w_down'][l], P['s_w_gate'][l], P['s_w_up'][l], P['s_w_down'][l])
    y = rmsnorm(x, P['final_g'])
    return y, (jnp.stack(nb_k), jnp.stack(nb_v), jnp.stack(na_c), jnp.stack(na_h), jnp.stack(nc_c), jnp.stack(nc_s))

def setup_inputs(seed: int = 0) -> dict:
    key = jax.random.key(seed)
    keys = iter(jax.random.split(key, 48))
    f32 = jnp.float32
    def nrm(shape, scale):
        return scale * jax.random.normal(next(keys), shape, f32)
    def gain(shape):
        return 1.0 + nrm(shape, 0.05)
    d = D_MODEL
    past_b = min(BAND_PAST, PAST_LEN)
    u = jax.random.uniform(next(keys), (N_EVEN, DA), f32, 0.9, 0.999)
    a0 = u ** (1.0 / LRU_C)
    a_lambda = jnp.log(a0) - jnp.log1p(-a0)
    dt = jnp.exp(jax.random.uniform(next(keys), (N_ODD, HC), f32, math.log(1e-3), math.log(1e-1)))
    c_dt_bias = dt + jnp.log(-jnp.expm1(-dt))
    c_A_log = jnp.log(jax.random.uniform(next(keys), (N_ODD, HC), f32, 1.0, 16.0))
    return {
        'x_prompt': nrm((BATCH, SEQ, d), 1.0),
        'x_sample': nrm((DEC_BATCH, DEC_SEQ, d), 1.0),
        'c_prompt': nrm((BATCH, d), 1.0),
        'c_sample': nrm((DEC_BATCH, d), 1.0),
        'cache_b_k': nrm((N_EVEN, DEC_BATCH, past_b, HB, DHB), 1.0),
        'cache_b_v': nrm((N_EVEN, DEC_BATCH, past_b, HB, DHB), 1.0),
        'state_a_conv': nrm((N_EVEN, DEC_BATCH, CONV_W - 1, DA), 1.0),
        'state_a_h': nrm((N_EVEN, DEC_BATCH, DA), 0.5),
        'state_c_conv': nrm((N_ODD, DEC_BATCH, CONV_W - 1, N_QKV), 1.0),
        'state_c_S': nrm((N_ODD, DEC_BATCH, HC, DK, DV), 0.1),
        'norm1_g': gain((DEPTH, d)),
        'norm2_g': gain((DEPTH, d)),
        'final_g': gain((d,)),
        'w_mod': nrm((DEPTH, d, 6 * d), 0.5 * d ** -0.5),
        'b_mod': nrm((DEPTH, 6 * d), 0.01),
        'w_in0': nrm((N_EVEN, d, IN0), d ** -0.5),
        'w_out0': nrm((N_EVEN, DA + DB, d), (DA + DB) ** -0.5),
        'a_conv_w': nrm((N_EVEN, CONV_W, DA), 0.5),
        'a_conv_b': nrm((N_EVEN, DA), 0.01),
        'a_w_r': nrm((N_EVEN, NB_A, DBLK_A, DBLK_A), DBLK_A ** -0.5),
        'a_b_r': nrm((N_EVEN, DA), 0.01),
        'a_w_i': nrm((N_EVEN, NB_A, DBLK_A, DBLK_A), DBLK_A ** -0.5),
        'a_b_i': nrm((N_EVEN, DA), 0.01),
        'a_lambda': a_lambda,
        'b_rel_bias': nrm((N_EVEN, HB, 2 * MAX_REL + 1), 0.2),
        'w_in1': nrm((N_ODD, d, IN1), d ** -0.5),
        'w_out1': nrm((N_ODD, DCV, d), DCV ** -0.5),
        'c_conv_w': nrm((N_ODD, CONV_W, N_QKV), 0.5),
        'c_A_log': c_A_log,
        'c_dt_bias': c_dt_bias,
        'c_norm_g': gain((N_ODD, DV)),
        'router_w': nrm((DEPTH, d, N_EXPERTS), d ** -0.5),
        'router_bias': nrm((DEPTH, N_EXPERTS), 0.01),
        'e_w_gate': nrm((DEPTH, N_EXPERTS, d, D_EXPERT), d ** -0.5),
        'e_w_up': nrm((DEPTH, N_EXPERTS, d, D_EXPERT), d ** -0.5),
        'e_w_down': nrm((DEPTH, N_EXPERTS, D_EXPERT, d), D_EXPERT ** -0.5),
        's_w_gate': nrm((DEPTH, d, D_SHARED), d ** -0.5),
        's_w_up': nrm((DEPTH, d, D_SHARED), d ** -0.5),
        's_w_down': nrm((DEPTH, D_SHARED, d), D_SHARED ** -0.5),
    }

def reference(x_prompt, x_sample, c_prompt, c_sample, cache_b_k, cache_b_v, state_a_conv, state_a_h,
              state_c_conv, state_c_S, norm1_g, norm2_g, final_g, w_mod, b_mod, w_in0, w_out0, a_conv_w,
              a_conv_b, a_w_r, a_b_r, a_w_i, a_b_i, a_lambda, b_rel_bias, w_in1, w_out1, c_conv_w, c_A_log,
              c_dt_bias, c_norm_g, router_w, router_bias, e_w_gate, e_w_up, e_w_down, s_w_gate, s_w_up, s_w_down):
    P = dict(norm1_g=norm1_g, norm2_g=norm2_g, final_g=final_g, w_mod=w_mod, b_mod=b_mod, w_in0=w_in0,
             w_out0=w_out0, a_conv_w=a_conv_w, a_conv_b=a_conv_b, a_w_r=a_w_r, a_b_r=a_b_r, a_w_i=a_w_i,
             a_b_i=a_b_i, a_lambda=a_lambda, b_rel_bias=b_rel_bias, w_in1=w_in1, w_out1=w_out1,
             c_conv_w=c_conv_w, c_A_log=c_A_log, c_dt_bias=c_dt_bias, c_norm_g=c_norm_g, router_w=router_w,
             router_bias=router_bias, e_w_gate=e_w_gate, e_w_up=e_w_up, e_w_down=e_w_down,
             s_w_gate=s_w_gate, s_w_up=s_w_up, s_w_down=s_w_down)
    dt = x_prompt.dtype
    bp = x_prompt.shape[0]
    y_prompt, (bk_p, bv_p, ac_p, ah_p, cc_p, cs_p) = run_group(
        x_prompt, c_prompt, P,
        jnp.zeros((N_EVEN, bp, CONV_W - 1, DA), dt), jnp.zeros((N_EVEN, bp, DA), dt), None, None,
        jnp.zeros((N_ODD, bp, CONV_W - 1, N_QKV), dt), jnp.zeros((N_ODD, bp, HC, DK, DV), dt))
    y_sample, (bk_s, bv_s, ac_s, ah_s, cc_s, cs_s) = run_group(
        x_sample, c_sample, P, state_a_conv, state_a_h, cache_b_k, cache_b_v, state_c_conv, state_c_S)
    return (y_prompt, y_sample, bk_p, bk_s, bv_p, bv_s, ac_p, ac_s, ah_p, ah_s, cc_p, cc_s, cs_p, cs_s)


_drawn_inputs = setup_inputs


def setup_inputs(seed=0):
    import zlib

    import numpy as np

    out = dict(_drawn_inputs(seed))
    spreads = {}
    factors = {'a_b_r': 8.0, 'a_b_i': 6.829, 'c_norm_g': 2.797}
    for name, (base, spread) in spreads.items():
        noise = np.random.default_rng([zlib.crc32(name.encode()), seed]).standard_normal(out[name].shape)
        drawn = base * np.exp(spread * noise) if base else spread * noise
        out[name] = __import__('jax').numpy.asarray(drawn.astype(out[name].dtype))
    for name, factor in factors.items():
        out[name] = (out[name] * factor).astype(out[name].dtype)
    return out
```

```python
import numpy as np
import concourse.bass as bass
from concourse import mybir

F32 = mybir.dt.float32
I32 = mybir.dt.int32
ALU = mybir.AluOpType
ACT = mybir.ActivationFunctionType
AX = mybir.AxisListType

D, NP_, NS, T = 1024, 256, 32, 288
KC = D // 128
GROUPS = [(0, NP_), (NP_, T)]
TILES = [(0, 128), (128, 128), (256, 32)]
CH, EPS = 64, 1e-6
HB, DHB, HC = 8, 64, 8
NE, EG, TOPK, DE = 64, 8, 8, 256
CAP = 128
LIM = 4096
XPAD = NP_ + NS + 6
SEG = NP_ + 3
XW = XPAD - 3
UNIT = 2048
NU = 6
LEVELS = [1, 2, 4, 8, 16, 32]

CST_W = dict(ident=128, ones=128, tri=128, same=128, mask=6 * 128, before=128, lower=64, iota=384, tok=3,
             slot=1, eps=2)
SML_W = dict(cond=16, norms=40, bmod=96, aconv=16, aconvb=4, abr=4, abi=4, alam=4, ah0=4, astate=12,
             cconv=96, cstate=72, cnorm=1, alog=8, dtb=8, rb=128, router=1024, wab=128)


def places(widths):
    at, out = 0, {}
    for name, w in widths.items():
        out[name] = (at, at + w)
        at += w
    return out, at


CST, CST_N = places(CST_W)
SML, SML_N = places(SML_W)

MOD_U, IN0_U, OUT0_U, MOE_U, IN1_U = 48, 10, 4, 3 + 3 * NE, 16
U_MOD = 0
U_IN0 = U_MOD + MOD_U
U_OUT0 = U_IN0 + IN0_U
U_MOE0 = U_OUT0 + OUT0_U
U_IN1 = U_MOE0 + MOE_U
U_OUT1 = U_IN1 + IN1_U
U_MOE1 = U_OUT1 + 4
U_MOES = [U_MOE0, U_MOE1]

SEMS = """ld_small ld_att ld_state st_mix st_small st_out w_used cond lamn lame lam sq ss rms h
 proj_ps proj_ev v_ps v_ev pad conv hst gate_ps gate_i lru_a lru_w lru_s lru_g ya
 s_ps s_sm p_exp p_nrm pt_ps pt_sb pv_ps pv_sb out_ps out_x
 tm_ps tm_sb h2_st lg_ps lgz xgz score mask rank_ps flag rowi sel sel_ps idx
 shu_ps shu_sb shh sht_ps sht_sb shd_ps shd_sb
 ig isx xg0 xg1 trx xta xtb up sg hd trh ht dn ya_e yb_e ysc0 ysc1 got0 got1 got2 got3 cb acc_ps acc_x
 ab_ps ab_act ab_sb ab_e gcum_ps gcum_e gdec
 padc cc cacc csilu lsq lss lrms qk_n gb_ps gb_e ldif lexp nmat kk_ps tk_ps tk_sb um
 y_ps y_sb z_ps xd u_ps batch s0 ws_ps vn o_ps su_ps s_new o_sb osq oss orms on ozs
 dve act pool passed passed_d""".split()
OVF = """od ovi ovd ova ovp og osc ow osel osel_ps""".split()


def build(nc, t):
    sem = {n: nc.alloc_semaphore(n) for n in SEMS}
    for l in range(2):
        for n in OVF:
            sem[f"{n}{l}"] = nc.alloc_semaphore(f"{n}{l}")
    w_loaded = [nc.alloc_semaphore(f"w_loaded{u}") for u in range(NU)]

    def sb(name, shape, dt=F32):
        return nc.alloc_sbuf_tensor(name, shape, dt)

    ring = sb("ring", [128, NU, UNIT])
    cst = sb("cst", [128, CST_N])
    sml = sb("sml", [128, SML_N])
    x = sb("x", [128, KC, T])
    h = sb("h", [128, KC, T])
    ycat = sb("ycat", [128, KC, T])
    rms = sb("rms", [128, T])
    condT = sb("condT", [128, KC, 2])
    mod = sb("mod", [128, 2, 48, 2])
    scale1 = sb("scale1", [128, 2, 2, KC, 2])
    hst = sb("hst", [128, 4, 2])
    cst3 = sb("cst3", [128, 4, 2, 3])
    cc3 = sb("cc3", [128, 24, 2, 3])
    arena = sb("arena", [128, 29400])
    ps = [nc.alloc_psum_tensor(f"ps{b}", [128, 512], F32) for b in range(8)]

    def C(name, p=128):
        return cst[0:p, CST[name][0]:CST[name][1]]

    def M(name, p=128):
        return sml[0:p, SML[name][0]:SML[name][1]]

    def carver(at):

        def carve(*dims):
            n = int(np.prod(dims))
            a = arena[:, at[0]:at[0] + n]
            at[0] += n
            assert at[0] <= 29400, at[0]
            if len(dims) == 2:
                a = a.rearrange("p (a b) -> p a b", a=dims[0])
            if len(dims) == 3:
                a = a.rearrange("p (a b c) -> p a b c", a=dims[0], b=dims[1])
            return a
        return carve

    ident, ones = C("ident"), C("ones")

    place = [0]
    cv = carver(place)
    xpad, gaT, qT, kT = cv(4, XPAD), cv(4, T), cv(4, T), cv(4, T)
    ksT = cv(4, T)
    vtm, vcache = cv(3, 512), cv(2, 512)
    biasP0, biasP1, biasS = cv(HB, 128), cv(HB, 256), cv(HB, T)
    bdr, bdi = cv(4, 128), cv(4, 128)
    xc, rg, ig_, aa, tt_ = (cv(4, XW) for _ in range(5))
    hh = cv(4, XW)
    lamw = cv(8, 4)
    s_sb, mx, rsum = cv(2, T), cv(2, 2), cv(2, 1)
    pT = cv(2, 3, 128)

    place = [0]
    cv = carver(place)
    qf, kf, vf, zf = (cv(HC, T) for _ in range(4))
    kdec = cv(3, HC, 128)
    share = cv(1, 5400)[:, 0, :]
    uu = share[:, 0:3072].rearrange("p (t h v) -> p t h v", t=3, h=HC)
    atm = share[:, 3072:3072 + 2304]
    raw = share[:, 0:2 * 4 * XPAD].rearrange("p (a c x) -> p a c x", a=2, c=4)
    cacc = share[:, 2400:2400 + 2 * 4 * XW].rearrange("p (a c x) -> p a c x", a=2, c=4)
    sst = cv(2, HC, 128)
    lbuf = cv(2, 512)
    SQ0 = place[0]
    nbuf, xbuf, dbuf, ybuf, ubuf, kbe, vbe, egb = (cv(2, 512) for _ in range(8))
    sqb = arena[:, SQ0:SQ0 + 16 * T].rearrange("p (c x) -> p c x", c=16)
    kdcol = cv(3, 8)
    gtm, btm, spt, gcol, glast, begc = (cv(3, 8) for _ in range(6))
    spw = cv(6, 24)
    sdec = cv(5, HC)

    def att(t):
        P = TILES[t][1]
        return atm[:, t * 1024:t * 1024 + HC * P].rearrange("p (h i) -> p h i", h=HC)

    def four(buf, P):
        return buf[:, 0:4 * P].rearrange("p (h i) -> p h i", h=4)

    place = [0]
    cv = carver(place)
    ysh = cv(3, D)
    xgb, yb = cv(2, D), cv(2, D)
    xgT = cv(2, KC, CAP)
    gb = cv(4, D)
    selb = cv(2, 3, 8 * CAP)
    silu_b, hid = cv(1, DE)[:, 0, :], cv(1, DE)[:, 0, :]
    hidT = cv(2, CAP)
    shs, shu_, shh_, shT = cv(3, DE), cv(3, DE), cv(3, DE), cv(3, 2, 128)
    lg, score, selv, msk, gates, rk, tmp1, tmp2 = (cv(3, NE) for _ in range(8))
    top2, gsc, gcmp, geq, grk, top8, gsum = cv(3, 8, 8), cv(3, 8), cv(3, 8, 8), cv(3, 8, 8), cv(3, 8), cv(3, 8), cv(3, 1)
    tg = cv(3, NE, 2)
    idxf = cv(2, NE)
    rowif = cv(3, 8)
    cntf, start, srow = cv(1, 66)[:, 0, :], cv(1, NE)[:, 0, :], cv(1, NE)[:, 0, :]
    rowi = cv(3, 8).bitcast(I32)
    idx = cv(NE, 3).bitcast(I32)
    icg = cv(2, 2).bitcast(I32)
    ics = cv(2, 1).bitcast(I32)
    ico = cv(1, 3)[:, 0, :].bitcast(I32)
    flagi = sb("flagi", [1, 1], I32)

    H2, Y = t["H2"], t["Y"]

    class Chain:

        def __init__(self, eng, own):
            self.eng, self.own, self.n = eng, own, {}

        def go(self, ins, name=None):
            name = name or self.own
            self.n[name] = self.n.get(name, 0) + 1
            ins.then_inc(sem[name], 1)
            self.last = name

        def __call__(self, ins, name=None):
            self.go(ins, name)
            self.eng.wait_ge(sem[self.last], self.n[self.last])

    def unit(n):
        return ring[:, n % NU, :]

    def wait_unit(eng, n):
        eng.wait_ge(w_loaded[n % NU], 16 * (n // NU + 1))

    with nc.Block() as block:
        @block.sync
        def _(sp):
            def used(n):
                if n < U_IN0:
                    return "w_used", n + 1
                if n < U_OUT0:
                    q = n - U_IN0
                    return ("proj_ps", 2 * q + 2) if q < 8 else ("v_ps", q - 7)
                if n < U_MOE0:
                    return "out_ps", 2 * (n - U_OUT0) + 2
                if U_IN1 <= n < U_OUT1:
                    return "proj_ps", 16 + 2 * (n - U_IN1) + 2
                if U_OUT1 <= n < U_MOE1:
                    return "out_ps", 8 + 2 * (n - U_OUT1) + 2
                l = 0 if n < U_IN1 else 1
                m, B = n - U_MOES[l], NE * l
                if m < 2:
                    return "shu_ps", 2 * l + m + 1
                if m == 2:
                    return "shd_ps", 3 * l + 3
                if m < 5:
                    return "up", B + 1
                if m == MOE_U - 1:
                    return "dn", B + NE
                e, r = (m - 5) // 3 + 1, (m - 5) % 3
                return ("up", B + e + 1) if r < 2 else ("dn", B + e)

            def load(n, src, i=None, per=0):
                if n >= NU:
                    name, v = used(n - NU)
                    sp.wait_ge(sem[name], v if i is None else i * per + v)
                sp.dma_start(ring[:, n % NU, :], src).then_inc(w_loaded[n % NU], 16)

            def at(w, i, k, n):
                return w[bass.ds(i * k + n, 1), :, :].rearrange("a p n -> p (a n)")

            for n in range(NU):
                load(n, t["wmod"][n, :, :])
            with sp.Fori(0, MOD_U // NU - 1) as i:
                for u in range(NU):
                    load(NU + u, at(t["wmod"], i, NU, NU + u), i, NU)
            for n in range(IN0_U):
                load(U_IN0 + n, t["win0"][n, :, :])
            for n in range(4):
                load(U_OUT0 + n, t["wout0"][n, :, :])

            def moe_loads(l):
                b, w = U_MOES[l], t["wexp"]
                W0 = l * (NE + 1) * 3
                for n in range(3):
                    load(b + n, w[W0 + 3 * NE + n, :, :])
                for n in range(2):
                    load(b + 3 + n, w[W0 + n, :, :])

                def pair(e0, i=None):
                    for n, j in enumerate((3 * e0, 3 * e0 + 1, 3 * e0 - 1)):
                        m = b + 5 + 3 * (e0 - 1) + n
                        load(m, w[W0 + j, :, :] if i is None else at(w, i, 6, W0 + j), i, 2)

                pair(1)
                pair(2)
                with sp.Fori(0, (NE - 4) // 2) as i:
                    pair(3, i)
                    pair(4, i)
                pair(NE - 1)
                load(b + MOE_U - 1, w[W0 + 3 * NE - 1, :, :])
                sp.wait_ge(sem["flag"], l + 1)
                more = sp.value_load(flagi[0:1, 0:1], min_val=0, max_val=1)
                with sp.If(more > 0):
                    sp.wait_ge(sem["dn"], NE * (l + 1))
                    with sp.Fori(0, 2) as bb:
                        with sp.Fori(0, NE) as e:
                            sp.wait_ge(sem[f"od{l}"], bb * NE + e + 1)
                            for n in range(3):
                                sp.dma_start(ring[:, n, :], at(w, e, 3, W0 + n)).then_inc(sem[f"ow{l}"], 16)
                    sp.wait_ge(sem[f"od{l}"], 2 * NE + 1)

            moe_loads(0)
            for n in range(IN1_U):
                load(U_IN1 + n, t["win1"][n, :, :])
            for n in range(4):
                load(U_OUT1 + n, t["wout1"][n, :, :])
            moe_loads(1)
            sp.wait_ge(sem["h"], 5)
            sp.dma_start(t["y"], h[:, :, :]).then_inc(sem["st_out"], 16)
            sp.wait_ge(sem["st_out"], 16)
            sp.wait_ge(sem["st_mix"], 16 * 4)
            sp.wait_ge(sem["st_small"], 16 * 5)

        @block.tensor
        def _(pe):
            mm = nc.tensor.matmul
            tr = nc.tensor.transpose

            pe.wait_ge(sem["cond"], 1)
            for l in range(2):
                with pe.Fori(0, MOD_U // NU // 2) as i:
                    for u in range(NU):
                        n = l * (MOD_U // 2) + u
                        pe.wait_ge(w_loaded[u], i * 16 + 16 * (n // NU + 1))
                        for a in range(2):
                            for k in range(KC):
                                last = mm(ps[l][:, bass.ds(i * (4 * NU) + (4 * u + 2 * a), 2)],
                                          ring[:, u, (a * KC + k) * 128:(a * KC + k + 1) * 128],
                                          condT[:, k, :], start=(k == 0), stop=(k == KC - 1))
                        last.then_inc(sem["w_used"], 1)

            def sum_squares(k):
                pe.wait_ge(sem["sq"], k + 1)
                for c in range(KC):
                    last = mm(ps[7][:, 0:T], ones, h[:, c, :], start=(c == 0), stop=(c == KC - 1))
                last.then_inc(sem["ss"], 1)

            def project(u0, tiles, base, rhs, rdy):
                for i in range(tiles):
                    n = u0 + i // 2
                    if i % 2 == 0:
                        wait_unit(pe, n)
                    if base + i >= 4:
                        pe.wait_ge(sem[rdy], base + i - 3)
                    for k in range(KC):
                        a = (i % 2) * KC + k
                        last = mm(ps[i % 4][:, 0:T], unit(n)[:, a * 128:(a + 1) * 128], rhs[:, k, :],
                                  start=(k == 0), stop=(k == KC - 1))
                    last.then_inc(sem["proj_ps" if rdy == "proj_ev" else "out_ps"], 1)

            sum_squares(0)
            pe.wait_ge(sem["h"], 1)
            project(U_IN0, 16, 0, h, "proj_ev")
            for kq in range(2):
                wait_unit(pe, U_IN0 + 8 + kq)
                for j, (t0, P) in enumerate(TILES):
                    for k in range(4):
                        last = mm(ps[4 + j][0:P, :], h[:, kq * 4 + k, t0:t0 + P],
                                  unit(U_IN0 + 8 + kq)[:, k * 512:(k + 1) * 512],
                                  start=(kq == 0 and k == 0), stop=(kq == 1 and k == 3))
                last.then_inc(sem["v_ps"], 1)
            pe.wait_ge(sem["ld_att"], 16 * 9)
            pe.wait_ge(sem["conv"], 1)
            pe.wait_ge(sem["proj_ev"], 16)
            for c in range(4):
                last = mm(ps[c][:, 0:XW], bdr[:, c, :], xc[:, c, :], start=True, stop=True)
            last.then_inc(sem["gate_ps"], 1)
            pe.wait_ge(sem["v_ev"], 1)
            for c in range(4):
                last = mm(ps[4 + c][:, 0:XW], bdi[:, c, :], xc[:, c, :], start=True, stop=True)
            last.then_inc(sem["gate_ps"], 1)
            units = [(j, hd) for j in range(3) for hd in range(HB)]

            def scores(n):
                j, hd = units[n]
                t0, P = TILES[j]
                b, c = DHB * (hd % 2), hd // 2
                nk = (128, 256, T)[j]
                keys = ksT if j == 2 else kT
                if n >= 2:
                    pe.wait_ge(sem["s_sm"], n - 1)
                mm(ps[n % 2][0:P, 0:nk], qT[b:b + DHB, c, t0:t0 + P], keys[b:b + DHB, c, 0:nk],
                   start=True, stop=True).then_inc(sem["s_ps"], 1)

            pe.wait_ge(sem["gate_i"], 1)
            scores(0)
            for n, (j, hd) in enumerate(units):
                t0, P = TILES[j]
                if n + 1 < len(units):
                    scores(n + 1)
                kts = [(0, 128)] if j == 0 else [(0, 128), (1, 128)] if j == 1 else [(0, 128), (1, 128), (2, 32)]
                pe.wait_ge(sem["p_nrm"], n + 1)
                if n >= 2:
                    pe.wait_ge(sem["pt_sb"], n - 1)
                for kt, K in kts:
                    last = tr(ps[2 + n % 2][0:K, kt * 128:kt * 128 + P],
                              s_sb[0:P, n % 2, kt * 128:kt * 128 + K], ident[0:P, 0:P])
                last.then_inc(sem["pt_ps"], 1)
                pe.wait_ge(sem["pt_sb"], n + 1)
                if n >= 2:
                    pe.wait_ge(sem["pv_sb"], n - 1)
                c = hd // 2
                for kt, K in kts:
                    val = vcache if (j == 2 and kt < 2) else vtm
                    last = mm(ps[4 + n % 2][:, 0:P], val[0:K, kt, c * 128:(c + 1) * 128], pT[0:K, n % 2, kt, 0:P],
                              start=(kt == 0), stop=(kt == kts[-1][0]))
                last.then_inc(sem["pv_ps"], 1)
            pe.wait_ge(sem["ya"], 1)
            pe.wait_ge(sem["pv_sb"], len(units))
            project(U_OUT0, 8, 0, ycat, "out_x")

            def moe(l):
                B, u0 = NE * l, U_MOES[l]
                pe.wait_ge(sem["h"], 2 * l + 2)
                for j, (t0, P) in enumerate(TILES):
                    for k in range(KC):
                        rw = M("router")[:, l * 512 + k * 64:l * 512 + (k + 1) * 64]
                        last = mm(ps[6][0:P, j * 64:(j + 1) * 64], h[:, k, t0:t0 + P], rw,
                                  start=(k == 0), stop=(k == KC - 1))
                last.then_inc(sem["lg_ps"], 1)
                for j, (t0, P) in enumerate(TILES):
                    for k in range(KC):
                        last = tr(ps[2 * j + k // 4][0:P, (k % 4) * 128:(k % 4 + 1) * 128], h[:, k, t0:t0 + P], ident)
                    last.then_inc(sem["tm_ps"], 1)
                pe.wait_ge(sem["tm_sb"], 3 * (l + 1))
                for q in range(2):
                    wait_unit(pe, u0 + q)
                    for j, (t0, P) in enumerate(TILES):
                        for k in range(4):
                            last = mm(ps[j][0:P, :], h[:, 4 * q + k, t0:t0 + P],
                                      unit(u0 + q)[:, k * 512:(k + 1) * 512],
                                      start=(q == 0 and k == 0), stop=(q == 1 and k == 3))
                    last.then_inc(sem["shu_ps"], 1)
                for j, (t0, P) in enumerate(TILES):
                    pe.wait_ge(sem["shh"], 3 * l + j + 1)
                    for a in range(2):
                        last = tr(ps[3][:, a * 128:a * 128 + P], shh_[0:P, j, a * 128:(a + 1) * 128],
                                  ident[0:P, 0:P])
                    last.then_inc(sem["sht_ps"], 1)
                    pe.wait_ge(sem["sht_sb"], 3 * l + j + 1)
                for j, (t0, P) in enumerate(TILES):
                    if j == 0:
                        wait_unit(pe, u0 + 2)
                        pe.wait_ge(sem["shu_sb"], 3 * (l + 1))
                    b0, b1 = ((0, 1), (4, 5), (2, 3))[j]
                    for hf, bk in ((0, b0), (1, b1)):
                        for a in range(2):
                            last = mm(ps[bk][0:P, :], shT[:, j, a, 0:P],
                                      unit(u0 + 2)[:, a * D + hf * 512:a * D + (hf + 1) * 512],
                                      start=(a == 0), stop=(a == 1))
                    last.then_inc(sem["shd_ps"], 1)
                pe.wait_ge(sem["mask"], l + 1)
                for j, (t0, P) in enumerate(TILES):
                    for jj in range(j + 1):
                        PP = TILES[jj][1]
                        w = C("before")[0:PP, 0:P] if jj == j else ones[0:PP, 0:P]
                        last = mm(ps[7][0:P, j * 64:(j + 1) * 64], w, msk[0:PP, jj, :], start=(jj == 0), stop=(jj == j))
                for jj, (t0, PP) in enumerate(TILES):
                    last = mm(ps[7][:, 192:256], ones[0:PP, :], msk[0:PP, jj, :], start=(jj == 0), stop=(jj == 2))
                last.then_inc(sem["rank_ps"], 1)

                def slot_tables(sel_name, ps_name, base):
                    for g in range(8):
                        pe.wait_ge(sem[sel_name], base + g + 1)
                        for e in range(8):
                            for j, (t0, P) in enumerate(TILES):
                                last = mm(ps[6][:, (8 * g + e) * 2:(8 * g + e) * 2 + 2],
                                          selb[0:P, g % 2, j, e * CAP:(e + 1) * CAP], tg[0:P, j, 8 * g + e, :],
                                          start=(j == 0), stop=(j == 2))
                        last.then_inc(sem[ps_name], 1)

                slot_tables("sel", "sel_ps", 8 * l)

                pe.wait_ge(sem["shd_sb"], 3 * (l + 1))

                def take(e, p):
                    pe.wait_ge(sem[f"xg{p}"], e * 8 + (8 * (B - p) + 16))
                    for k in range(KC):
                        last = tr(ps[4 + k // 4][:, (k % 4) * 128:(k % 4 + 1) * 128], xgb[:, p, k * 128:(k + 1) * 128],
                                  ident)
                    last.then_inc(sem["trx"], 1)

                def up(e, p, n, i):
                    for q in range(2):
                        s = (n + q) % NU
                        v = 16 * ((n + q) // NU + 1)
                        pe.wait_ge(w_loaded[s], v if i is None else i * 16 + v)
                        for k in range(4):
                            last = mm(ps[2][:, :], xgT[:, p, 4 * q + k, :], ring[:, s, k * 512:(k + 1) * 512],
                                      start=(q == 0 and k == 0), stop=(q == 1 and k == 3))
                    last.then_inc(sem["up"], 1)

                def hidden(e):
                    pe.wait_ge(sem["hd"], e + (B + 1))
                    for a in range(2):
                        last = tr(ps[3][:, a * 128:(a + 1) * 128], hid[:, a * 128:(a + 1) * 128], ident)
                    last.then_inc(sem["trh"], 1)

                def down(e, n, i, first=False):
                    pe.wait_ge(sem["ht"], e + (B + 1))
                    if not first:
                        pe.wait_ge(sem["ya_e"], e + B)
                        pe.wait_ge(sem["yb_e"], e + B)
                    s, v = n % NU, 16 * (n // NU + 1)
                    pe.wait_ge(w_loaded[s], v if i is None else i * 16 + v)
                    for a in range(2):
                        for hf in range(2):
                            last = mm(ps[hf][:, :], hidT[:, a, :], ring[:, s, a * D + hf * 512:a * D + (hf + 1) * 512],
                                      start=(a == 0), stop=(a == 1))
                    last.then_inc(sem["dn"], 1)

                take(0, 0)

                def step(e0, i=None):
                    e = e0 if i is None else i * 2 + e0
                    n = u0 + 3 + (0 if e0 == 0 else 2 + 3 * (e0 - 1))
                    if e0 > 0:
                        hidden(e - 1)
                    if e0 + 1 < NE:
                        pe.wait_ge(sem["xta"], e + (B + 1))
                        pe.wait_ge(sem["xtb"], e + (B + 1))
                        take(e + 1, (e0 + 1) % 2)
                    else:
                        pe.wait_ge(sem["xta"], e + (B + 1))
                        pe.wait_ge(sem["xtb"], e + (B + 1))
                    up(e, e0 % 2, n, i)
                    if e0 > 0:
                        down(e - 1, n + 2, i, first=(e0 == 1))

                for e in range(3):
                    step(e)
                with pe.Fori(0, (NE - 6) // 2) as i:
                    step(3, i)
                    step(4, i)
                for e in range(NE - 3, NE):
                    step(e)
                hidden(NE - 1)
                down(NE - 1, u0 + 3 + 2 + 3 * (NE - 1), None)

                pe.wait_ge(sem["flag"], l + 1)
                more = pe.value_load(flagi[0:1, 0:1], min_val=0, max_val=1)
                with pe.If(more > 0):
                    s = lambda n: sem[f"{n}{l}"]
                    pe.wait_ge(sem["ya_e"], B + NE)
                    pe.wait_ge(sem["yb_e"], B + NE)
                    with pe.Fori(0, 2) as bb:
                        for g in range(8):
                            pe.wait_ge(s("osel"), bb * 8 + (g + 1))
                            for e in range(8):
                                for j, (t0, P) in enumerate(TILES):
                                    last = mm(ps[6][:, (8 * g + e) * 2:(8 * g + e) * 2 + 2],
                                              selb[0:P, g % 2, j, e * CAP:(e + 1) * CAP], tg[0:P, j, 8 * g + e, :],
                                              start=(j == 0), stop=(j == 2))
                            last.then_inc(s("osel_ps"), 1)
                        with pe.Fori(0, NE) as e:
                            J = bb * NE + e
                            pe.wait_ge(s("og"), J * 16 + 16)
                            for k in range(KC):
                                last = tr(ps[4 + k // 4][:, (k % 4) * 128:(k % 4 + 1) * 128],
                                          xgb[:, 0, k * 128:(k + 1) * 128], ident)
                            last.then_inc(s("ovp"), 1)
                            pe.wait_ge(s("ova"), J * 4 + 1)
                            pe.wait_ge(s("ow"), J * 48 + 48)
                            for k in range(KC):
                                last = mm(ps[2][:, :], xgT[:, 0, k, :],
                                          ring[:, k // 4, (k % 4) * 512:(k % 4 + 1) * 512],
                                          start=(k == 0), stop=(k == KC - 1))
                            last.then_inc(s("ovp"), 1)
                            pe.wait_ge(s("ovd"), J * 2 + 2)
                            for a in range(2):
                                last = tr(ps[3][:, a * 128:(a + 1) * 128], hid[:, a * 128:(a + 1) * 128], ident)
                            last.then_inc(s("ovp"), 1)
                            pe.wait_ge(s("ova"), J * 4 + 3)
                            for a in range(2):
                                for hf in range(2):
                                    last = mm(ps[hf][:, :], hidT[:, a, :],
                                              ring[:, 2, a * D + hf * 512:a * D + (hf + 1) * 512],
                                              start=(a == 0), stop=(a == 1))
                            last.then_inc(s("ovp"), 1)
                    pe.wait_ge(s("ova"), 8 * NE)
                pe.wait_ge(sem["ya_e"], B + NE)
                pe.wait_ge(sem["yb_e"], B + NE)
                for j, (t0, P) in enumerate(TILES):
                    pe.wait_ge(sem["cb"], 24 * l + 8 * (j + 1))
                    for k in range(KC):
                        last = tr(ps[2 * j + k // 4][:, (k % 4) * 128:(k % 4) * 128 + P],
                                  ysh[0:P, j, k * 128:(k + 1) * 128], ident[0:P, 0:P])
                    last.then_inc(sem["acc_ps"], 1)

            sum_squares(1)
            moe(0)

            sum_squares(2)
            pe.wait_ge(sem["h"], 3)
            for j, (t0, P) in enumerate(TILES):
                for k in range(KC):
                    last = mm(ps[6][0:P, j * 16:(j + 1) * 16], h[:, k, t0:t0 + P], M("wab")[:, k * 16:(k + 1) * 16],
                              start=(k == 0), stop=(k == KC - 1))
            last.then_inc(sem["ab_ps"], 1)
            pe.wait_ge(sem["acc_x"], 1)
            project(U_IN1, 32, 16, h, "proj_ev")
            pe.wait_ge(sem["ab_sb"], 1)
            for j, (t0, P) in enumerate(TILES):
                mm(ps[6][0:P, 64 + j * 8:72 + j * 8], C("tri")[0:P, 0:P], gtm[0:P, j, :], start=True, stop=True)
                last = mm(ps[6][0:P, 96 + j * 8:104 + j * 8], C("same")[0:P, 0:P], gtm[0:P, j, :],
                          start=True, stop=True)
            last.then_inc(sem["gcum_ps"], 1)
            pe.wait_ge(sem["proj_ev"], 48)
            for n in range(16):
                pe.wait_ge(sem["lsq"], n // 4 + 1)
                if n >= 4:
                    pe.wait_ge(sem["lrms"], n - 3)
                mm(ps[n % 4][:, 0:T], ones, sqb[:, n, :], start=True, stop=True).then_inc(sem["lss"], 1)

            batches = [(j, g) for j in range(3) for g in range(2)]
            for n, (j, g) in enumerate(batches):
                t0, P = TILES[j]
                hs = range(4 * g, 4 * g + 4)
                blk = lambda b: ps[b][:, 0:4 * P].rearrange("p (h i) -> p h i", h=4)
                if n:
                    pe.wait_ge(sem["batch"], n)
                else:
                    pe.wait_ge(sem["qk_n"], 16)
                    pe.wait_ge(sem["gdec"], 1)
                for a, hd in enumerate(hs):
                    last = mm(blk(0)[:, a, :], gtm[0:P, j, hd:hd + 1].broadcast_to([P, 128]), C("tri")[0:P, 0:P],
                              start=True, stop=True)
                last.then_inc(sem["gb_ps"], 1)
                for a, hd in enumerate(hs):
                    last = mm(blk(1)[0:P, a, :], btm[0:P, j, hd:hd + 1].broadcast_to([P, P]), ident[0:P, 0:P],
                              start=True, stop=True)
                for a, hd in enumerate(hs):
                    last = mm(blk(2)[0:P, a, :], kf[:, hd, t0:t0 + P], kf[:, hd, t0:t0 + P], start=True, stop=True)
                for a, hd in enumerate(hs):
                    last = mm(blk(3)[0:P, a, :], kf[:, hd, t0:t0 + P], qf[:, hd, t0:t0 + P], start=True, stop=True)
                last.then_inc(sem["kk_ps"], 1)
                for a, hd in enumerate(hs):
                    tr(ps[4][0:P, a * 128:(a + 1) * 128], kf[:, hd, t0:t0 + P], ident)
                    last = tr(ps[5][0:P, a * 128:(a + 1) * 128], vf[:, hd, t0:t0 + P], ident)
                last.then_inc(sem["tk_ps"], 1)
                levels = LEVELS if P == 128 else LEVELS[:5]
                done = sum(6 if TILES[jj][1] == 128 else 5 for jj, _ in batches[:n])
                u_ = lambda buf: four(buf, P)
                for s_, sz in enumerate(levels):
                    m = done + s_
                    pe.wait_ge(sem["um"], m + 1)
                    pe.wait_ge(sem["xd"], m + n + 1)
                    for a in range(4):
                        last = mm(blk(6)[0:P, a, :], u_(ubuf[:, m % 2, :])[0:P, a, :], u_(dbuf[:, 0, :])[0:P, a, :],
                                  start=True, stop=True)
                    last.then_inc(sem["y_ps"], 1)
                    pe.wait_ge(sem["y_sb"], m + 1)
                    for a in range(4):
                        mm(blk(0)[0:P, a, :], u_(xbuf[:, 0, :])[0:P, a, :], u_(ybuf[:, 0, :])[0:P, a, :],
                           start=True, stop=True)
                    for a in range(4):
                        last = mm(blk(1)[0:P, a, :], u_(ybuf[:, 0, :])[0:P, a, :], u_(xbuf[:, 0, :])[0:P, a, :],
                                  start=True, stop=True)
                    last.then_inc(sem["z_ps"], 1)
                pe.wait_ge(sem["xd"], done + len(levels) + n + 1)
                pe.wait_ge(sem["tk_sb"], n + 1)
                for a in range(4):
                    mm(ps[2][0:P, a * 128:(a + 1) * 128], u_(xbuf[:, 0, :])[0:P, a, :], vbe[0:P, 0, a * 128:(a + 1) * 128],
                       start=True, stop=True)
                for a in range(4):
                    last = mm(blk(3)[:, a, :], kbe[0:P, 0, a * 128:(a + 1) * 128], u_(xbuf[:, 0, :])[0:P, a, :],
                              start=True, stop=True)
                last.then_inc(sem["u_ps"], 1)

            pe.wait_ge(sem["batch"], 6)
            pe.wait_ge(sem["s0"], 1)
            pe.wait_ge(sem["ld_state"], 16)
            for n in range(10):
                c, g = n // 2, n % 2
                j = c // 2
                t0, P = TILES[j]
                r0, R = (64 * (c % 2), 64) if c < 4 else (0, 32)
                st = sst[:, 0 if c < 4 else 1, :, :]
                wb, ob_, sbk = (0, 1, 2) if n % 2 == 0 else (3, 4, 5)
                if n >= 2:
                    pe.wait_ge(sem["o_sb"], n - 1)
                    pe.wait_ge(sem["s_new"], n - 1)
                for a in range(4):
                    hd = 4 * g + a
                    last = mm(ps[wb][0:P, a * 128:(a + 1) * 128], h[:, hd, t0:t0 + P], st[:, hd, :], start=True, stop=True)
                last.then_inc(sem["ws_ps"], 1)
                pe.wait_ge(sem["vn"], n + 1)
                ob = ps[ob_][:, 0:4 * R].rearrange("p (h i) -> p h i", h=4)
                for a in range(4):
                    hd = 4 * g + a
                    mm(ob[:, a, :], st[:, hd, :], qf[:, hd, t0 + r0:t0 + r0 + R], start=True, stop=False)
                    last = mm(ob[:, a, :], uu[r0:r0 + R, j, hd, :], att(j)[r0:r0 + R, hd, r0:r0 + R],
                              start=False, stop=True)
                last.then_inc(sem["o_ps"], 1)
                for a in range(4):
                    hd = 4 * g + a
                    last = mm(ps[sbk][:, a * 128:(a + 1) * 128], kdec[r0:r0 + R, j, hd, :], uu[r0:r0 + R, j, hd, :],
                              start=True, stop=True)
                last.then_inc(sem["su_ps"], 1)
            for n in range(8):
                pe.wait_ge(sem["osq"], 1)
                if n >= 4:
                    pe.wait_ge(sem["orms"], n - 3)
                mm(ps[4 + n % 4][:, 0:T], ones, vf[:, n, :], start=True, stop=True).then_inc(sem["oss"], 1)
            pe.wait_ge(sem["ozs"], 1)
            project(U_OUT1, 8, 8, ycat, "out_x")
            sum_squares(3)
            moe(1)
            sum_squares(4)

        @block.scalar
        def _(act):
            A = nc.scalar.activation
            L = Chain(act, "act")
            for dst, src in ((sml[:, :], t["small"]), (cst[:, :], t["const"]), (x[:, :, :], t["x"])):
                act.dma_start(dst, src).then_inc(sem["ld_small"], 16)
            act.dma_start(biasP0, t["biasP0"]).then_inc(sem["ld_att"], 16)
            act.dma_start(biasP1, t["biasP1"]).then_inc(sem["ld_att"], 16)
            act.dma_start(biasS[0:NS], t["biasS"]).then_inc(sem["ld_att"], 16)
            act.dma_start(ksT[:, :, 0:NP_], t["kcache"]).then_inc(sem["ld_att"], 16)
            act.dma_start(vcache, t["vcache"]).then_inc(sem["ld_att"], 16)
            act.wait_ge(sem["pad"], 1)
            for hf in range(2):
                for dst, src in ((bdr, t["wr"]), (bdi, t["wi"])):
                    act.dma_start(dst[64 * hf:64 * hf + 64, :, 64 * hf:64 * hf + 64],
                                  src[:, hf, :, :]).then_inc(sem["ld_att"], 16)
            act.wait_ge(sem["ld_small"], 48)
            L(A(condT[:, :, :], M("cond").rearrange("p (k g) -> p k g", g=2), ACT.Silu), "cond")
            act.wait_ge(sem["lamn"], 1)
            L(A(lamw[:, 1, :], lamw[:, 0, :], ACT.Exp), "lame")

            def norm_root(k):
                act.wait_ge(sem["ss"], k + 1)
                if k:
                    act.wait_ge(sem["h"], k)
                L(A(rms[:, :], ps[7][:, 0:T], ACT.Sqrt, scale=1.0 / D, bias=C("eps")[:, 0:1]), "rms")

            norm_root(0)
            for i in range(16):
                act.wait_ge(sem["proj_ps"], i + 1)
                src, c = ps[i % 4], i % 4
                if i < 4:
                    (A(xpad[:, c, 3:3 + NP_], src[:, 0:NP_], ACT.Copy))
                    A(xpad[:, c, SEG + 3:SEG + 3 + NS], src[:, NP_:T], ACT.Copy).then_inc(sem["proj_ev"], 1)
                elif i < 8:
                    A(gaT[:, c, :], src[:, 0:T], ACT.Copy).then_inc(sem["proj_ev"], 1)
                elif i < 12:
                    A(qT[:, c, :], src[:, 0:T], ACT.Copy).then_inc(sem["proj_ev"], 1)
                else:
                    (A(ksT[:, c, NP_:T], src[:, NP_:T], ACT.Copy))
                    A(kT[:, c, :], src[:, 0:T], ACT.Copy).then_inc(sem["proj_ev"], 1)
            act.wait_ge(sem["proj_ev"], 16)
            act.dma_start(t["k"], kT).then_inc(sem["st_mix"], 16)
            act.wait_ge(sem["v_ev"], 1)
            for j, (t0, P) in enumerate(TILES):
                act.dma_start(t["v"][t0:t0 + P, :], vtm[0:P, j, :]).then_inc(sem["st_mix"], 16)
            act.wait_ge(sem["gate_ps"], 1)
            for c in range(4):
                (A(rg[:, c, :], ps[c][:, 0:XW], ACT.Sigmoid, bias=M("abr")[:, c:c + 1]))
            act.wait_ge(sem["gate_ps"], 2)
            for c in range(3):
                (A(ig_[:, c, :], ps[4 + c][:, 0:XW], ACT.Sigmoid, bias=M("abi")[:, c:c + 1]))
            L(A(ig_[:, 3, :], ps[7][:, 0:XW], ACT.Sigmoid, bias=M("abi")[:, 3:4]), "gate_i")
            act.wait_ge(sem["lam"], 1)
            for c in range(4):
                (A(aa[:, c, :], rg[:, c, :], ACT.Exp, scale=lamw[:, 6, c:c + 1]))
            for c in range(4):
                ins = A(tt_[:, c, :], rg[:, c, :], ACT.Tanh, scale=lamw[:, 7, c:c + 1])
            L(ins, "lru_a")
            act.wait_ge(sem["lru_w"], 1)
            L(A(tt_[:, :, :], tt_[:, :, :], ACT.Sqrt), "lru_s")
            L(A(rg[:, :, 0:T], rg[:, :, 0:T], ACT.Tanh, scale=0.7978845608028654), "lru_g")
            for n in range(24):
                j, hd = n // 8, n % 8
                t0, P = TILES[j]
                nk = (128, 256, T)[j]
                act.wait_ge(sem["s_sm"], n + 1)
                L(A(s_sb[0:P, n % 2, 0:nk], s_sb[0:P, n % 2, 0:nk], ACT.Exp, bias=mx[0:P, n % 2, 1:2],
                    accum_out=rsum[0:P, n % 2, :]), "p_exp")
                act.wait_ge(sem["pt_ps"], n + 1)
                if n >= 2:
                    act.wait_ge(sem["pv_ps"], n - 1)
                kts = [(0, 128)] if j == 0 else [(0, 128), (1, 128)] if j == 1 else [(0, 128), (1, 128), (2, 32)]
                for kt, K in kts:
                    ins = A(pT[0:K, n % 2, kt, 0:P], ps[2 + n % 2][0:K, kt * 128:kt * 128 + P], ACT.Copy)
                    if kt == kts[-1][0]:
                        ins.then_inc(sem["pt_sb"], 1)
                act.wait_ge(sem["pv_ps"], n + 1)
                b = DHB * (hd % 2)
                A(ycat[b:b + DHB, 4 + hd // 2, t0:t0 + P], ps[4 + n % 2][b:b + DHB, 0:P], ACT.Copy)\
                    .then_inc(sem["pv_sb"], 1)

            def moe(l):
                B = NE * l
                act.wait_ge(sem["lg_ps"], l + 1)
                act.wait_ge(sem["lgz"], l + 1)
                act.wait_ge(sem["st_mix"], 16 * 4)
                if l:
                    act.wait_ge(sem["st_small"], 16 * 5)
                for j, (t0, P) in enumerate(TILES):
                    ins = A(lg[0:P, j, :], ps[6][0:P, j * 64:(j + 1) * 64], ACT.Copy)
                    L(ins, "act")
                L(A(score, lg, ACT.Sigmoid), "score")
                for j, (t0, P) in enumerate(TILES):
                    act.wait_ge(sem["tm_ps"], 3 * l + j + 1)
                    for hf in range(2):
                        ins = A(gb[0:P, j, hf * 512:(hf + 1) * 512], ps[2 * j + hf][0:P, :], ACT.Copy)
                        L(ins, "tm_sb" if hf else None)
                        if hf:
                            act.dma_start(H2[t0:t0 + P, :], gb[0:P, j, :]).then_inc(sem["h2_st"], 16)
                act.wait_ge(sem["shu_ps"], 2 * l + 2)
                for j, (t0, P) in enumerate(TILES):
                    A(shs[0:P, j, :], ps[j][0:P, 0:DE], ACT.Silu)
                    L(A(shu_[0:P, j, :], ps[j][0:P, DE:2 * DE], ACT.Copy), "shu_sb")
                for j, (t0, P) in enumerate(TILES):
                    act.wait_ge(sem["sht_ps"], 3 * l + j + 1)
                    for a in range(2):
                        L(A(shT[:, j, a, 0:P], ps[3][:, a * 128:a * 128 + P], ACT.Copy),
                          "sht_sb" if a else None)
                for j, (t0, P) in enumerate(TILES):
                    act.wait_ge(sem["shd_ps"], 3 * l + j + 1)
                    for hf, bk in enumerate(((0, 1), (4, 5), (2, 3))[j]):
                        L(A(ysh[0:P, j, hf * 512:(hf + 1) * 512], ps[bk][0:P, :], ACT.Copy), "shd_sb" if hf else None)

                def take(e, p, i):
                    act.wait_ge(sem["trx"], e + (B + 1))
                    if p[0]:
                        act.wait_ge(sem["up"], e + (B - 1))
                    A(xgT[:, p[1], 0:4, :], ps[4][:, :].rearrange("p (k s) -> p k s", k=4), ACT.Copy)\
                        .then_inc(sem["xta"], 1)

                def rows(e, p, old):
                    act.wait_ge(sem["dn"], e + (B + 1))
                    if old:
                        act.wait_ge(sem[f"ysc{p}"], e * 8 + 8 * (B - p))
                    A(yb[:, p, 0:512], ps[0][:, :], ACT.Copy).then_inc(sem["ya_e"], 1)

                def step(e0, i=None):
                    e = e0 if i is None else i * 2 + e0
                    if e0 + 1 < NE:
                        take(e + 1, (e0 + 1 >= 2, (e0 + 1) % 2), i)
                    act.wait_ge(sem["up"], e + (B + 1))
                    if e0:
                        act.wait_ge(sem["hd"], e + B)
                    A(silu_b, ps[2][:, 0:DE], ACT.Silu).then_inc(sem["sg"], 1)
                    if e0:
                        rows(e - 1, (e0 - 1) % 2, e0 >= 3)

                take(0, (False, 0), None)
                for e in range(3):
                    step(e)
                with act.Fori(0, (NE - 6) // 2) as i:
                    step(3, i)
                    step(4, i)
                for e in range(NE - 3, NE):
                    step(e)
                rows(NE - 1, (NE - 1) % 2, True)

                act.wait_ge(sem["flag"], l + 1)
                more = act.value_load(flagi[0:1, 0:1], min_val=0, max_val=1)
                with act.If(more > 0):
                    s = lambda n: sem[f"{n}{l}"]
                    with act.Fori(0, 2) as bb:
                        with act.Fori(0, NE) as e:
                            J = bb * NE + e
                            act.wait_ge(s("ovp"), J * 4 + 1)
                            for hf in range(2):
                                ins = A(xgT[:, 0, 4 * hf:4 * hf + 4, :],
                                        ps[4 + hf][:, :].rearrange("p (k s) -> p k s", k=4), ACT.Copy)
                            ins.then_inc(s("ova"), 1)
                            act.wait_ge(s("ovp"), J * 4 + 2)
                            A(silu_b, ps[2][:, 0:DE], ACT.Silu).then_inc(s("ova"), 1)
                            act.wait_ge(s("ovp"), J * 4 + 3)
                            A(hidT, ps[3][:, 0:256].rearrange("p (a s) -> p a s", a=2), ACT.Copy).then_inc(s("ova"), 1)
                            act.wait_ge(s("ovp"), J * 4 + 4)
                            for hf in range(2):
                                ins = A(yb[:, 0, hf * 512:(hf + 1) * 512], ps[hf][:, :], ACT.Copy)
                            ins.then_inc(s("ova"), 1)

            norm_root(1)
            moe(0)
            norm_root(2)
            act.wait_ge(sem["padc"], 1)
            act.wait_ge(sem["acc_x"], 1)
            act.dma_start(sst[:, 1, :, :], t["S0"]).then_inc(sem["ld_state"], 16)
            def conv_silu(n):
                act.wait_ge(sem["cacc"], 4 * (n + 1))
                dst = (qf, kf, vf)[n // 2][:, 4 * (n % 2):4 * (n % 2) + 4, :]
                A(dst[:, :, 0:NP_], cacc[:, n % 2, :, 0:NP_], ACT.Silu)
                A(dst[:, :, NP_:T], cacc[:, n % 2, :, SEG:SEG + NS], ACT.Silu).then_inc(sem["csilu"], 1)

            for i in range(32):
                n, c = i // 4, i % 4
                act.wait_ge(sem["proj_ps"], 16 + i + 1)
                src = ps[i % 4]
                if i < 24:
                    if n >= 2:
                        act.wait_ge(sem["cacc"], 4 * (n - 2) + c + 1)
                    A(raw[:, n % 2, c, 3:3 + NP_], src[:, 0:NP_], ACT.Copy)
                    A(raw[:, n % 2, c, SEG + 3:SEG + 3 + NS], src[:, NP_:T], ACT.Copy).then_inc(sem["proj_ev"], 1)
                else:
                    A(zf[:, i - 24, :], src[:, 0:T], ACT.Silu).then_inc(sem["proj_ev"], 1)
                if c == 3 and 1 <= n <= 6:
                    conv_silu(n - 1)
            act.wait_ge(sem["ab_e"], 1)
            L(A(spw[:, 1, :], spw[:, 0, :], ACT.Exp), "ab_act")
            for j, (t0, P) in enumerate(TILES):
                (A(btm[0:P, j, :], ps[6][0:P, j * 16 + 8:j * 16 + 16], ACT.Sigmoid))
            L(A(spw[:, 5, 0:8], M("alog"), ACT.Exp), "ab_act")
            act.wait_ge(sem["gcum_e"], 1)
            A(begc, gcol, ACT.Exp)
            L(A(kdcol, glast, ACT.Exp), "ab_act")
            for n in range(16):
                act.wait_ge(sem["lss"], n + 1)
                if n >= 2:
                    act.wait_ge(sem["qk_n"], n - 1)
                sc = 128.0 if n < 8 else 1.0
                L(A(lbuf[:, n % 2, 0:T], ps[n % 4][:, 0:T], ACT.Sqrt, scale=sc,
                    bias=C("eps")[:, 1:2] if n < 8 else C("eps")[:, 0:1]), "lrms")
            lv = 0
            for n in range(6):
                j, g = n // 2, n % 2
                t0, P = TILES[j]
                act.wait_ge(sem["gb_ps"], n + 1)
                if n:
                    act.wait_ge(sem["tk_sb"], n)
                L(A(four(egb[:, 0, :], P), ps[0][:, 0:4 * P].rearrange("p (h i) -> p h i", h=4), ACT.Exp), "gb_e")
                act.wait_ge(sem["ldif"], n + 1)
                L(A(four(lbuf[:, 0, :], P)[0:P], four(lbuf[:, 0, :], P)[0:P], ACT.Exp), "lexp")
                for s_ in range(6 if P == 128 else 5):
                    act.wait_ge(sem["y_ps"], lv + 1)
                    L(A(four(ybuf[:, 0, :], P)[0:P], ps[6][0:P, 0:4 * P].rearrange("p (h i) -> p h i", h=4),
                        ACT.Copy), "y_sb")
                    lv += 1
                act.wait_ge(sem["u_ps"], n + 1)
                L(A(uu[0:P, j, 4 * g:4 * g + 4, :], ps[2][0:P, :].rearrange("p (h v) -> p h v", h=4), ACT.Copy), "act")
                L(A(h[:, 4 * g:4 * g + 4, t0:t0 + P], ps[3][:, 0:4 * P].rearrange("p (h i) -> p h i", h=4), ACT.Copy),
                  "batch")
            for n in range(10):
                c, g = n // 2, n % 2
                t0 = TILES[c // 2][0]
                r0, R = (64 * (c % 2), 64) if c < 4 else (0, 32)
                act.wait_ge(sem["o_ps"], n + 1)
                L(A(ycat[:, 4 * g:4 * g + 4, t0 + r0:t0 + r0 + R],
                    ps[1 + 3 * (n % 2)][:, 0:4 * R].rearrange("p (h i) -> p h i", h=4), ACT.Copy), "o_sb")
            for n in range(8):
                act.wait_ge(sem["oss"], n + 1)
                if n >= 2:
                    act.wait_ge(sem["on"], n - 1)
                L(A(lbuf[:, n % 2, 0:T], ps[4 + n % 4][:, 0:T], ACT.Sqrt, scale=1.0 / 128, bias=C("eps")[:, 0:1]), "orms")
            norm_root(3)
            moe(1)
            norm_root(4)

        @block.vector
        def _(dve):
            V = nc.vector
            L = Chain(dve, "dve")

            def tt(o, a, b, op):
                return V.tensor_tensor(o, a, b, op)

            def ts(o, a, s1, s2, op0, op1=None):
                return V.tensor_scalar(o, a, s1, s2, op0, op1) if op1 is not None else V.tensor_scalar(o, a, s1, None, op0)

            def stt(o, a, s, b, op0, op1):
                return V.scalar_tensor_tensor(out=o, in0=a, scalar=s, in1=b, op0=op0, op1=op1)

            def log1p(out, e, w1, w2):
                L(ts(w1, e, 2.0, None, ALU.add))
                L(V.reciprocal(w1, w1))
                L(tt(w1, w1, e, ALU.mult))
                L(tt(w2, w1, w1, ALU.mult))
                L(ts(out, w2, 1.0 / 17, None, ALU.mult))
                for k in (15, 13, 11, 9, 7, 5, 3):
                    L(stt(out, out, 1.0 / k, w2, ALU.add, ALU.mult))
                L(stt(out, out, 1.0, w1, ALU.add, ALU.mult))
                L(ts(out, out, 2.0, None, ALU.mult))

            L(V.memset(bdr, 0.0))
            L(V.memset(bdi, 0.0), "pad")
            dve.wait_ge(sem["ld_small"], 48)
            L(V.memset(xpad[:, :, 0:3], 0.0))
            L(V.tensor_copy(xpad[:, :, SEG:SEG + 3], M("astate").rearrange("p (c j) -> p c j", c=4)))
            lam = M("alam")
            L(ts(lamw[:, 2, :], lam, -1.0, None, ALU.mult))
            L(tt(lamw[:, 0, :], lam, lamw[:, 2, :], ALU.min), "lamn")
            L(ts(lamw[:, 2, :], lamw[:, 2, :], 0.0, None, ALU.max))
            dve.wait_ge(sem["lame"], 1)
            log1p(lamw[:, 3, :], lamw[:, 1, :], lamw[:, 4, :], lamw[:, 5, :])
            L(tt(lamw[:, 3, :], lamw[:, 3, :], lamw[:, 2, :], ALU.add))
            L(ts(lamw[:, 7, :], lamw[:, 3, :], 8.0, None, ALU.mult))
            L(ts(lamw[:, 6, :], lamw[:, 3, :], -8.0, None, ALU.mult), "lam")

            def squares(k):
                L(tt(h[:, :, :], x[:, :, :], x[:, :, :], ALU.mult), "sq")

            def apply_norm(k, l, which):
                dve.wait_ge(sem["rms"], k + 1)
                L(V.reciprocal(rms[:, :], rms[:, :]))
                L(tt(h[:, :, :], x[:, :, :], rms[:, :].unsqueeze(1).broadcast_to([128, KC, T]), ALU.mult))
                for c in range(KC):
                    for g, (a, b) in enumerate(GROUPS):
                        lastop = c == KC - 1 and g == 1
                        if l is None:
                            ins = ts(h[:, c, a:b], h[:, c, a:b], M("norms")[:, 32 + c:33 + c], None, ALU.mult)
                        else:
                            ins = ts(h[:, c, a:b], h[:, c, a:b], scale1[:, l, which, c, g:g + 1],
                                     mod[:, l, 24 * which + c, g:g + 1], ALU.mult, ALU.add)
                        (L if lastop else L.go)(ins, "h" if lastop else None)

            squares(0)
            for l in range(2):
                dve.wait_ge(sem["w_used"], (MOD_U // 2) * (l + 1))
                L(tt(mod[:, l, :, :], ps[l][:, 0:96].rearrange("p (m g) -> p m g", g=2),
                     M("bmod")[:, l * 48:(l + 1) * 48].unsqueeze(2).broadcast_to([128, 48, 2]), ALU.add))
                for w in range(2):
                    g_ = M("norms")[:, (2 * l + w) * 8:(2 * l + w + 1) * 8].unsqueeze(2).broadcast_to([128, KC, 2])
                    L(stt(scale1[:, l, w, :, :], mod[:, l, 24 * w + 8:24 * w + 16, :], 1.0, g_, ALU.add, ALU.mult))
            apply_norm(0, 0, 0)
            cw = M("aconv").rearrange("p (c j) -> p c j", c=4)
            for c in range(4):
                dve.wait_ge(sem["proj_ev"], c + 1)
                L(ts(xc[:, c, :], xpad[:, c, 0:XW], cw[:, c, 0:1], M("aconvb")[:, c:c + 1], ALU.mult, ALU.add))
                for j in range(1, 4):
                    last = c == 3 and j == 3
                    L(stt(xc[:, c, :], xpad[:, c, j:j + XW], cw[:, c, j:j + 1], xc[:, c, :], ALU.mult, ALU.add),
                      "conv" if last else None)
            L(V.tensor_copy(cst3[:, :, 0, :], xpad[:, :, NP_:NP_ + 3]))
            L(V.tensor_copy(cst3[:, :, 1, :], xpad[:, :, SEG + NS:SEG + NS + 3]))
            dve.wait_ge(sem["proj_ev"], 8)
            L(tt(hh[:, :, 0:T], gaT, gaT, ALU.mult))
            L(ts(hh[:, :, 0:T], hh[:, :, 0:T], 0.044715, 1.0, ALU.mult, ALU.add))
            dve.wait_ge(sem["v_ps"], 2)
            for j, (t0, P) in enumerate(TILES):
                L(V.tensor_copy(vtm[0:P, j, :], ps[4 + j][0:P, :]), "v_ev" if j == 2 else None)
            dve.wait_ge(sem["lru_a"], 1)
            L(tt(rg[:, :, 0:T], hh[:, :, 0:T], gaT, ALU.mult))
            L(tt(ig_, ig_, xc, ALU.mult))
            L(tt(xc, aa, aa, ALU.mult))
            L(stt(tt_, xc, 1.0, tt_, ALU.add, ALU.mult), "lru_w")
            dve.wait_ge(sem["lru_s"], 1)
            L(tt(tt_, tt_, ig_, ALU.mult))
            for c in range(4):
                L.go(V.tensor_tensor_scan(hh[:, c, 0:NP_], aa[:, c, 0:NP_], tt_[:, c, 0:NP_], 0.0, ALU.mult, ALU.add))
                L(V.tensor_tensor_scan(hh[:, c, SEG:SEG + NS], aa[:, c, SEG:SEG + NS], tt_[:, c, SEG:SEG + NS],
                                       M("ah0")[:, c:c + 1], ALU.mult, ALU.add))
            L(V.tensor_copy(hst[:, :, 0:1], hh[:, :, NP_ - 1:NP_]))
            L(V.tensor_copy(hst[:, :, 1:2], hh[:, :, SEG + NS - 1:SEG + NS]), "hst")
            dve.wait_ge(sem["lru_g"], 1)
            L(stt(gaT, rg[:, :, 0:T], 1.0, gaT, ALU.add, ALU.mult))
            L(stt(ycat[:, 0:4, 0:NP_], hh[:, :, 0:NP_], 0.5, gaT[:, :, 0:NP_], ALU.mult, ALU.mult))
            L(stt(ycat[:, 0:4, NP_:T], hh[:, :, SEG:SEG + NS], 0.5, gaT[:, :, NP_:T], ALU.mult, ALU.mult), "ya")
            dve.wait_ge(sem["ld_att"], 16 * 9)
            L(V.memset(biasP0[0:64, :, 64:128], -1e30))
            L(V.memset(biasP1[0:64, :, 192:256], -1e30))
            for n in range(24):
                j, hd = n // 8, n % 8
                t0, P = TILES[j]
                nk = (128, 256, T)[j]
                bias = (biasP0, biasP1, biasS)[j]
                dve.wait_ge(sem["s_ps"], n + 1)
                if n >= 2:
                    dve.wait_ge(sem["pt_ps"], n - 1)
                L(stt(s_sb[0:P, n % 2, 0:nk], ps[n % 2][0:P, 0:nk], DHB ** -0.5, bias[0:P, hd, :], ALU.mult, ALU.add))
                L(V.reduce_max(mx[0:P, n % 2, 0:1], s_sb[0:P, n % 2, 0:nk], AX.X))
                L(ts(mx[0:P, n % 2, 1:2], mx[0:P, n % 2, 0:1], -1.0, None, ALU.mult), "s_sm")
                dve.wait_ge(sem["p_exp"], n + 1)
                L(V.reciprocal(rsum[0:P, n % 2, :], rsum[0:P, n % 2, :]))
                L(ts(s_sb[0:P, n % 2, 0:nk], s_sb[0:P, n % 2, 0:nk], rsum[0:P, n % 2, :], None, ALU.mult), "p_nrm")

            def residual(base, l):
                for i in range(8):
                    dve.wait_ge(sem["out_ps"], base + i + 1)
                    for g, (a, b) in enumerate(GROUPS):
                        L(stt(x[:, i, a:b], ps[i % 4][:, a:b], mod[:, l, 16 + i, g:g + 1], x[:, i, a:b],
                              ALU.mult, ALU.add), "out_x" if g else None)

            residual(0, 0)

            def moe(l):
                B = NE * l
                dve.wait_ge(sem["st_mix"], 16 * 4)
                if l:
                    dve.wait_ge(sem["st_small"], 16 * 5)
                L(V.memset(lg, 0.0), "lgz")
                L(V.memset(xgb, 0.0), "xgz")
                dve.wait_ge(sem["score"], l + 1)
                rb = M("rb")[:, l * 64:(l + 1) * 64].unsqueeze(1).broadcast_to([128, 3, NE])
                L(tt(selv, score, rb, ALU.add))
                for j in range(3):
                    for g in range(8):
                        ins = V.max(top2[:, j, g, :], selv[:, j, g * 8:(g + 1) * 8])
                        (L if (j, g) == (2, 7) else L.go)(ins)
                L(tt(gsc.unsqueeze(3), top2[:, :, :, 0:1], top2[:, :, :, 1:2], ALU.add))
                for j in range(3):
                    other = gsc[:, j, :].unsqueeze(1).broadcast_to([128, 8, 8])
                    own = gsc[:, j, :].unsqueeze(2).broadcast_to([128, 8, 8])
                    L(tt(gcmp[:, j], other, own, ALU.is_gt))
                    L(tt(geq[:, j], other, own, ALU.is_equal))
                    L(tt(geq[:, j], geq[:, j], C("lower").rearrange("p (a b) -> p a b", a=8), ALU.mult))
                    L(tt(gcmp[:, j], gcmp[:, j], geq[:, j], ALU.add))
                    L(V.reduce_sum(grk[:, j, :], gcmp[:, j], AX.X))
                L(ts(grk, grk, 4.0, None, ALU.is_lt))
                L(ts(gsc, grk, 1.0, 1e30, ALU.subtract, ALU.mult))
                for j in range(3):
                    e8 = lambda v: v[:, j, :].rearrange("p (g e) -> p g e", g=8)
                    L(tt(e8(tmp1), e8(selv), grk[:, j, :].unsqueeze(2).broadcast_to([128, 8, 8]), ALU.mult))
                    L(tt(e8(tmp1), e8(tmp1), gsc[:, j, :].unsqueeze(2).broadcast_to([128, 8, 8]), ALU.add))
                for j in range(3):
                    L(V.max(top8[:, j, :], tmp1[:, j, :]))
                    L(V.match_replace(out=tmp2[:, j, :], in_to_replace=top8[:, j, :], in_values=tmp1[:, j, :],
                                      imm_value=-3e30))
                L(tt(msk, tmp2, tmp1, ALU.is_lt), "mask")
                L(tt(gates, score, msk, ALU.mult))
                L(V.reduce_sum(gsum[:, :, :], gates, AX.X))
                L(V.reciprocal(gsum[:, :, :], gsum[:, :, :]))
                L(tt(gates, gates, gsum.broadcast_to([128, 3, NE]), ALU.mult))
                L(ts(tg[:, :, :, 1:2], gates.unsqueeze(3), 2.5, None, ALU.mult))
                for j in range(3):
                    L(V.tensor_copy(tg[:, j, :, 0:1], C("tok")[:, j:j + 1].unsqueeze(2).broadcast_to([128, NE, 1])))
                dve.wait_ge(sem["rank_ps"], l + 1)
                L(V.tensor_copy(cntf[:, 0:NE], ps[7][:, 192:256]))
                L(V.reduce_max(cntf[0:1, 64:65], cntf[0:1, 0:NE], AX.X))
                L(ts(flagi[0:1, 0:1], cntf[0:1, 64:65], float(CAP), None, ALU.is_gt), "flag")
                L(V.memset(rk, 0.0))
                for j, (t0, P) in enumerate(TILES):
                    L(V.tensor_copy(rk[0:P, j, :], ps[7][0:P, j * 64:(j + 1) * 64]))
                L(V.tensor_tensor_scan(start, ones[:, 0:NE], cntf[:, 0:NE], 0.0, ALU.mult, ALU.add))
                L(tt(start, start, cntf[:, 0:NE], ALU.subtract))
                L(ts(srow, start, C("slot"), None, ALU.add))
                L(ts(start, start, 1.0, None, ALU.add))
                base_ = start.unsqueeze(1).broadcast_to([128, 3, NE])
                L(tt(tmp1, rk, base_, ALU.add))
                L(tt(tmp1, tmp1, msk, ALU.mult))
                for j in range(3):
                    L(V.max(rowif[:, j, :], tmp1[:, j, :]))
                L(ts(rowi[:, :, :], rowif, -1.0, None, ALU.add), "rowi")
                L(stt(rk, rk, 1.0, msk, ALU.add, ALU.mult))
                L(ts(rk, rk, -1.0, None, ALU.add))

                def one_hots(g, off, sem_, wait):
                    if wait is not None:
                        dve.wait_ge(*wait)
                    for j, (t0, P) in enumerate(TILES):
                        o = selb[0:P, g % 2, j, :].rearrange("p (e s) -> p e s", e=8)
                        io = cst[0:P, bass.ds(off, CAP)] if not isinstance(off, int) else cst[0:P, off:off + CAP]
                        ins = tt(o, io.unsqueeze(1).broadcast_to([P, 8, CAP]),
                                 rk[0:P, j, 8 * g:8 * g + 8].unsqueeze(2).broadcast_to([P, 8, CAP]), ALU.is_equal)
                    ins.then_inc(sem_, 1)

                for g in range(8):
                    one_hots(g, CST["iota"][0], sem["sel"], (sem["sel_ps"], 8 * l + g - 1) if 8 * l + g >= 2 else None)

                def tables(chain, shift):
                    tabs = ps[6][:, 0:128].rearrange("p (e c) -> p e c", c=2)
                    chain(ts(idxf[:, 0, :].unsqueeze(2), tabs[:, :, 0:1], float(LIM), None, ALU.add))
                    chain(V.tensor_copy(idx[:, :, 0:1], idxf[:, 0, :].unsqueeze(2)))
                    chain(V.tensor_copy(idx[:, :, 1:2].bitcast(F32), tabs[:, :, 1:2]))
                    chain(ts(idxf[:, 0, :], idxf[:, 0, :], float(LIM), 65536.0, ALU.is_ge, ALU.mult))
                    chain(tt(idxf[:, 0, :], idxf[:, 0, :], srow, ALU.add))
                    if shift is not None:
                        chain(tt(idxf[:, 0, :], idxf[:, 0, :], shift, ALU.add))
                    return V.tensor_copy(idx[:, :, 2:3], idxf[:, 0, :].unsqueeze(2))

                dve.wait_ge(sem["sel_ps"], 8 * l + 8)
                L(tables(L, None), "idx")

                def copy_gather(e, p, wait):
                    if wait:
                        dve.wait_ge(sem[f"xg{p}"], e * 8 + 8 * (B - p))
                    src = idx[:, e:e + 1, 0:2] if isinstance(e, int) else idx[:, bass.ds(e, 1), 0:2]
                    V.tensor_copy(icg[:, p:p + 1, :], src).then_inc(sem["ig"], 1)

                def copy_scatter(e, p, wait):
                    if wait:
                        dve.wait_ge(sem[f"ysc{p}"], e * 8 + 8 * (B - p))
                    src = idx[:, e:e + 1, 2:3] if isinstance(e, int) else idx[:, bass.ds(e, 1), 2:3]
                    V.tensor_copy(ics[:, p:p + 1, :], src).then_inc(sem["isx"], 1)

                def take(e, p, wait):
                    dve.wait_ge(sem["trx"], e + (B + 1))
                    if wait:
                        dve.wait_ge(sem["up"], e + (B - 1))
                    V.tensor_copy(xgT[:, p, 4:8, :], ps[5][:, :].rearrange("p (k s) -> p k s", k=4))\
                        .then_inc(sem["xtb"], 1)

                def hidden_T(e, wait):
                    dve.wait_ge(sem["trh"], e + (B + 1))
                    if wait:
                        dve.wait_ge(sem["dn"], e + B)
                    V.tensor_copy(hidT, ps[3][:, 0:256].rearrange("p (a s) -> p a s", a=2)).then_inc(sem["ht"], 1)

                def rows(e, p, wait):
                    copy_scatter(e, p, wait)
                    dve.wait_ge(sem["dn"], e + (B + 1))
                    V.tensor_copy(yb[:, p, 512:1024], ps[1][:, :]).then_inc(sem["yb_e"], 1)

                def step(e0, i=None):
                    e = e0 if i is None else i * 2 + e0
                    if e0:
                        hidden_T(e - 1, e0 >= 2)
                    if e0 + 1 < NE:
                        take(e + 1, (e0 + 1) % 2, e0 + 1 >= 2)
                    dve.wait_ge(sem["sg"], e + (B + 1))
                    dve.wait_ge(sem["ig"], e + (B + 1))
                    if e0:
                        dve.wait_ge(sem["trh"], e + B)
                    stt(hid, ps[2][:, DE:2 * DE], icg[:, e0 % 2, 1:2].bitcast(F32), silu_b, ALU.mult, ALU.mult)\
                        .then_inc(sem["hd"], 1)
                    if e0 + 2 < NE:
                        dve.wait_ge(sem["hd"], e + (B + 1))
                        copy_gather(e + 2, e0 % 2, True)
                    if e0:
                        rows(e - 1, (e0 - 1) % 2, e0 >= 3)

                copy_gather(0, 0, False)
                copy_gather(1, 1, False)
                take(0, 0, False)
                for e in range(3):
                    step(e)
                with dve.Fori(0, (NE - 6) // 2) as i:
                    step(3, i)
                    step(4, i)
                for e in range(NE - 3, NE):
                    step(e)
                hidden_T(NE - 1, True)
                rows(NE - 1, (NE - 1) % 2, True)

                dve.wait_ge(sem["flag"], l + 1)
                more = dve.value_load(flagi[0:1, 0:1], min_val=0, max_val=1)
                with dve.If(more > 0):
                    s = lambda n: sem[f"{n}{l}"]
                    for p in range(2):
                        dve.wait_ge(sem[f"ysc{p}"], 8 * (B + NE))
                    with dve.Fori(0, 2) as bb:
                        for g in range(8):
                            if g >= 2:
                                dve.wait_ge(s("osel_ps"), bb * 8 + (g - 1))
                            else:
                                dve.wait_ge(s("od"), bb * NE + 1)
                            one_hots(g, bb * CAP + (CST["iota"][0] + CAP), s("osel"), None)
                        dve.wait_ge(s("osel_ps"), bb * 8 + 8)
                        cnt = [0]

                        def chain(ins):
                            cnt[0] += 1
                            ins.then_inc(s("ovi"), 1)
                            dve.wait_ge(s("ovi"), bb * 7 + cnt[0])

                        chain(tables(chain, cst[:, bass.ds(bb * CAP + (CST["iota"][0] + CAP), 1)]
                                     .broadcast_to([128, NE])))
                        assert cnt[0] == 7, cnt
                        dve.sem_inc(sem["passed_d"], 1)
                        with dve.Fori(0, NE) as e:
                            J = bb * NE + e
                            dve.wait_ge(s("od"), J + 1)
                            V.tensor_copy(ico[:, :].unsqueeze(1), idx[:, bass.ds(e, 1), :]).then_inc(s("ovd"), 1)
                            dve.wait_ge(s("ova"), J * 4 + 2)
                            dve.wait_ge(s("ovd"), J * 2 + 1)
                            stt(hid, ps[2][:, DE:2 * DE], ico[:, 1:2].bitcast(F32), silu_b, ALU.mult, ALU.mult)\
                                .then_inc(s("ovd"), 1)

                dve.wait_ge(sem["shd_sb"], 3 * (l + 1))
                for n in range(24):
                    j, k = n // 8, n % 8
                    P = TILES[j][1]
                    dve.wait_ge(sem[f"got{n % 4}"], 16 * ((24 * l + n) // 4 + 1))
                    L(tt(ysh[0:P, j, :], ysh[0:P, j, :], gb[0:P, n % 4, :], ALU.add), "cb")
                for j, (t0, P) in enumerate(TILES):
                    dve.wait_ge(sem["acc_ps"], 3 * l + j + 1)
                    for k in range(KC):
                        ins = stt(x[:, k, t0:t0 + P], ps[2 * j + k // 4][:, (k % 4) * 128:(k % 4) * 128 + P],
                                  mod[:, l, 40 + k, (1 if j == 2 else 0):(2 if j == 2 else 1)], x[:, k, t0:t0 + P],
                                  ALU.mult, ALU.add)
                        L(ins, "acc_x" if (j, k) == (2, KC - 1) else None)

            squares(1)
            apply_norm(1, 0, 1)
            moe(0)
            squares(2)
            apply_norm(2, 1, 0)
            L(V.memset(raw[:, :, :, 0:3], 0.0), "padc")
            L(V.memset(sst[:, 0, :, :], 0.0), "s0")
            cw1 = M("cconv").rearrange("p (c j) -> p c j", c=24)
            cs1 = M("cstate").rearrange("p (c j) -> p c j", c=24)
            for n in range(6):
                for c in range(4):
                    i = 4 * n + c
                    r = raw[:, n % 2, c, :]
                    dve.wait_ge(sem["proj_ev"], 16 + i + 1)
                    L(V.tensor_copy(r[:, SEG:SEG + 3], cs1[:, i, :]))
                    L(V.tensor_copy(cc3[:, i, 0, :], r[:, NP_:NP_ + 3]))
                    L(V.tensor_copy(cc3[:, i, 1, :], r[:, SEG + NS:SEG + NS + 3]), "cc" if i == 23 else None)
                    if n >= 2 and c == 0:
                        dve.wait_ge(sem["csilu"], n - 1)
                    o = cacc[:, n % 2, c, :]
                    L(ts(o, r[:, 0:XW], cw1[:, i, 0:1], None, ALU.mult))
                    for j in range(1, 4):
                        L(stt(o, r[:, j:j + XW], cw1[:, i, j:j + 1], o, ALU.mult, ALU.add), "cacc" if j == 3 else None)
            dve.wait_ge(sem["ab_ps"], 1)
            L(V.memset(spt, 0.0))
            L(V.memset(btm, 0.0))
            for j, (t0, P) in enumerate(TILES):
                L(tt(spt[0:P, j, :], ps[6][0:P, j * 16:j * 16 + 8], M("dtb", P), ALU.add))
            s3 = lambda v: v.rearrange("p (t h) -> p t h", t=3)
            L(ts(s3(spw[:, 2, :]), spt, -1.0, None, ALU.mult))
            L(tt(s3(spw[:, 0, :]), spt, s3(spw[:, 2, :]), ALU.min), "ab_e")
            L(ts(spt, spt, 0.0, None, ALU.max))
            dve.wait_ge(sem["ab_act"], 2)
            log1p(spw[:, 2, :], spw[:, 1, :], spw[:, 3, :], spw[:, 4, :])
            L(tt(spt, spt, s3(spw[:, 2, :]), ALU.add))
            L(stt(gtm, spt, -1.0, spw[:, 5, 0:8].unsqueeze(1).broadcast_to([128, 3, 8]), ALU.mult, ALU.mult), "ab_sb")
            dve.wait_ge(sem["gcum_ps"], 1)
            L(V.memset(gcol, 0.0))
            L(V.memset(glast, 0.0))
            for j, (t0, P) in enumerate(TILES):
                L(V.tensor_copy(gcol[0:P, j, :], ps[6][0:P, 64 + j * 8:72 + j * 8]))
                L(tt(glast[0:P, j, :], ps[6][0:P, 96 + j * 8:104 + j * 8], gcol[0:P, j, :], ALU.subtract),
                  "gcum_e" if j == 2 else None)
            dve.wait_ge(sem["ab_act"], 3)
            L(tt(begc, begc, btm, ALU.mult), "gdec")
            dve.wait_ge(sem["csilu"], 6)
            for n in range(4):
                src = (qf, kf)[n // 2][:, 4 * (n % 2):4 * (n % 2) + 4, :]
                L(tt(sqb[:, 4 * n:4 * n + 4, :], src, src, ALU.mult), "lsq")
            for n in range(16):
                v = (qf, kf)[n // 8][:, n % 8, :]
                dve.wait_ge(sem["lrms"], n + 1)
                L(V.reciprocal(lbuf[:, n % 2, 0:T], lbuf[:, n % 2, 0:T]))
                L(tt(v, v, lbuf[:, n % 2, 0:T], ALU.mult), "qk_n")
            lv = 0
            for n in range(6):
                j, g = n // 2, n % 2
                t0, P = TILES[j]
                f = lambda b: four(b, P)[0:P]
                pb = lambda b: ps[b][0:P, 0:4 * P].rearrange("p (h i) -> p h i", h=4)
                hsl = slice(4 * g, 4 * g + 4)
                dve.wait_ge(sem["gb_e"], n + 1)
                if n:
                    dve.wait_ge(sem["um"], lv)
                    dve.wait_ge(sem["u_ps"], n)
                L(tt(f(lbuf[:, 0, :]), pb(0), gcol[0:P, j, hsl].unsqueeze(2).broadcast_to([P, 4, P]), ALU.subtract))
                L(ts(f(lbuf[:, 0, :]), f(lbuf[:, 0, :]), 0.0, None, ALU.min), "ldif")
                L(V.tensor_copy(f(xbuf[:, 0, :]), ident[0:P, 0:P].unsqueeze(1).broadcast_to([P, 4, P])))
                L(V.tensor_copy(f(dbuf[:, 0, :]), ident[0:P, 0:P].unsqueeze(1).broadcast_to([P, 4, P])), "xd")
                dve.wait_ge(sem["lexp"], n + 1)
                L(tt(f(lbuf[:, 0, :]), f(lbuf[:, 0, :]), C("tri")[0:P, 0:P].unsqueeze(1).broadcast_to([P, 4, P]), ALU.mult))
                dve.wait_ge(sem["kk_ps"], n + 1)
                L(tt(f(nbuf[:, 0, :]), pb(2), f(lbuf[:, 0, :]), ALU.mult))
                L(tt(f(nbuf[:, 0, :]), f(nbuf[:, 0, :]), pb(1), ALU.mult), "nmat")
                L(tt(att(j)[0:P, hsl, :], pb(3), f(lbuf[:, 0, :]), ALU.mult), "dve")
                eg = four(egb[:, 0, :], P)
                L(tt(qf[:, hsl, t0:t0 + P], qf[:, hsl, t0:t0 + P], eg, ALU.mult))
                for cc, col in ((2 * j, 63), (2 * j + 1, 127)) if j < 2 else ((4, 31),):
                    L(V.tensor_copy(sdec[:, cc, hsl].unsqueeze(2), eg[:, :, col:col + 1]))
                dve.wait_ge(sem["tk_ps"], n + 1)
                tk = lambda b: ps[b][0:P, :].rearrange("p (h d) -> p h d", h=4)
                bc = lambda v: v[0:P, j, hsl].unsqueeze(2).broadcast_to([P, 4, 128])
                L(tt(kbe[0:P, 0, :].rearrange("p (h d) -> p h d", h=4), tk(4), bc(begc), ALU.mult))
                L(tt(kdec[0:P, j, hsl, :], tk(4), bc(kdcol), ALU.mult))
                L(tt(vbe[0:P, 0, :].rearrange("p (h d) -> p h d", h=4), tk(5), bc(btm), ALU.mult), "tk_sb")
                for s_ in range(6 if P == 128 else 5):
                    dve.wait_ge(sem["z_ps"], lv + 1)
                    L(tt(f(dbuf[:, 0, :]), f(dbuf[:, 0, :]), pb(0), ALU.subtract))
                    L(tt(f(xbuf[:, 0, :]), f(xbuf[:, 0, :]), pb(1), ALU.subtract), "xd")
                    lv += 1
            dve.wait_ge(sem["batch"], 6)
            for n in range(10):
                c, g = n // 2, n % 2
                j = c // 2
                r0, R = (64 * (c % 2), 64) if c < 4 else (0, 32)
                hsl = slice(4 * g, 4 * g + 4)
                st = sst[:, 0 if c < 4 else 1, :, :]
                dve.wait_ge(sem["ws_ps"], n + 1)
                L(tt(uu[r0:r0 + R, j, hsl, :], uu[r0:r0 + R, j, hsl, :],
                     ps[3 * (n % 2)][r0:r0 + R, :].rearrange("p (h v) -> p h v", h=4), ALU.subtract), "vn")
                dve.wait_ge(sem["su_ps"], n + 1)
                for a in range(4):
                    hd = 4 * g + a
                    L(stt(st[:, hd, :], st[:, hd, :], sdec[:, c, hd:hd + 1], ps[2 + 3 * (n % 2)][:, a * 128:(a + 1) * 128],
                          ALU.mult, ALU.add), "s_new" if a == 3 else None)
            dve.wait_ge(sem["o_sb"], 10)
            L(tt(vf, ycat[:, :, :], ycat[:, :, :], ALU.mult), "osq")
            for n in range(8):
                dve.wait_ge(sem["orms"], n + 1)
                L(V.reciprocal(lbuf[:, n % 2, 0:T], lbuf[:, n % 2, 0:T]))
                L(tt(ycat[:, n, :], ycat[:, n, :], lbuf[:, n % 2, 0:T], ALU.mult), "on")
            L(stt(ycat[:, :, :], ycat[:, :, :], M("cnorm"), zf, ALU.mult, ALU.mult), "ozs")
            residual(8, 1)
            squares(3)
            apply_norm(3, 1, 1)
            moe(1)
            squares(4)
            apply_norm(4, None, None)

        @block.gpsimd
        def _(po):
            L = Chain(po, "pool")
            po.wait_ge(sem["conv"], 1)
            po.wait_ge(sem["hst"], 1)
            po.dma_start(t["aconv"], cst3[:, :, :, :]).then_inc(sem["st_small"], 16)
            po.dma_start(t["ah"], hst[:, :, :]).then_inc(sem["st_small"], 16)

            def gather(index, dst, src, bound):
                return po.indirect_dma_start(dst, None, src, bass.IndirectOffsetOnAxis(ap=index, axis=0),
                                             bounds_check=bound, oob_is_err=False)

            def scatter(index, dst, src, bound):
                return po.indirect_dma_start(dst, bass.IndirectOffsetOnAxis(ap=index, axis=0), src, None,
                                             bounds_check=bound, oob_is_err=False)

            def moe(l):
                B = NE * l
                for j, (t0, P) in enumerate(TILES):
                    po.wait_ge(sem["shu_sb"], 3 * l + j + 1)
                    po.tensor_tensor(shh_[0:P, j, :], shs[0:P, j, :], shu_[0:P, j, :], ALU.mult)\
                        .then_inc(sem["shh"], 1)
                po.wait_ge(sem["h2_st"], 48 * (l + 1))
                po.wait_ge(sem["xgz"], l + 1)

                def fetch(e, p, wait):
                    if wait:
                        po.wait_ge(sem["trx"], e + (B - 1))
                    po.wait_ge(sem["ig"], e + (B + 1))
                    po.sem_inc(sem["passed"], 1)
                    gather(icg[:, p, 0:1], xgb[:, p, :], H2, T - 1).then_inc(sem[f"xg{p}"], 16)

                def store(e, p):
                    po.wait_ge(sem["isx"], e + (B + 1))
                    po.wait_ge(sem["ya_e"], e + (B + 1))
                    po.wait_ge(sem["yb_e"], e + (B + 1))
                    po.sem_inc(sem["passed"], 1)
                    scatter(ics[:, p, 0:1], Y, yb[:, p, :], T * TOPK - 1).then_inc(sem[f"ysc{p}"], 16)

                def step(e0, i=None):
                    e = e0 if i is None else i * 2 + e0
                    if e0 + 2 < NE:
                        fetch(e + 2, e0 % 2, True)
                    if e0:
                        store(e - 1, (e0 - 1) % 2)

                fetch(0, 0, False)
                fetch(1, 1, False)
                for e in range(3):
                    step(e)
                with po.Fori(0, (NE - 6) // 2) as i:
                    step(3, i)
                    step(4, i)
                for e in range(NE - 3, NE):
                    step(e)
                store(NE - 1, (NE - 1) % 2)
                for p in range(2):
                    po.wait_ge(sem[f"ysc{p}"], 8 * (B + NE))

                po.wait_ge(sem["flag"], l + 1)
                more = po.value_load(flagi[0:1, 0:1], min_val=0, max_val=1)
                with po.If(more > 0):
                    s = lambda n: sem[f"{n}{l}"]
                    po.sem_inc(s("od"), 1)
                    with po.Fori(0, 2) as bb:
                        with po.Fori(0, NE) as e:
                            J = bb * NE + e
                            po.wait_ge(s("ovd"), J * 2 + 1)
                            po.sem_inc(sem["passed"], 1)
                            gather(ico[:, 0:1], xgb[:, 0, :], H2, T - 1).then_inc(s("og"), 16)
                            po.wait_ge(s("ova"), J * 4 + 4)
                            po.sem_inc(sem["passed"], 1)
                            scatter(ico[:, 2:3], Y, yb[:, 0, :], T * TOPK - 1).then_inc(s("osc"), 16)
                            po.wait_ge(s("osc"), J * 16 + 16)
                            po.sem_inc(s("od"), 1)
                po.wait_ge(sem["rowi"], l + 1)
                for n in range(24):
                    j, k = n // 8, n % 8
                    P = TILES[j][1]
                    if n >= 4:
                        po.wait_ge(sem["cb"], 24 * l + n - 3)
                    gather(rowi[0:P, j, k:k + 1], gb[0:P, n % 4, :], Y, T * TOPK - 1).then_inc(sem[f"got{n % 4}"], 16)

            moe(0)
            lv = 0
            for n in range(6):
                P = TILES[n // 2][1]
                f = lambda v: v[0:P, 0:4 * P].rearrange("p (h i) -> p h i", h=4)
                po.wait_ge(sem["nmat"], n + 1)
                for k in range(6 if P == 128 else 5):
                    if lv >= 2:
                        po.wait_ge(sem["y_ps"], lv - 1)
                    m = C("mask")[0:P, k * 128:k * 128 + P].unsqueeze(1).broadcast_to([P, 4, P])
                    po.tensor_tensor(f(ubuf[:, lv % 2, :]), f(nbuf[:, 0, :]), m, ALU.mult).then_inc(sem["um"], 1)
                    lv += 1
            po.wait_ge(sem["cc"], 1)
            po.dma_start(t["cconv"], cc3[:, :, :, :]).then_inc(sem["st_small"], 16)
            po.wait_ge(sem["s_new"], 10)
            for g in range(2):
                po.dma_start(t["S"][g, :, :, :], sst[:, g, :, :]).then_inc(sem["st_small"], 16)
            po.wait_ge(sem["st_small"], 16 * 5)
            moe(1)


def constants():
    c = np.zeros((128, CST_N), np.float32)
    m, i = np.arange(128)[:, None], np.arange(128)[None, :]

    def put(name, v):
        c[:, CST[name][0]:CST[name][1]] = v

    put("ident", m == i)
    put("ones", 1)
    put("tri", (m <= i) & (m // CH == i // CH))
    put("same", m // CH == i // CH)
    put("mask", np.concatenate([(m // (2 * s) == i // (2 * s)) & (i // s % 2 == 1) & (m // s % 2 == 0)
                                for s in LEVELS], axis=1))
    put("before", m < i)
    g = np.arange(8)
    put("lower", (g[None, :] < g[:, None]).reshape(1, 64))
    put("iota", np.arange(384))
    put("tok", m + 128 * np.arange(3) - LIM)
    put("slot", m)
    put("eps", np.array([EPS, 128 * EPS]))
    return c


def kernel(**inputs):
    import concourse.bacc as bacc
    from concourse.bass_utils import run_bass_kernel_spmd

    a = {k: np.asarray(v) for k, v in inputs.items()}

    def chunks(v):
        v = v.reshape(v.shape[:-1] + (-1, 128))
        return np.moveaxis(v, -1, 0).reshape(128, -1)

    def tiles(w):
        return np.ascontiguousarray(w.reshape(KC, 128, -1, 2, 128).transpose(2, 1, 3, 0, 4)).reshape(-1, 128, UNIT)

    def halves(w):
        return np.ascontiguousarray(w.reshape(2, 4, 128, 512).transpose(0, 2, 1, 3)).reshape(2, 128, UNIT)

    def expert_units(l):
        gu = np.concatenate([np.concatenate([a["e_w_gate"][l], a["s_w_gate"][l][None]]),
                             np.concatenate([a["e_w_up"][l], a["s_w_up"][l][None]])], axis=-1)
        dn = np.concatenate([a["e_w_down"][l], a["s_w_down"][l][None]])
        out = np.empty((NE + 1, 3, 128, UNIT), np.float32)
        out[:, 0:2] = gu.reshape(NE + 1, 2, 4, 128, 512).transpose(0, 1, 3, 2, 4).reshape(NE + 1, 2, 128, UNIT)
        out[:, 2] = dn.reshape(NE + 1, 2, 128, D).transpose(0, 2, 1, 3).reshape(NE + 1, 128, UNIT)
        return out.reshape(-1, 128, UNIT)

    small = np.zeros((128, SML_N), np.float32)

    def put(name, v):
        small[:, SML[name][0]:SML[name][1]] = v

    cond = np.stack([a["c_prompt"][0], a["c_sample"][0]])
    put("cond", cond.reshape(2, KC, 128).transpose(2, 1, 0).reshape(128, 16))
    norms = np.stack([a["norm1_g"][0], a["norm2_g"][0], a["norm1_g"][1], a["norm2_g"][1], a["final_g"]])
    put("norms", chunks(norms))
    put("bmod", chunks(a["b_mod"]))
    put("aconv", a["a_conv_w"][0].reshape(4, 4, 128).transpose(2, 1, 0).reshape(128, 16))
    put("aconvb", chunks(a["a_conv_b"][0]))
    put("abr", chunks(a["a_b_r"][0]))
    put("abi", chunks(a["a_b_i"][0]))
    put("alam", chunks(a["a_lambda"][0]))
    put("ah0", chunks(a["state_a_h"][0, 0]))
    put("astate", a["state_a_conv"][0, 0].reshape(3, 4, 128).transpose(2, 1, 0).reshape(128, 12))
    put("cconv", a["c_conv_w"][0].reshape(4, 24, 128).transpose(2, 1, 0).reshape(128, 96))
    put("cstate", a["state_c_conv"][0, 0].reshape(3, 24, 128).transpose(2, 1, 0).reshape(128, 72))
    put("cnorm", a["c_norm_g"][0][:, None])
    put("alog", a["c_A_log"][0][None])
    put("dtb", a["c_dt_bias"][0][None])
    put("rb", a["router_bias"].reshape(1, 128))
    put("router", a["router_w"].reshape(2, KC, 128, NE).transpose(2, 0, 1, 3).reshape(128, 1024))
    w1 = a["w_in1"][0]
    put("wab", w1[:, 4096:4112].reshape(KC, 128, 16).transpose(1, 0, 2).reshape(128, 128))

    table = a["b_rel_bias"][0]

    def band(q0, nq, nk):
        rel = np.clip((q0 + np.arange(nq))[:, None] - np.arange(nk)[None, :], -128, 128) + 128
        return np.ascontiguousarray(table[:, rel].transpose(1, 0, 2))

    x = np.concatenate([a["x_prompt"][0], a["x_sample"][0]])
    w0 = a["w_in0"][0]
    arrays = {
        "small": small, "const": constants(),
        "x": np.ascontiguousarray(x.reshape(T, KC, 128).transpose(2, 1, 0)),
        "biasP0": band(0, 128, 128), "biasP1": band(128, 128, 256), "biasS": band(256, NS, T),
        "kcache": np.ascontiguousarray(a["cache_b_k"][0, 0].reshape(NP_, 4, 128).transpose(2, 1, 0)),
        "vcache": np.ascontiguousarray(a["cache_b_v"][0, 0].reshape(2, 128, 512).transpose(1, 0, 2)),
        "wr": np.ascontiguousarray(a["a_w_r"][0].reshape(4, 2, 64, 64).transpose(2, 1, 0, 3)),
        "wi": np.ascontiguousarray(a["a_w_i"][0].reshape(4, 2, 64, 64).transpose(2, 1, 0, 3)),
        "S0": np.ascontiguousarray(a["state_c_S"][0, 0].transpose(1, 0, 2)),
        "wmod": np.concatenate([tiles(a["w_mod"][0]), tiles(a["w_mod"][1])]),
        "win0": np.concatenate([tiles(w0[:, 0:2048]), halves(w0[:, 2048:2560])]),
        "wout0": tiles(a["w_out0"][0]),
        "win1": tiles(w1[:, 0:4096]),
        "wout1": tiles(a["w_out1"][0]),
        "wexp": np.concatenate([expert_units(0), expert_units(1)]),
    }
    outs = {"y": (128, KC, T), "k": (128, 4, T), "v": (T, 512), "aconv": (128, 4, 2, 3), "ah": (128, 4, 2),
            "cconv": (128, 24, 2, 3), "S": (2, 128, HC, 128)}
    nc = bacc.Bacc("TRN2", target_bir_lowering=False, num_devices=1)
    t = {n: nc.dram_tensor(f"in_{n}", v.shape, F32, kind="ExternalInput").ap() for n, v in arrays.items()}
    t.update({n: nc.dram_tensor(f"out_{n}", s, F32, kind="ExternalOutput").ap() for n, s in outs.items()})
    t["H2"] = nc.dram_tensor("h_rows", (T, D), F32, kind="Internal").ap()
    t["Y"] = nc.dram_tensor("expert_rows", (T * TOPK, D), F32, kind="Internal").ap()
    build(nc, t)
    r = run_bass_kernel_spmd(nc, [{f"in_{n}": v for n, v in arrays.items()}], core_ids=[0]).results[0]
    r = {n: r[f"out_{n}"] for n in outs}

    y = r["y"].transpose(2, 1, 0).reshape(T, D)
    k = r["k"].transpose(2, 1, 0).reshape(T, HB, DHB)
    v = r["v"].reshape(T, HB, DHB)
    conv_a = r["aconv"].transpose(2, 3, 1, 0).reshape(2, 3, 512)
    h_a = r["ah"].transpose(2, 1, 0).reshape(2, 512)
    conv_c = r["cconv"].transpose(2, 3, 1, 0).reshape(2, 3, 3072)
    S = r["S"].transpose(0, 2, 1, 3)
    c = np.ascontiguousarray
    return (c(y[None, 0:NP_]), c(y[None, NP_:T]), c(k[None, None, 0:NP_]), c(k[None, None, NP_:T]),
            c(v[None, None, 0:NP_]), c(v[None, None, NP_:T]), c(conv_a[None, 0:1]), c(conv_a[None, 1:2]),
            c(h_a[None, 0:1]), c(h_a[None, 1:2]), c(conv_c[None, 0:1]), c(conv_c[None, 1:2]),
            c(S[None, 0:1]), c(S[None, 1:2]))
```

```python
import numpy as np
import concourse.bass as bass
from concourse import mybir

F32 = mybir.dt.float32
I32 = mybir.dt.int32
BF16 = mybir.dt.bfloat16
ALU = mybir.AluOpType
ACT = mybir.ActivationFunctionType
AX = mybir.AxisListType

D, NP_, NS, T = 1024, 256, 32, 288
KC = D // 128
GROUPS = [(0, NP_), (NP_, T)]
TILES = [(0, 128), (128, 128), (256, 32)]
CH, EPS = 64, 1e-6
HB, DHB, HC = 8, 64, 8
NE, EG, TOPK, DE = 64, 8, 8, 256
CAP = 96
LIM = 4096
XPAD = NP_ + NS + 6
SEG = NP_ + 3
XW = XPAD - 3
UNIT = 2048
NU = 6
LEVELS = [1, 2, 4, 8, 16, 32]
LEV_N = [6, 6, 5]
STEP0 = [0, 12, 24]
assert T % CAP == 0 and T // CAP == 3

CST_W = dict(ident=128, ones=128, tri=128, same=128, mask=6 * 128, before=128, lower=64, iota=T,
             slot=1, eps=2, pick=31, l2=2)
SML_W = dict(cond=16, norms=40, bmod=96, aconv=16, aconvb=4, abr=4, abi=4, alam=4, ah0=4, astate=12,
             cconv=96, cstate=72, cnorm=1, alog=8, dtb=8, rb=128, router=1024, wab=128)


def places(widths):
    at, out = 0, {}
    for name, w in widths.items():
        out[name] = (at, at + w)
        at += w
    return out, at


CST, CST_N = places(CST_W)
SML, SML_N = places(SML_W)

MOD_U, IN0_U, OUT0_U, MOE_U, IN1_U = 24, 10, 4, 3 + 3 * NE, 16
U_MOD0 = 0
U_IN0 = U_MOD0 + MOD_U
U_MOD1 = U_IN0 + IN0_U
U_OUT0 = U_MOD1 + MOD_U
MOD_B = MOD_U // 2
U_MOE0 = U_OUT0 + OUT0_U
U_IN1 = U_MOE0 + MOE_U
U_OUT1 = U_IN1 + IN1_U
U_MOE1 = U_OUT1 + 4
U_MODS = [U_MOD0, U_MOD1]
U_MOES = [U_MOE0, U_MOE1]

SEMS = """ld_small ld_att ld_state st_mix st_small st_out w_used mod_row mod_t cond lamn lame lam sq ss rms h
 proj_ps proj_ev v_ps v_ev pad conv hst gate_ps gate_i lru_a lru_w lru_s lru_g ya
 s_ps s_sm p_exp p_nrm pt_ps pt_sb pv_ps pv_sb out_ps out_x
 tm_ps tm_sb h2_st lg_ps lgz xgz score mask rank_ps flag rowi sel sel_ps
 shu_ps shu_sb shh sht_ps sht_sb shd_ps shd_sb
 ig isx xg0 xg1 trx xta xtb up sg hd trh ht dn ya_e yb_e ysc0 ysc1 got0 got1 got2 got3 cb acc_ps acc_x
 ab_ps ab_act ab_sb ab_e gcum_ps gcum_e gdec
 padc cc cacc csilu lsq lss lrms qk_n gb_ps gb_e ldif lexp nmat kk_ps tk_ps tk_sb um
 y_ps y_sb z_ps xd u_ps batch s0 ws_ps vn o_ps su_ps s_new o_sb osq oss orms on ozs
 dve act passed""".split()
OVF = """od ovi ovd ova ovp og osc ow osel osel_ps""".split()


def build(nc, t):
    sem = {n: nc.alloc_semaphore(n) for n in SEMS}
    for l in range(2):
        for n in OVF:
            sem[f"{n}{l}"] = nc.alloc_semaphore(f"{n}{l}")
    w_loaded = [nc.alloc_semaphore(f"w_loaded{u}") for u in range(NU)]

    def sb(name, shape, dt=F32):
        return nc.alloc_sbuf_tensor(name, shape, dt)

    ring = sb("ring", [128, NU, UNIT])
    cst = sb("cst", [128, CST_N])
    sml = sb("sml", [128, SML_N])
    x = sb("x", [128, KC, T])
    h = sb("h", [128, KC, T])
    ycat = sb("ycat", [128, KC, T])
    rms = sb("rms", [128, T])
    condT = sb("condT", [128, KC, 2])
    mod = sb("mod", [128, 2, 48, 2])
    scale1 = sb("scale1", [128, 2, 2, KC, 2])
    hst = sb("hst", [128, 4, 2])
    cst3 = sb("cst3", [128, 4, 2, 3])
    cc3 = sb("cc3", [128, 24, 2, 3])
    arena = sb("arena", [128, 29400])
    ps = [nc.alloc_psum_tensor(f"ps{b}", [128, 512], F32) for b in range(8)]

    def C(name, p=128):
        return cst[0:p, CST[name][0]:CST[name][1]]

    def M(name, p=128):
        return sml[0:p, SML[name][0]:SML[name][1]]

    def carver(at):

        def carve(*dims):
            n = int(np.prod(dims))
            a = arena[:, at[0]:at[0] + n]
            at[0] += n
            assert at[0] <= 29400, at[0]
            if len(dims) == 2:
                a = a.rearrange("p (a b) -> p a b", a=dims[0])
            if len(dims) == 3:
                a = a.rearrange("p (a b c) -> p a b c", a=dims[0], b=dims[1])
            return a
        return carve

    ident, ones = C("ident"), C("ones")

    place = [0]
    cv = carver(place)
    xpad, gaT, qT, kT = cv(4, XPAD), cv(4, T), cv(4, T), cv(4, T)
    ksT = cv(4, T)
    vtm, vcache = cv(3, 512), cv(2, 512)
    biasP0, biasP1, biasS = cv(HB, 128), cv(HB, 256), cv(HB, T)
    bdr, bdi = cv(4, 128), cv(4, 128)
    xc, rg, ig_, aa, tt_ = (cv(4, XW) for _ in range(5))
    hh = cv(4, XW)
    lamw = cv(8, 4)
    s_sb, mx, rsum = cv(2, T), cv(2, 2), cv(2, 1)
    pT = cv(2, 3, 128)
    modrow = cv(2, 512)

    place = [0]
    cv = carver(place)
    qf, kf, vf, zf = (cv(HC, T) for _ in range(4))
    kdec = cv(3, HC, 128)
    share = cv(1, 5400)[:, 0, :]
    uu = share[:, 0:3072].rearrange("p (t h v) -> p t h v", t=3, h=HC)
    atm = share[:, 3072:3072 + 2304]
    raw = share[:, 0:2 * 4 * XPAD].rearrange("p (a c x) -> p a c x", a=2, c=4)
    cacc = share[:, 2400:2400 + 2 * 4 * XW].rearrange("p (a c x) -> p a c x", a=2, c=4)
    sst = cv(2, HC, 128)
    lbuf = cv(2, 512)
    SQ0 = place[0]
    nbuf, xbuf, dbuf, ybuf, ubuf, kbe, vbe, egb = (cv(2, 512) for _ in range(8))
    sqb = arena[:, SQ0:SQ0 + 16 * T].rearrange("p (c x) -> p c x", c=16)
    kdcol = cv(3, 8)
    gtm, btm, spt, gcol, glast, begc = (cv(3, 8) for _ in range(6))
    spw = cv(6, 24)
    sdec = cv(5, HC)

    def att(t):
        P = TILES[t][1]
        return atm[:, t * 1024:t * 1024 + HC * P].rearrange("p (h i) -> p h i", h=HC)

    def four(buf, P):
        return buf[:, 0:4 * P].rearrange("p (h i) -> p h i", h=4)

    place = [0]
    cv = carver(place)
    ysh = cv(3, D)
    xgb, yb = cv(2, D), cv(2, D)
    xgT = cv(2, KC, CAP)
    gb = cv(4, D)
    selb = cv(2, 3, 4 * CAP).bitcast(BF16)
    silu_b, hid = cv(1, DE)[:, 0, :], cv(1, DE)[:, 0, :]
    hidT = cv(2, CAP)
    shs, shu_, shh_, shT = cv(3, DE), cv(3, DE), cv(3, DE), cv(3, 2, 128)
    lg, score, selv, msk, gates, rk, tmp1, tmp2 = (cv(3, NE) for _ in range(8))
    top2, gsc, gcmp, geq, grk, top8, gsum = cv(3, 8, 8), cv(3, 8), cv(3, 8, 8), cv(3, 8, 8), cv(3, 8), cv(3, 8), cv(3, 1)
    tg = cv(3, NE, 3).bitcast(BF16)
    rkb, slots = cv(3, NE // 2).bitcast(BF16), cv(1, CAP // 2)[:, 0, :].bitcast(BF16)
    idxf = cv(2, NE)
    rowif = cv(3, 8)
    cntf, start, srow = cv(1, 66)[:, 0, :], cv(1, NE)[:, 0, :], cv(1, NE)[:, 0, :]
    rowi = cv(3, 8).bitcast(I32)
    idx = cv(NE, 3).bitcast(I32)
    icg = cv(2, 1).bitcast(I32)
    ics = cv(2, 1).bitcast(I32)
    ico = cv(1, 3)[:, 0, :].bitcast(I32)
    flagi = sb("flagi", [1, 1], I32)

    rk_flat, rkb_flat = rk.rearrange("p a b -> p (a b)"), rkb.rearrange("p a b -> p (a b)")
    H2, Y = t["H2"], t["Y"]

    class Chain:

        def __init__(self, eng, own):
            self.eng, self.own, self.n = eng, own, {}

        def go(self, ins, name=None):
            name = name or self.own
            self.n[name] = self.n.get(name, 0) + 1
            ins.then_inc(sem[name], 1)
            self.last = name

        def __call__(self, ins, name=None):
            self.go(ins, name)
            self.eng.wait_ge(sem[self.last], self.n[self.last])

    def unit(n):
        return ring[:, n % NU, :]

    def wait_unit(eng, n):
        eng.wait_ge(w_loaded[n % NU], 16 * (n // NU + 1))

    with nc.Block() as block:
        @block.sync
        def _(sp):
            def used(n):
                if n < U_IN0:
                    return "w_used", n + 1
                if U_MOD1 <= n < U_OUT0:
                    return "w_used", MOD_U + (n - U_MOD1) + 1
                if n < U_MOD1:
                    q = n - U_IN0
                    return ("proj_ps", 2 * q + 2) if q < 8 else ("v_ps", q - 7)
                if n < U_MOE0:
                    return "out_ps", 2 * (n - U_OUT0) + 2
                if U_IN1 <= n < U_OUT1:
                    return "proj_ps", 16 + 2 * (n - U_IN1) + 2
                if U_OUT1 <= n < U_MOE1:
                    return "out_ps", 8 + 2 * (n - U_OUT1) + 2
                l = 0 if n < U_IN1 else 1
                m, B = n - U_MOES[l], NE * l
                if m < 2:
                    return "shu_ps", 2 * l + m + 1
                if m == 2:
                    return "shd_ps", 3 * l + 3
                if m < 5:
                    return "up", B + 1
                if m == MOE_U - 1:
                    return "dn", B + NE
                e, r = (m - 5) // 3 + 1, (m - 5) % 3
                return ("up", B + e + 1) if r < 2 else ("dn", B + e)

            def load(n, src, i=None, per=0):
                if n >= NU:
                    name, v = used(n - NU)
                    sp.wait_ge(sem[name], v if i is None else i * per + v)
                sp.dma_start(ring[:, n % NU, :], src).then_inc(w_loaded[n % NU], 16)

            def at(w, i, k, n):
                return w[bass.ds(i * k + n, 1), :, :].rearrange("a p n -> p (a n)")

            for n in range(NU):
                load(n, t["wmod"][n, :, :])
            with sp.Fori(0, MOD_U // NU - 1) as i:
                for u in range(NU):
                    load(NU + u, at(t["wmod"], i, NU, NU + u), i, NU)
            for n in range(IN0_U):
                load(U_IN0 + n, t["win0"][n, :, :])
            for n in range(NU):
                load(U_MOD1 + n, t["wmod"][MOD_U + n, :, :])
            with sp.Fori(0, MOD_U // NU - 1) as i:
                for u in range(NU):
                    load(U_MOD1 + NU + u, at(t["wmod"], i, NU, MOD_U + NU + u), i, NU)
            for n in range(4):
                load(U_OUT0 + n, t["wout0"][n, :, :])

            def moe_loads(l):
                b, w = U_MOES[l], t["wexp"]
                W0 = l * (NE + 1) * 3
                for n in range(3):
                    load(b + n, w[W0 + 3 * NE + n, :, :])
                for n in range(2):
                    load(b + 3 + n, w[W0 + n, :, :])

                def pair(e0, i=None):
                    for n, j in enumerate((3 * e0, 3 * e0 + 1, 3 * e0 - 1)):
                        m = b + 5 + 3 * (e0 - 1) + n
                        load(m, w[W0 + j, :, :] if i is None else at(w, i, 6, W0 + j), i, 2)

                pair(1)
                pair(2)
                with sp.Fori(0, (NE - 4) // 2) as i:
                    pair(3, i)
                    pair(4, i)
                pair(NE - 1)
                load(b + MOE_U - 1, w[W0 + 3 * NE - 1, :, :])
                sp.wait_ge(sem["flag"], l + 1)
                more = sp.value_load(flagi[0:1, 0:1], min_val=0, max_val=1)
                with sp.If(more > 0):
                    sp.wait_ge(sem["dn"], NE * (l + 1))
                    with sp.Fori(0, 2) as bb:
                        with sp.Fori(0, NE) as e:
                            sp.wait_ge(sem[f"od{l}"], bb * NE + e + 1)
                            for n in range(3):
                                sp.dma_start(ring[:, n, :], at(w, e, 3, W0 + n)).then_inc(sem[f"ow{l}"], 16)
                    sp.wait_ge(sem[f"od{l}"], 2 * NE + 1)

            moe_loads(0)
            for n in range(IN1_U):
                load(U_IN1 + n, t["win1"][n, :, :])
            for n in range(4):
                load(U_OUT1 + n, t["wout1"][n, :, :])
            moe_loads(1)
            sp.wait_ge(sem["h"], 5)
            sp.dma_start(t["y"], h[:, :, :]).then_inc(sem["st_out"], 16)
            sp.wait_ge(sem["st_out"], 16)
            sp.wait_ge(sem["st_mix"], 16 * 4)
            sp.wait_ge(sem["st_small"], 16 * 5)

        @block.tensor
        def _(pe):
            mm = nc.tensor.matmul
            tr = nc.tensor.transpose

            def mod_unit(l, n, bank):
                b, q = n // 2, n % 2
                wait_unit(pe, U_MODS[l] + n)
                for k in range(4):
                    last = mm(ps[bank][0:2, :], condT[:, 4 * q + k, :], unit(U_MODS[l] + n)[:, k * 512:(k + 1) * 512],
                              start=(q == 0 and k == 0), stop=(q == 1 and k == 3))
                last.then_inc(sem["w_used"], 1)

            def mod_turn(l, b, bank):
                pe.wait_ge(sem["mod_row"], MOD_B * l + b + 1)
                for q in range(4):
                    last = tr(ps[bank][:, (4 * b + q) * 2:(4 * b + q) * 2 + 2], modrow[0:2, b % 2, q * 128:(q + 1) * 128],
                              ident[0:2, 0:2])
                last.then_inc(sem["mod_t"], 1)

            def sum_squares(k):
                pe.wait_ge(sem["sq"], k + 1)
                for c in range(KC):
                    last = mm(ps[7][:, 0:T], ones, h[:, c, :], start=(c == 0), stop=(c == KC - 1))
                last.then_inc(sem["ss"], 1)

            def project(u0, tiles, base, rhs, rdy):
                for i in range(tiles):
                    n = u0 + i // 2
                    if i % 2 == 0:
                        wait_unit(pe, n)
                    if base + i >= 4:
                        pe.wait_ge(sem[rdy], base + i - 3)
                    for k in range(KC):
                        a = (i % 2) * KC + k
                        last = mm(ps[i % 4][:, 0:T], unit(n)[:, a * 128:(a + 1) * 128], rhs[:, k, :],
                                  start=(k == 0), stop=(k == KC - 1))
                    last.then_inc(sem["proj_ps" if rdy == "proj_ev" else "out_ps"], 1)

            sum_squares(0)
            pe.wait_ge(sem["cond"], 1)
            for b in range(MOD_B):
                if b >= 2:
                    pe.wait_ge(sem["mod_row"], b - 1)
                mod_unit(0, 2 * b, b % 2)
                mod_unit(0, 2 * b + 1, b % 2)
                if b:
                    mod_turn(0, b - 1, 2)
            mod_turn(0, MOD_B - 1, 2)
            pe.wait_ge(sem["h"], 1)
            project(U_IN0, 16, 0, h, "proj_ev")
            for kq in range(2):
                wait_unit(pe, U_IN0 + 8 + kq)
                for j, (t0, P) in enumerate(TILES):
                    for k in range(4):
                        last = mm(ps[4 + j][0:P, :], h[:, kq * 4 + k, t0:t0 + P],
                                  unit(U_IN0 + 8 + kq)[:, k * 512:(k + 1) * 512],
                                  start=(kq == 0 and k == 0), stop=(kq == 1 and k == 3))
                last.then_inc(sem["v_ps"], 1)
            pe.wait_ge(sem["ld_att"], 16 * 9)
            pe.wait_ge(sem["conv"], 1)
            pe.wait_ge(sem["proj_ev"], 16)
            for c in range(4):
                last = mm(ps[c][:, 0:XW], bdr[:, c, :], xc[:, c, :], start=True, stop=True)
            last.then_inc(sem["gate_ps"], 1)
            pe.wait_ge(sem["v_ev"], 1)
            for c in range(4):
                last = mm(ps[4 + c][:, 0:XW], bdi[:, c, :], xc[:, c, :], start=True, stop=True)
            last.then_inc(sem["gate_ps"], 1)
            units = [(j, hd) for j in range(3) for hd in range(HB)]

            def scores(n):
                j, hd = units[n]
                t0, P = TILES[j]
                b, c = DHB * (hd % 2), hd // 2
                nk = (128, 256, T)[j]
                keys = ksT if j == 2 else kT
                if n >= 2:
                    pe.wait_ge(sem["s_sm"], n - 1)
                mm(ps[n % 2][0:P, 0:nk], qT[b:b + DHB, c, t0:t0 + P], keys[b:b + DHB, c, 0:nk],
                   start=True, stop=True).then_inc(sem["s_ps"], 1)

            pe.wait_ge(sem["gate_i"], 1)
            scores(0)
            for n, (j, hd) in enumerate(units):
                t0, P = TILES[j]
                if n + 1 < len(units):
                    scores(n + 1)
                if n >= 2 and n % 2 == 0:
                    pe.wait_ge(sem["mod_row"], MOD_B + n // 2)
                mod_unit(1, n, 6)
                if n >= 2 and n % 2 == 0:
                    mod_turn(1, n // 2 - 1, 7)
                kts = [(0, 128)] if j == 0 else [(0, 128), (1, 128)] if j == 1 else [(0, 128), (1, 128), (2, 32)]
                pe.wait_ge(sem["p_nrm"], n + 1)
                if n >= 2:
                    pe.wait_ge(sem["pt_sb"], n - 1)
                for kt, K in kts:
                    last = tr(ps[2 + n % 2][0:K, kt * 128:kt * 128 + P],
                              s_sb[0:P, n % 2, kt * 128:kt * 128 + K], ident[0:P, 0:P])
                last.then_inc(sem["pt_ps"], 1)
                pe.wait_ge(sem["pt_sb"], n + 1)
                if n >= 2:
                    pe.wait_ge(sem["pv_sb"], n - 1)
                c = hd // 2
                for kt, K in kts:
                    val = vcache if (j == 2 and kt < 2) else vtm
                    last = mm(ps[4 + n % 2][:, 0:P], val[0:K, kt, c * 128:(c + 1) * 128], pT[0:K, n % 2, kt, 0:P],
                              start=(kt == 0), stop=(kt == kts[-1][0]))
                last.then_inc(sem["pv_ps"], 1)
            mod_turn(1, MOD_B - 1, 7)
            pe.wait_ge(sem["ya"], 1)
            pe.wait_ge(sem["pv_sb"], len(units))
            project(U_OUT0, 8, 0, ycat, "out_x")

            def moe(l):
                B, u0 = NE * l, U_MOES[l]
                pe.wait_ge(sem["h"], 2 * l + 2)
                for j, (t0, P) in enumerate(TILES):
                    for k in range(KC):
                        rw = M("router")[:, l * 512 + k * 64:l * 512 + (k + 1) * 64]
                        last = mm(ps[6][0:P, j * 64:(j + 1) * 64], h[:, k, t0:t0 + P], rw,
                                  start=(k == 0), stop=(k == KC - 1))
                last.then_inc(sem["lg_ps"], 1)
                for j, (t0, P) in enumerate(TILES):
                    for k in range(KC):
                        last = tr(ps[2 * j + k // 4][0:P, (k % 4) * 128:(k % 4 + 1) * 128], h[:, k, t0:t0 + P], ident)
                    last.then_inc(sem["tm_ps"], 1)
                pe.wait_ge(sem["tm_sb"], 3 * (l + 1))
                for q in range(2):
                    wait_unit(pe, u0 + q)
                    for j, (t0, P) in enumerate(TILES):
                        for k in range(4):
                            last = mm(ps[j][0:P, :], h[:, 4 * q + k, t0:t0 + P],
                                      unit(u0 + q)[:, k * 512:(k + 1) * 512],
                                      start=(q == 0 and k == 0), stop=(q == 1 and k == 3))
                    last.then_inc(sem["shu_ps"], 1)
                for j, (t0, P) in enumerate(TILES):
                    pe.wait_ge(sem["shh"], 3 * l + j + 1)
                    for a in range(2):
                        last = tr(ps[3][:, a * 128:a * 128 + P], shh_[0:P, j, a * 128:(a + 1) * 128],
                                  ident[0:P, 0:P])
                    last.then_inc(sem["sht_ps"], 1)
                    pe.wait_ge(sem["sht_sb"], 3 * l + j + 1)
                for j, (t0, P) in enumerate(TILES):
                    if j == 0:
                        wait_unit(pe, u0 + 2)
                        pe.wait_ge(sem["shu_sb"], 3 * (l + 1))
                    b0, b1 = ((0, 1), (4, 5), (2, 3))[j]
                    for hf, bk in ((0, b0), (1, b1)):
                        for a in range(2):
                            last = mm(ps[bk][0:P, :], shT[:, j, a, 0:P],
                                      unit(u0 + 2)[:, a * D + hf * 512:a * D + (hf + 1) * 512],
                                      start=(a == 0), stop=(a == 1))
                    last.then_inc(sem["shd_ps"], 1)
                pe.wait_ge(sem["mask"], l + 1)
                for j, (t0, P) in enumerate(TILES):
                    for jj in range(j + 1):
                        PP = TILES[jj][1]
                        w = C("before")[0:PP, 0:P] if jj == j else ones[0:PP, 0:P]
                        last = mm(ps[7][0:P, j * 64:(j + 1) * 64], w, msk[0:PP, jj, :], start=(jj == 0), stop=(jj == j))
                for jj, (t0, PP) in enumerate(TILES):
                    last = mm(ps[7][:, 192:256], ones[0:PP, :], msk[0:PP, jj, :], start=(jj == 0), stop=(jj == 2))
                last.then_inc(sem["rank_ps"], 1)

                def slot_tables(sel_name, ps_name, base):
                    for g in range(8):
                        pe.wait_ge(sem[sel_name], base + g + 1)
                        for e in range(8):
                            for j, (t0, P) in enumerate(TILES):
                                last = mm(ps[6][0:CAP, (8 * g + e) * 5:(8 * g + e) * 5 + 5],
                                          selb[0:P, g % 2, j, e * CAP:(e + 1) * CAP], tg[0:P, j, 8 * g + e, 0:5],
                                          start=(j == 0), stop=(j == 2))
                        last.then_inc(sem[ps_name], 1)

                slot_tables("sel", "sel_ps", 8 * l)

                pe.wait_ge(sem["shd_sb"], 3 * (l + 1))

                def take(e, p):
                    pe.wait_ge(sem[f"xg{p}"], e * 8 + (8 * (B - p) + 16))
                    for k in range(KC):
                        last = tr(ps[4 + k // 4][:, (k % 4) * CAP:(k % 4 + 1) * CAP],
                                  xgb[0:CAP, p, k * 128:(k + 1) * 128], ident[0:CAP, 0:CAP])
                    last.then_inc(sem["trx"], 1)

                def up(e, p, n, i):
                    for q in range(2):
                        s = (n + q) % NU
                        v = 16 * ((n + q) // NU + 1)
                        pe.wait_ge(w_loaded[s], v if i is None else i * 16 + v)
                        for k in range(4):
                            last = mm(ps[2][0:CAP, :], xgT[:, p, 4 * q + k, :], ring[:, s, k * 512:(k + 1) * 512],
                                      start=(q == 0 and k == 0), stop=(q == 1 and k == 3))
                    last.then_inc(sem["up"], 1)

                def hidden(e):
                    pe.wait_ge(sem["hd"], e + (B + 1))
                    for a in range(2):
                        last = tr(ps[3][:, a * CAP:(a + 1) * CAP], hid[0:CAP, a * 128:(a + 1) * 128], ident[0:CAP, 0:CAP])
                    last.then_inc(sem["trh"], 1)

                def down(e, n, i, first=False):
                    pe.wait_ge(sem["ht"], e + (B + 1))
                    if not first:
                        pe.wait_ge(sem["ya_e"], e + B)
                        pe.wait_ge(sem["yb_e"], e + B)
                    s, v = n % NU, 16 * (n // NU + 1)
                    pe.wait_ge(w_loaded[s], v if i is None else i * 16 + v)
                    for a in range(2):
                        for hf in range(2):
                            last = mm(ps[hf][0:CAP, :], hidT[:, a, :], ring[:, s, a * D + hf * 512:a * D + (hf + 1) * 512],
                                      start=(a == 0), stop=(a == 1))
                    last.then_inc(sem["dn"], 1)

                take(0, 0)

                def step(e0, i=None):
                    e = e0 if i is None else i * 2 + e0
                    n = u0 + 3 + (0 if e0 == 0 else 2 + 3 * (e0 - 1))
                    if e0 > 0:
                        hidden(e - 1)
                    if e0 + 1 < NE:
                        pe.wait_ge(sem["xta"], e + (B + 1))
                        pe.wait_ge(sem["xtb"], e + (B + 1))
                        take(e + 1, (e0 + 1) % 2)
                    else:
                        pe.wait_ge(sem["xta"], e + (B + 1))
                        pe.wait_ge(sem["xtb"], e + (B + 1))
                    up(e, e0 % 2, n, i)
                    if e0 > 0:
                        down(e - 1, n + 2, i, first=(e0 == 1))

                for e in range(3):
                    step(e)
                with pe.Fori(0, (NE - 6) // 2) as i:
                    step(3, i)
                    step(4, i)
                for e in range(NE - 3, NE):
                    step(e)
                hidden(NE - 1)
                down(NE - 1, u0 + 3 + 2 + 3 * (NE - 1), None)

                pe.wait_ge(sem["flag"], l + 1)
                more = pe.value_load(flagi[0:1, 0:1], min_val=0, max_val=1)
                with pe.If(more > 0):
                    s = lambda n: sem[f"{n}{l}"]
                    pe.wait_ge(sem["ya_e"], B + NE)
                    pe.wait_ge(sem["yb_e"], B + NE)
                    with pe.Fori(0, 2) as bb:
                        for g in range(8):
                            pe.wait_ge(s("osel"), bb * 8 + (g + 1))
                            for e in range(8):
                                for j, (t0, P) in enumerate(TILES):
                                    last = mm(ps[6][0:CAP, (8 * g + e) * 5:(8 * g + e) * 5 + 5],
                                              selb[0:P, g % 2, j, e * CAP:(e + 1) * CAP], tg[0:P, j, 8 * g + e, 0:5],
                                              start=(j == 0), stop=(j == 2))
                            last.then_inc(s("osel_ps"), 1)
                        with pe.Fori(0, NE) as e:
                            J = bb * NE + e
                            pe.wait_ge(s("og"), J * 16 + 16)
                            for k in range(KC):
                                last = tr(ps[4 + k // 4][:, (k % 4) * CAP:(k % 4 + 1) * CAP],
                                          xgb[0:CAP, 0, k * 128:(k + 1) * 128], ident[0:CAP, 0:CAP])
                            last.then_inc(s("ovp"), 1)
                            pe.wait_ge(s("ova"), J * 4 + 1)
                            pe.wait_ge(s("ow"), J * 48 + 48)
                            for k in range(KC):
                                last = mm(ps[2][0:CAP, :], xgT[:, 0, k, :],
                                          ring[:, k // 4, (k % 4) * 512:(k % 4 + 1) * 512],
                                          start=(k == 0), stop=(k == KC - 1))
                            last.then_inc(s("ovp"), 1)
                            pe.wait_ge(s("ovd"), J * 2 + 2)
                            for a in range(2):
                                last = tr(ps[3][:, a * CAP:(a + 1) * CAP], hid[0:CAP, a * 128:(a + 1) * 128], ident[0:CAP, 0:CAP])
                            last.then_inc(s("ovp"), 1)
                            pe.wait_ge(s("ova"), J * 4 + 3)
                            for a in range(2):
                                for hf in range(2):
                                    last = mm(ps[hf][0:CAP, :], hidT[:, a, :],
                                              ring[:, 2, a * D + hf * 512:a * D + (hf + 1) * 512],
                                              start=(a == 0), stop=(a == 1))
                            last.then_inc(s("ovp"), 1)
                    pe.wait_ge(s("ova"), 8 * NE)
                pe.wait_ge(sem["ya_e"], B + NE)
                pe.wait_ge(sem["yb_e"], B + NE)
                for j, (t0, P) in enumerate(TILES):
                    pe.wait_ge(sem["cb"], 24 * l + 8 * (j + 1))
                    for k in range(KC):
                        last = tr(ps[2 * j + k // 4][:, (k % 4) * 128:(k % 4) * 128 + P],
                                  ysh[0:P, j, k * 128:(k + 1) * 128], ident[0:P, 0:P])
                    last.then_inc(sem["acc_ps"], 1)

            sum_squares(1)
            moe(0)

            sum_squares(2)
            pe.wait_ge(sem["h"], 3)
            for j, (t0, P) in enumerate(TILES):
                for k in range(KC):
                    last = mm(ps[6][0:P, j * 16:(j + 1) * 16], h[:, k, t0:t0 + P], M("wab")[:, k * 16:(k + 1) * 16],
                              start=(k == 0), stop=(k == KC - 1))
            last.then_inc(sem["ab_ps"], 1)
            pe.wait_ge(sem["acc_x"], 1)
            project(U_IN1, 32, 16, h, "proj_ev")
            pe.wait_ge(sem["ab_sb"], 1)
            for j, (t0, P) in enumerate(TILES):
                mm(ps[6][0:P, 64 + j * 8:72 + j * 8], C("tri")[0:P, 0:P], gtm[0:P, j, :], start=True, stop=True)
                last = mm(ps[6][0:P, 96 + j * 8:104 + j * 8], C("same")[0:P, 0:P], gtm[0:P, j, :],
                          start=True, stop=True)
            last.then_inc(sem["gcum_ps"], 1)
            pe.wait_ge(sem["proj_ev"], 48)
            for n in range(16):
                if n % 4 == 0:
                    pe.wait_ge(sem["lsq"], n // 4 + 1)
                last = mm(ps[0][0:16, 0:T], C("pick")[:, 15 - n:31 - n], sqb[:, n, :], start=(n == 0), stop=(n == 15))
            last.then_inc(sem["lss"], 1)
            for n in range(16):
                pe.wait_ge(sem["qk_n"], max(n - 2, 1))
                mm(ps[1 + n % 4][:, 0:T], ident[0:16, n:n + 1].broadcast_to([16, 128]), lbuf[0:16, 0, 0:T],
                   start=True, stop=True).then_inc(sem["lss"], 1)

            for j, (t0, P) in enumerate(TILES):
                blk = lambda b: ps[b][:, 0:4 * P].rearrange("p (h i) -> p h i", h=4)
                u_ = lambda buf: four(buf, P)[0:P]
                for g in range(2):
                    n = 2 * j + g
                    hs = range(4 * g, 4 * g + 4)
                    if g:
                        pe.wait_ge(sem["tk_sb"], n)
                        pe.wait_ge(sem["gb_e"], n)
                    elif j:
                        pe.wait_ge(sem["batch"], n)
                    else:
                        pe.wait_ge(sem["qk_n"], 17)
                        pe.wait_ge(sem["gdec"], 1)
                    for a, hd in enumerate(hs):
                        last = mm(blk(0)[:, a, :], gtm[0:P, j, hd:hd + 1].broadcast_to([P, 128]), C("tri")[0:P, 0:P],
                                  start=True, stop=True)
                    last.then_inc(sem["gb_ps"], 1)
                    for a, hd in enumerate(hs):
                        mm(blk(1)[0:P, a, :], btm[0:P, j, hd:hd + 1].broadcast_to([P, P]), ident[0:P, 0:P],
                           start=True, stop=True)
                    for a, hd in enumerate(hs):
                        mm(blk(2)[0:P, a, :], kf[:, hd, t0:t0 + P], kf[:, hd, t0:t0 + P], start=True, stop=True)
                    for a, hd in enumerate(hs):
                        last = mm(blk(3)[0:P, a, :], kf[:, hd, t0:t0 + P], qf[:, hd, t0:t0 + P], start=True, stop=True)
                    last.then_inc(sem["kk_ps"], 1)
                    for a, hd in enumerate(hs):
                        tr(ps[4][0:P, a * 128:(a + 1) * 128], kf[:, hd, t0:t0 + P], ident)
                        last = tr(ps[5][0:P, a * 128:(a + 1) * 128], vf[:, hd, t0:t0 + P], ident)
                    last.then_inc(sem["tk_ps"], 1)
                for lv in range(LEV_N[j]):
                    for g in range(2):
                        m = STEP0[j] + 2 * lv + g
                        pe.wait_ge(sem["um"], m + 1)
                        pe.wait_ge(sem["xd"], 2 * (j + 1) + STEP0[j] if lv == 0 else 2 * (j + 1) + m - 1)
                        for a in range(4):
                            last = mm(blk(6 + g)[0:P, a, :], u_(ubuf[:, g, :])[:, a, :], u_(dbuf[:, g, :])[:, a, :],
                                      start=True, stop=True)
                        last.then_inc(sem["y_ps"], 1)
                    for g in range(2):
                        pe.wait_ge(sem["y_sb"], STEP0[j] + 2 * lv + g + 1)
                        if lv == 0 and g:
                            pe.wait_ge(sem["tk_sb"], 2 * (j + 1))
                        for a in range(4):
                            mm(blk(2 * g)[0:P, a, :], u_(xbuf[:, g, :])[:, a, :], u_(ybuf[:, g, :])[:, a, :],
                               start=True, stop=True)
                        for a in range(4):
                            last = mm(blk(2 * g + 1)[0:P, a, :], u_(ybuf[:, g, :])[:, a, :], u_(xbuf[:, g, :])[:, a, :],
                                      start=True, stop=True)
                        last.then_inc(sem["z_ps"], 1)
                for g in range(2):
                    pe.wait_ge(sem["xd"], 2 * (j + 1) + STEP0[j] + 2 * LEV_N[j] - 1 + g)
                    pe.wait_ge(sem["tk_sb"], 2 * (j + 1))
                    for a in range(4):
                        mm(ps[4 + 2 * g][0:P, a * 128:(a + 1) * 128], u_(xbuf[:, g, :])[:, a, :],
                           vbe[0:P, g, a * 128:(a + 1) * 128], start=True, stop=True)
                    for a in range(4):
                        last = mm(blk(5 + 2 * g)[:, a, :], kbe[0:P, g, a * 128:(a + 1) * 128], u_(xbuf[:, g, :])[:, a, :],
                                  start=True, stop=True)
                    last.then_inc(sem["u_ps"], 1)

            pe.wait_ge(sem["batch"], 6)
            pe.wait_ge(sem["s0"], 1)
            pe.wait_ge(sem["ld_state"], 16)
            for n in range(10):
                c, g = n // 2, n % 2
                j = c // 2
                t0, P = TILES[j]
                r0, R = (64 * (c % 2), 64) if c < 4 else (0, 32)
                st = sst[:, 0 if c < 4 else 1, :, :]
                wb, ob_, sbk = (0, 1, 2) if n % 2 == 0 else (3, 4, 5)
                if n >= 2:
                    pe.wait_ge(sem["o_sb"], n - 1)
                    pe.wait_ge(sem["s_new"], n - 1)
                for a in range(4):
                    hd = 4 * g + a
                    last = mm(ps[wb][0:P, a * 128:(a + 1) * 128], h[:, hd, t0:t0 + P], st[:, hd, :], start=True, stop=True)
                last.then_inc(sem["ws_ps"], 1)
                pe.wait_ge(sem["vn"], n + 1)
                ob = ps[ob_][:, 0:4 * R].rearrange("p (h i) -> p h i", h=4)
                for a in range(4):
                    hd = 4 * g + a
                    mm(ob[:, a, :], st[:, hd, :], qf[:, hd, t0 + r0:t0 + r0 + R], start=True, stop=False)
                    last = mm(ob[:, a, :], uu[r0:r0 + R, j, hd, :], att(j)[r0:r0 + R, hd, r0:r0 + R],
                              start=False, stop=True)
                last.then_inc(sem["o_ps"], 1)
                for a in range(4):
                    hd = 4 * g + a
                    last = mm(ps[sbk][:, a * 128:(a + 1) * 128], kdec[r0:r0 + R, j, hd, :], uu[r0:r0 + R, j, hd, :],
                              start=True, stop=True)
                last.then_inc(sem["su_ps"], 1)
            pe.wait_ge(sem["osq"], 1)
            for n in range(8):
                last = mm(ps[6][0:8, 0:T], C("pick")[:, 15 - n:23 - n], vf[:, n, :], start=(n == 0), stop=(n == 7))
            last.then_inc(sem["oss"], 1)
            for n in range(8):
                pe.wait_ge(sem["on"], max(n - 2, 1))
                mm(ps[n % 4][:, 0:T], ident[0:8, n:n + 1].broadcast_to([8, 128]), lbuf[0:8, 0, 0:T],
                   start=True, stop=True).then_inc(sem["oss"], 1)
            pe.wait_ge(sem["ozs"], 1)
            project(U_OUT1, 8, 8, ycat, "out_x")
            sum_squares(3)
            moe(1)
            sum_squares(4)

        @block.scalar
        def _(act):
            A = nc.scalar.activation
            L = Chain(act, "act")
            for dst, src in ((sml[:, :], t["small"]), (cst[:, :], t["const"]), (x[:, :, :], t["x"])):
                act.dma_start(dst, src).then_inc(sem["ld_small"], 16)
            act.dma_start(biasP0, t["biasP0"]).then_inc(sem["ld_att"], 16)
            act.dma_start(biasP1, t["biasP1"]).then_inc(sem["ld_att"], 16)
            act.dma_start(biasS[0:NS], t["biasS"]).then_inc(sem["ld_att"], 16)
            act.dma_start(ksT[:, :, 0:NP_], t["kcache"]).then_inc(sem["ld_att"], 16)
            act.dma_start(vcache, t["vcache"]).then_inc(sem["ld_att"], 16)
            act.wait_ge(sem["pad"], 1)
            for hf in range(2):
                for dst, src in ((bdr, t["wr"]), (bdi, t["wi"])):
                    act.dma_start(dst[64 * hf:64 * hf + 64, :, 64 * hf:64 * hf + 64],
                                  src[:, hf, :, :]).then_inc(sem["ld_att"], 16)
            act.wait_ge(sem["ld_small"], 48)
            L(A(condT[:, :, :], M("cond").rearrange("p (k g) -> p k g", g=2), ACT.Silu), "cond")
            act.wait_ge(sem["lamn"], 1)
            L(A(lamw[:, 1, :], lamw[:, 0, :], ACT.Exp), "lame")

            def norm_root(k):
                act.wait_ge(sem["ss"], k + 1)
                if k:
                    act.wait_ge(sem["h"], k)
                L(A(rms[:, :], ps[7][:, 0:T], ACT.Sqrt, scale=1.0 / D, bias=C("eps")[:, 0:1]), "rms")

            def mod_rows(l, b, bank):
                act.wait_ge(sem["w_used"], MOD_U * l + 2 * (b + 1))
                if b >= 2:
                    act.wait_ge(sem["mod_t"], MOD_B * l + b - 1)
                A(modrow[0:2, b % 2, :], ps[bank][0:2, :], ACT.Copy).then_inc(sem["mod_row"], 1)

            norm_root(0)
            for b in range(MOD_B):
                mod_rows(0, b, b % 2)
            for i in range(16):
                act.wait_ge(sem["proj_ps"], i + 1)
                src, c = ps[i % 4], i % 4
                if i < 4:
                    (A(xpad[:, c, 3:3 + NP_], src[:, 0:NP_], ACT.Copy))
                    A(xpad[:, c, SEG + 3:SEG + 3 + NS], src[:, NP_:T], ACT.Copy).then_inc(sem["proj_ev"], 1)
                elif i < 8:
                    A(gaT[:, c, :], src[:, 0:T], ACT.Copy).then_inc(sem["proj_ev"], 1)
                elif i < 12:
                    A(qT[:, c, :], src[:, 0:T], ACT.Copy).then_inc(sem["proj_ev"], 1)
                else:
                    (A(ksT[:, c, NP_:T], src[:, NP_:T], ACT.Copy))
                    A(kT[:, c, :], src[:, 0:T], ACT.Copy).then_inc(sem["proj_ev"], 1)
            act.wait_ge(sem["proj_ev"], 16)
            act.dma_start(t["k"], kT).then_inc(sem["st_mix"], 16)
            act.wait_ge(sem["v_ev"], 1)
            for j, (t0, P) in enumerate(TILES):
                act.dma_start(t["v"][t0:t0 + P, :], vtm[0:P, j, :]).then_inc(sem["st_mix"], 16)
            act.wait_ge(sem["gate_ps"], 1)
            for c in range(4):
                (A(rg[:, c, :], ps[c][:, 0:XW], ACT.Sigmoid, bias=M("abr")[:, c:c + 1]))
            act.wait_ge(sem["gate_ps"], 2)
            for c in range(3):
                (A(ig_[:, c, :], ps[4 + c][:, 0:XW], ACT.Sigmoid, bias=M("abi")[:, c:c + 1]))
            L(A(ig_[:, 3, :], ps[7][:, 0:XW], ACT.Sigmoid, bias=M("abi")[:, 3:4]), "gate_i")
            act.wait_ge(sem["lam"], 1)
            for c in range(4):
                (A(aa[:, c, :], rg[:, c, :], ACT.Exp, scale=lamw[:, 6, c:c + 1]))
            for c in range(4):
                ins = A(tt_[:, c, :], rg[:, c, :], ACT.Tanh, scale=lamw[:, 7, c:c + 1])
            L(ins, "lru_a")
            act.wait_ge(sem["lru_w"], 1)
            L(A(tt_[:, :, :], tt_[:, :, :], ACT.Sqrt), "lru_s")
            L(A(rg[:, :, 0:T], rg[:, :, 0:T], ACT.Tanh, scale=0.7978845608028654), "lru_g")
            for n in range(24):
                j, hd = n // 8, n % 8
                t0, P = TILES[j]
                nk = (128, 256, T)[j]
                act.wait_ge(sem["s_sm"], n + 1)
                L(A(s_sb[0:P, n % 2, 0:nk], s_sb[0:P, n % 2, 0:nk], ACT.Exp, bias=mx[0:P, n % 2, 1:2],
                    accum_out=rsum[0:P, n % 2, :]), "p_exp")
                act.wait_ge(sem["pt_ps"], n + 1)
                if n >= 2:
                    act.wait_ge(sem["pv_ps"], n - 1)
                kts = [(0, 128)] if j == 0 else [(0, 128), (1, 128)] if j == 1 else [(0, 128), (1, 128), (2, 32)]
                for kt, K in kts:
                    ins = A(pT[0:K, n % 2, kt, 0:P], ps[2 + n % 2][0:K, kt * 128:kt * 128 + P], ACT.Copy)
                    if kt == kts[-1][0]:
                        ins.then_inc(sem["pt_sb"], 1)
                if n % 2:
                    mod_rows(1, n // 2, 6)
                act.wait_ge(sem["pv_ps"], n + 1)
                b = DHB * (hd % 2)
                A(ycat[b:b + DHB, 4 + hd // 2, t0:t0 + P], ps[4 + n % 2][b:b + DHB, 0:P], ACT.Copy)\
                    .then_inc(sem["pv_sb"], 1)

            def moe(l):
                B = NE * l
                act.wait_ge(sem["lg_ps"], l + 1)
                act.wait_ge(sem["lgz"], l + 1)
                act.wait_ge(sem["st_mix"], 16 * 4)
                if l:
                    act.wait_ge(sem["st_small"], 16 * 5)
                for j, (t0, P) in enumerate(TILES):
                    ins = A(lg[0:P, j, :], ps[6][0:P, j * 64:(j + 1) * 64], ACT.Copy)
                    L(ins, "act")
                L(A(score, lg, ACT.Sigmoid), "score")
                for j, (t0, P) in enumerate(TILES):
                    act.wait_ge(sem["tm_ps"], 3 * l + j + 1)
                    for hf in range(2):
                        ins = A(gb[0:P, j, hf * 512:(hf + 1) * 512], ps[2 * j + hf][0:P, :], ACT.Copy)
                        L(ins, "tm_sb" if hf else None)
                        if hf:
                            act.dma_start(H2[t0:t0 + P, :], gb[0:P, j, :]).then_inc(sem["h2_st"], 16)
                act.wait_ge(sem["shu_ps"], 2 * l + 2)
                for j, (t0, P) in enumerate(TILES):
                    A(shs[0:P, j, :], ps[j][0:P, 0:DE], ACT.Silu)
                    L(A(shu_[0:P, j, :], ps[j][0:P, DE:2 * DE], ACT.Copy), "shu_sb")
                for j, (t0, P) in enumerate(TILES):
                    act.wait_ge(sem["sht_ps"], 3 * l + j + 1)
                    for a in range(2):
                        L(A(shT[:, j, a, 0:P], ps[3][:, a * 128:a * 128 + P], ACT.Copy),
                          "sht_sb" if a else None)
                for j, (t0, P) in enumerate(TILES):
                    act.wait_ge(sem["shd_ps"], 3 * l + j + 1)
                    for hf, bk in enumerate(((0, 1), (4, 5), (2, 3))[j]):
                        L(A(ysh[0:P, j, hf * 512:(hf + 1) * 512], ps[bk][0:P, :], ACT.Copy), "shd_sb" if hf else None)

                def take(e, p, i):
                    act.wait_ge(sem["trx"], e + (B + 1))
                    if p[0]:
                        act.wait_ge(sem["up"], e + (B - 1))
                    A(xgT[:, p[1], 0:4, :], ps[4][:, 0:4 * CAP].rearrange("p (k s) -> p k s", k=4), ACT.Copy)\
                        .then_inc(sem["xta"], 1)

                def rows(e, p, old):
                    act.wait_ge(sem["dn"], e + (B + 1))
                    if old:
                        act.wait_ge(sem[f"ysc{p}"], e * 8 + 8 * (B - p))
                    A(yb[0:CAP, p, 0:512], ps[0][0:CAP, :], ACT.Copy).then_inc(sem["ya_e"], 1)

                def step(e0, i=None):
                    e = e0 if i is None else i * 2 + e0
                    if e0 + 1 < NE:
                        take(e + 1, (e0 + 1 >= 2, (e0 + 1) % 2), i)
                    act.wait_ge(sem["up"], e + (B + 1))
                    if e0:
                        act.wait_ge(sem["hd"], e + B)
                    A(silu_b[0:CAP], ps[2][0:CAP, 0:DE], ACT.Silu).then_inc(sem["sg"], 1)
                    if e0:
                        rows(e - 1, (e0 - 1) % 2, e0 >= 3)

                take(0, (False, 0), None)
                for e in range(3):
                    step(e)
                with act.Fori(0, (NE - 6) // 2) as i:
                    step(3, i)
                    step(4, i)
                for e in range(NE - 3, NE):
                    step(e)
                rows(NE - 1, (NE - 1) % 2, True)

                act.wait_ge(sem["flag"], l + 1)
                more = act.value_load(flagi[0:1, 0:1], min_val=0, max_val=1)
                with act.If(more > 0):
                    s = lambda n: sem[f"{n}{l}"]
                    with act.Fori(0, 2) as bb:
                        with act.Fori(0, NE) as e:
                            J = bb * NE + e
                            act.wait_ge(s("ovp"), J * 4 + 1)
                            for hf in range(2):
                                ins = A(xgT[:, 0, 4 * hf:4 * hf + 4, :],
                                        ps[4 + hf][:, 0:4 * CAP].rearrange("p (k s) -> p k s", k=4), ACT.Copy)
                            ins.then_inc(s("ova"), 1)
                            act.wait_ge(s("ovp"), J * 4 + 2)
                            A(silu_b[0:CAP], ps[2][0:CAP, 0:DE], ACT.Silu).then_inc(s("ova"), 1)
                            act.wait_ge(s("ovp"), J * 4 + 3)
                            A(hidT, ps[3][:, 0:2 * CAP].rearrange("p (a s) -> p a s", a=2), ACT.Copy).then_inc(s("ova"), 1)
                            act.wait_ge(s("ovp"), J * 4 + 4)
                            for hf in range(2):
                                ins = A(yb[0:CAP, 0, hf * 512:(hf + 1) * 512], ps[hf][0:CAP, :], ACT.Copy)
                            ins.then_inc(s("ova"), 1)

            norm_root(1)
            moe(0)
            norm_root(2)
            act.wait_ge(sem["padc"], 1)
            act.wait_ge(sem["acc_x"], 1)
            act.dma_start(sst[:, 1, :, :], t["S0"]).then_inc(sem["ld_state"], 16)
            def conv_silu(n):
                act.wait_ge(sem["cacc"], 4 * (n + 1))
                dst = (qf, kf, vf)[n // 2][:, 4 * (n % 2):4 * (n % 2) + 4, :]
                A(dst[:, :, 0:NP_], cacc[:, n % 2, :, 0:NP_], ACT.Silu)
                A(dst[:, :, NP_:T], cacc[:, n % 2, :, SEG:SEG + NS], ACT.Silu).then_inc(sem["csilu"], 1)

            for i in range(32):
                n, c = i // 4, i % 4
                act.wait_ge(sem["proj_ps"], 16 + i + 1)
                src = ps[i % 4]
                if i < 24:
                    if n >= 2:
                        act.wait_ge(sem["cacc"], 4 * (n - 2) + c + 1)
                    A(raw[:, n % 2, c, 3:3 + NP_], src[:, 0:NP_], ACT.Copy)
                    A(raw[:, n % 2, c, SEG + 3:SEG + 3 + NS], src[:, NP_:T], ACT.Copy).then_inc(sem["proj_ev"], 1)
                else:
                    A(zf[:, i - 24, :], src[:, 0:T], ACT.Silu).then_inc(sem["proj_ev"], 1)
                if c == 3 and 1 <= n <= 6:
                    conv_silu(n - 1)
            act.wait_ge(sem["ab_e"], 1)
            L(A(spw[:, 1, :], spw[:, 0, :], ACT.Exp), "ab_act")
            for j, (t0, P) in enumerate(TILES):
                (A(btm[0:P, j, :], ps[6][0:P, j * 16 + 8:j * 16 + 16], ACT.Sigmoid))
            L(A(spw[:, 5, 0:8], M("alog"), ACT.Exp), "ab_act")
            act.wait_ge(sem["gcum_e"], 1)
            A(begc, gcol, ACT.Exp)
            L(A(kdcol, glast, ACT.Exp), "ab_act")
            act.wait_ge(sem["lss"], 1)
            L(A(lbuf[0:16, 0, 0:T], ps[0][0:16, 0:T], ACT.Sqrt, scale=C("l2", 16)[:, 0:1], bias=C("l2", 16)[:, 1:2]), "lrms")
            for j, (t0, P) in enumerate(TILES):
                blk = lambda b: ps[b][:, 0:4 * P].rearrange("p (h i) -> p h i", h=4)
                for g in range(2):
                    n = 2 * j + g
                    act.wait_ge(sem["gb_ps"], n + 1)
                    if n >= 2:
                        act.wait_ge(sem["tk_sb"], n - 1)
                    L(A(four(egb[:, g, :], P), blk(0), ACT.Exp), "gb_e")
                    act.wait_ge(sem["ldif"], n + 1)
                    L(A(four(lbuf[:, g, :], P)[0:P], four(lbuf[:, g, :], P)[0:P], ACT.Exp), "lexp")
                for m in range(STEP0[j], STEP0[j] + 2 * LEV_N[j]):
                    act.wait_ge(sem["y_ps"], m + 1)
                    L.go(A(four(ybuf[:, m % 2, :], P)[0:P], blk(6 + m % 2)[0:P], ACT.Copy), "y_sb")
                for g in range(2):
                    act.wait_ge(sem["u_ps"], 2 * j + g + 1)
                    L(A(uu[0:P, j, 4 * g:4 * g + 4, :], ps[4 + 2 * g][0:P, :].rearrange("p (h v) -> p h v", h=4), ACT.Copy),
                      "act")
                    L(A(h[:, 4 * g:4 * g + 4, t0:t0 + P], blk(5 + 2 * g), ACT.Copy), "batch")
            for n in range(10):
                c, g = n // 2, n % 2
                t0 = TILES[c // 2][0]
                r0, R = (64 * (c % 2), 64) if c < 4 else (0, 32)
                act.wait_ge(sem["o_ps"], n + 1)
                L(A(ycat[:, 4 * g:4 * g + 4, t0 + r0:t0 + r0 + R],
                    ps[1 + 3 * (n % 2)][:, 0:4 * R].rearrange("p (h i) -> p h i", h=4), ACT.Copy), "o_sb")
            act.wait_ge(sem["oss"], 1)
            L(A(lbuf[0:8, 0, 0:T], ps[6][0:8, 0:T], ACT.Sqrt, scale=1.0 / 128, bias=C("eps", 8)[:, 0:1]), "orms")
            norm_root(3)
            moe(1)
            norm_root(4)

        @block.vector
        def _(dve):
            V = nc.vector
            L = Chain(dve, "dve")

            def tt(o, a, b, op):
                return V.tensor_tensor(o, a, b, op)

            def ts(o, a, s1, s2, op0, op1=None):
                return V.tensor_scalar(o, a, s1, s2, op0, op1) if op1 is not None else V.tensor_scalar(o, a, s1, None, op0)

            def stt(o, a, s, b, op0, op1):
                return V.scalar_tensor_tensor(out=o, in0=a, scalar=s, in1=b, op0=op0, op1=op1)

            def log1p(out, e, w1, w2):
                L(ts(w1, e, 2.0, None, ALU.add))
                L(V.reciprocal(w1, w1))
                L(tt(w1, w1, e, ALU.mult))
                L(tt(w2, w1, w1, ALU.mult))
                L(ts(out, w2, 1.0 / 17, None, ALU.mult))
                for k in (15, 13, 11, 9, 7, 5, 3):
                    L(stt(out, out, 1.0 / k, w2, ALU.add, ALU.mult))
                L(stt(out, out, 1.0, w1, ALU.add, ALU.mult))
                L(ts(out, out, 2.0, None, ALU.mult))

            L(V.memset(bdr, 0.0))
            L(V.memset(bdi, 0.0), "pad")
            dve.wait_ge(sem["ld_small"], 48)
            L(V.memset(xpad[:, :, 0:3], 0.0))
            L(V.tensor_copy(xpad[:, :, SEG:SEG + 3], M("astate").rearrange("p (c j) -> p c j", c=4)))
            lam = M("alam")
            L(ts(lamw[:, 2, :], lam, -1.0, None, ALU.mult))
            L(tt(lamw[:, 0, :], lam, lamw[:, 2, :], ALU.min), "lamn")
            L(ts(lamw[:, 2, :], lamw[:, 2, :], 0.0, None, ALU.max))
            dve.wait_ge(sem["lame"], 1)
            log1p(lamw[:, 3, :], lamw[:, 1, :], lamw[:, 4, :], lamw[:, 5, :])
            L(tt(lamw[:, 3, :], lamw[:, 3, :], lamw[:, 2, :], ALU.add))
            L(ts(lamw[:, 7, :], lamw[:, 3, :], 8.0, None, ALU.mult))
            L(ts(lamw[:, 6, :], lamw[:, 3, :], -8.0, None, ALU.mult), "lam")

            def squares(k):
                L(tt(h[:, :, :], x[:, :, :], x[:, :, :], ALU.mult), "sq")

            def vectors(l, bank):
                dve.wait_ge(sem["mod_t"], MOD_B * (l + 1))
                L(tt(mod[:, l, :, :], ps[bank][:, 0:96].rearrange("p (m g) -> p m g", g=2),
                     M("bmod")[:, l * 48:(l + 1) * 48].unsqueeze(2).broadcast_to([128, 48, 2]), ALU.add))
                for w in range(2):
                    g_ = M("norms")[:, (2 * l + w) * 8:(2 * l + w + 1) * 8].unsqueeze(2).broadcast_to([128, KC, 2])
                    L(stt(scale1[:, l, w, :, :], mod[:, l, 24 * w + 8:24 * w + 16, :], 1.0, g_, ALU.add, ALU.mult))

            def apply_norm(k, l, which):
                dve.wait_ge(sem["rms"], k + 1)
                L(V.reciprocal(rms[:, :], rms[:, :]))
                L(tt(h[:, :, :], x[:, :, :], rms[:, :].unsqueeze(1).broadcast_to([128, KC, T]), ALU.mult))
                if k == 0:
                    vectors(0, 2)
                for c in range(KC):
                    for g, (a, b) in enumerate(GROUPS):
                        lastop = c == KC - 1 and g == 1
                        if l is None:
                            ins = ts(h[:, c, a:b], h[:, c, a:b], M("norms")[:, 32 + c:33 + c], None, ALU.mult)
                        else:
                            ins = ts(h[:, c, a:b], h[:, c, a:b], scale1[:, l, which, c, g:g + 1],
                                     mod[:, l, 24 * which + c, g:g + 1], ALU.mult, ALU.add)
                        (L if lastop else L.go)(ins, "h" if lastop else None)

            squares(0)
            apply_norm(0, 0, 0)
            cw = M("aconv").rearrange("p (c j) -> p c j", c=4)
            for c in range(4):
                dve.wait_ge(sem["proj_ev"], c + 1)
                L(ts(xc[:, c, :], xpad[:, c, 0:XW], cw[:, c, 0:1], M("aconvb")[:, c:c + 1], ALU.mult, ALU.add))
                for j in range(1, 4):
                    last = c == 3 and j == 3
                    L(stt(xc[:, c, :], xpad[:, c, j:j + XW], cw[:, c, j:j + 1], xc[:, c, :], ALU.mult, ALU.add),
                      "conv" if last else None)
            L(V.tensor_copy(cst3[:, :, 0, :], xpad[:, :, NP_:NP_ + 3]))
            L(V.tensor_copy(cst3[:, :, 1, :], xpad[:, :, SEG + NS:SEG + NS + 3]))
            dve.wait_ge(sem["proj_ev"], 8)
            L(tt(hh[:, :, 0:T], gaT, gaT, ALU.mult))
            L(ts(hh[:, :, 0:T], hh[:, :, 0:T], 0.044715, 1.0, ALU.mult, ALU.add))
            dve.wait_ge(sem["v_ps"], 2)
            for j, (t0, P) in enumerate(TILES):
                L(V.tensor_copy(vtm[0:P, j, :], ps[4 + j][0:P, :]), "v_ev" if j == 2 else None)
            dve.wait_ge(sem["lru_a"], 1)
            L(tt(rg[:, :, 0:T], hh[:, :, 0:T], gaT, ALU.mult))
            L(tt(ig_, ig_, xc, ALU.mult))
            L(tt(xc, aa, aa, ALU.mult))
            L(stt(tt_, xc, 1.0, tt_, ALU.add, ALU.mult), "lru_w")
            dve.wait_ge(sem["lru_s"], 1)
            L(tt(tt_, tt_, ig_, ALU.mult))
            for c in range(4):
                L.go(V.tensor_tensor_scan(hh[:, c, 0:NP_], aa[:, c, 0:NP_], tt_[:, c, 0:NP_], 0.0, ALU.mult, ALU.add))
                L(V.tensor_tensor_scan(hh[:, c, SEG:SEG + NS], aa[:, c, SEG:SEG + NS], tt_[:, c, SEG:SEG + NS],
                                       M("ah0")[:, c:c + 1], ALU.mult, ALU.add))
            L(V.tensor_copy(hst[:, :, 0:1], hh[:, :, NP_ - 1:NP_]))
            L(V.tensor_copy(hst[:, :, 1:2], hh[:, :, SEG + NS - 1:SEG + NS]), "hst")
            dve.wait_ge(sem["lru_g"], 1)
            L(stt(gaT, rg[:, :, 0:T], 1.0, gaT, ALU.add, ALU.mult))
            L(stt(ycat[:, 0:4, 0:NP_], hh[:, :, 0:NP_], 0.5, gaT[:, :, 0:NP_], ALU.mult, ALU.mult))
            L(stt(ycat[:, 0:4, NP_:T], hh[:, :, SEG:SEG + NS], 0.5, gaT[:, :, NP_:T], ALU.mult, ALU.mult), "ya")
            dve.wait_ge(sem["ld_att"], 16 * 9)
            L(V.memset(biasP0[0:64, :, 64:128], -1e30))
            L(V.memset(biasP1[0:64, :, 192:256], -1e30))
            for n in range(24):
                j, hd = n // 8, n % 8
                t0, P = TILES[j]
                nk = (128, 256, T)[j]
                bias = (biasP0, biasP1, biasS)[j]
                dve.wait_ge(sem["s_ps"], n + 1)
                if n >= 2:
                    dve.wait_ge(sem["pt_ps"], n - 1)
                L(stt(s_sb[0:P, n % 2, 0:nk], ps[n % 2][0:P, 0:nk], DHB ** -0.5, bias[0:P, hd, :], ALU.mult, ALU.add))
                L(V.reduce_max(mx[0:P, n % 2, 0:1], s_sb[0:P, n % 2, 0:nk], AX.X))
                L(ts(mx[0:P, n % 2, 1:2], mx[0:P, n % 2, 0:1], -1.0, None, ALU.mult), "s_sm")
                dve.wait_ge(sem["p_exp"], n + 1)
                L(V.reciprocal(rsum[0:P, n % 2, :], rsum[0:P, n % 2, :]))
                L(ts(s_sb[0:P, n % 2, 0:nk], s_sb[0:P, n % 2, 0:nk], rsum[0:P, n % 2, :], None, ALU.mult), "p_nrm")

            def residual(base, l):
                for i in range(8):
                    dve.wait_ge(sem["out_ps"], base + i + 1)
                    for g, (a, b) in enumerate(GROUPS):
                        L(stt(x[:, i, a:b], ps[i % 4][:, a:b], mod[:, l, 16 + i, g:g + 1], x[:, i, a:b],
                              ALU.mult, ALU.add), "out_x" if g else None)

            vectors(1, 7)
            residual(0, 0)

            def moe(l):
                B = NE * l
                dve.wait_ge(sem["st_mix"], 16 * 4)
                if l:
                    dve.wait_ge(sem["st_small"], 16 * 5)
                L(V.memset(lg, 0.0), "lgz")
                L(V.memset(xgb, 0.0), "xgz")
                dve.wait_ge(sem["score"], l + 1)
                rb = M("rb")[:, l * 64:(l + 1) * 64].unsqueeze(1).broadcast_to([128, 3, NE])
                L(tt(selv, score, rb, ALU.add))
                for j in range(3):
                    for g in range(8):
                        ins = V.max(top2[:, j, g, :], selv[:, j, g * 8:(g + 1) * 8])
                        (L if (j, g) == (2, 7) else L.go)(ins)
                L(tt(gsc.unsqueeze(3), top2[:, :, :, 0:1], top2[:, :, :, 1:2], ALU.add))
                for j in range(3):
                    other = gsc[:, j, :].unsqueeze(1).broadcast_to([128, 8, 8])
                    own = gsc[:, j, :].unsqueeze(2).broadcast_to([128, 8, 8])
                    L(tt(gcmp[:, j], other, own, ALU.is_gt))
                    L(tt(geq[:, j], other, own, ALU.is_equal))
                    L(tt(geq[:, j], geq[:, j], C("lower").rearrange("p (a b) -> p a b", a=8), ALU.mult))
                    L(tt(gcmp[:, j], gcmp[:, j], geq[:, j], ALU.add))
                    L(V.reduce_sum(grk[:, j, :], gcmp[:, j], AX.X))
                L(ts(grk, grk, 4.0, None, ALU.is_lt))
                L(ts(gsc, grk, 1.0, 1e30, ALU.subtract, ALU.mult))
                for j in range(3):
                    e8 = lambda v: v[:, j, :].rearrange("p (g e) -> p g e", g=8)
                    L(tt(e8(tmp1), e8(selv), grk[:, j, :].unsqueeze(2).broadcast_to([128, 8, 8]), ALU.mult))
                    L(tt(e8(tmp1), e8(tmp1), gsc[:, j, :].unsqueeze(2).broadcast_to([128, 8, 8]), ALU.add))
                for j in range(3):
                    L(V.max(top8[:, j, :], tmp1[:, j, :]))
                    L(V.match_replace(out=tmp2[:, j, :], in_to_replace=top8[:, j, :], in_values=tmp1[:, j, :],
                                      imm_value=-3e30))
                L(tt(msk, tmp2, tmp1, ALU.is_lt), "mask")
                L(tt(gates, score, msk, ALU.mult))
                L(V.reduce_sum(gsum[:, :, :], gates, AX.X))
                L(V.reciprocal(gsum[:, :, :], gsum[:, :, :]))
                L(tt(gates, gates, gsum.broadcast_to([128, 3, NE]), ALU.mult))
                L(ts(gates, gates, 2.5, None, ALU.mult))
                L(V.tensor_copy(tg[:, :, :, 2:3], gates.unsqueeze(3)))
                for c in (3, 4):
                    L(tt(gates.unsqueeze(3), gates.unsqueeze(3), tg[:, :, :, c - 1:c], ALU.subtract))
                    L(V.tensor_copy(tg[:, :, :, c:c + 1], gates.unsqueeze(3)))
                for j in range(3):
                    L(V.tensor_copy(tg[:, j, :, 0:1], C("slot").unsqueeze(2).broadcast_to([128, NE, 1])))
                    L(V.memset(tg[:, j, :, 1:2], float(128 * j - LIM)))
                L(V.tensor_copy(slots, C("iota")[:, 0:CAP]))
                dve.wait_ge(sem["rank_ps"], l + 1)
                L(V.tensor_copy(cntf[:, 0:NE], ps[7][:, 192:256]))
                L(V.reduce_max(cntf[0:1, 64:65], cntf[0:1, 0:NE], AX.X))
                L(ts(flagi[0:1, 0:1], cntf[0:1, 64:65], float(CAP), None, ALU.is_gt), "flag")
                L(V.memset(rk, 0.0))
                for j, (t0, P) in enumerate(TILES):
                    L(V.tensor_copy(rk[0:P, j, :], ps[7][0:P, j * 64:(j + 1) * 64]))
                L(V.tensor_tensor_scan(start, ones[:, 0:NE], cntf[:, 0:NE], 0.0, ALU.mult, ALU.add))
                L(tt(start, start, cntf[:, 0:NE], ALU.subtract))
                L(ts(srow, start, C("slot"), None, ALU.add))
                L(ts(start, start, 1.0, None, ALU.add))
                base_ = start.unsqueeze(1).broadcast_to([128, 3, NE])
                L(tt(tmp1, rk, base_, ALU.add))
                L(tt(tmp1, tmp1, msk, ALU.mult))
                for j in range(3):
                    L(V.max(rowif[:, j, :], tmp1[:, j, :]))
                L(ts(rowi[:, :, :], rowif, -1.0, None, ALU.add), "rowi")
                L(stt(rk, rk, 1.0, msk, ALU.add, ALU.mult))
                L(ts(rk, rk, -1.0, None, ALU.add))
                L(V.tensor_copy(rkb_flat, rk_flat))

                def one_hots(g, sem_, wait):
                    if wait is not None:
                        dve.wait_ge(*wait)
                    for j, (t0, P) in enumerate(TILES):
                        o = selb[0:P, g % 2, j, :].rearrange("p (e s) -> p e s", e=8)
                        ins = tt(o, slots[0:P].unsqueeze(1).broadcast_to([P, 8, CAP]),
                                 rkb[0:P, j, 8 * g:8 * g + 8].unsqueeze(2).broadcast_to([P, 8, CAP]), ALU.is_equal)
                    ins.then_inc(sem_, 1)

                for g in range(8):
                    one_hots(g, sem["sel"], (sem["sel_ps"], 8 * l + g - 1) if 8 * l + g >= 2 else None)

                def tables(chain, shift):
                    tabs = ps[6][0:CAP, 0:5 * NE].rearrange("p (e c) -> p e c", c=5)
                    f, ix = idxf[0:CAP, 0, :], idx[0:CAP]
                    chain(ts(f.unsqueeze(2), tabs[:, :, 0:1], float(LIM), None, ALU.add))
                    chain(tt(f.unsqueeze(2), f.unsqueeze(2), tabs[:, :, 1:2], ALU.add))
                    chain(V.tensor_copy(ix[:, :, 0:1], f.unsqueeze(2)))
                    gate = ix[:, :, 1:2].bitcast(F32)
                    chain(V.tensor_copy(gate, tabs[:, :, 2:3]))
                    chain(tt(gate, gate, tabs[:, :, 3:4], ALU.add))
                    chain(tt(gate, gate, tabs[:, :, 4:5], ALU.add))
                    chain(ts(f, f, float(LIM), 65536.0, ALU.is_ge, ALU.mult))
                    chain(tt(f, f, srow[0:CAP], ALU.add))
                    if shift is not None:
                        chain(tt(f, f, shift, ALU.add))
                    return V.tensor_copy(ix[:, :, 2:3], f.unsqueeze(2))

                dve.wait_ge(sem["sel_ps"], 8 * l + 8)
                L(tables(L, None))

                def copy_gather(e, p, wait):
                    if wait:
                        dve.wait_ge(sem[f"xg{p}"], e * 8 + 8 * (B - p))
                    src = idx[0:CAP, e:e + 1, 0:1] if isinstance(e, int) else idx[0:CAP, bass.ds(e, 1), 0:1]
                    V.tensor_copy(icg[0:CAP, p:p + 1, :], src).then_inc(sem["ig"], 1)

                def copy_scatter(e, p, wait):
                    if wait:
                        dve.wait_ge(sem[f"ysc{p}"], e * 8 + 8 * (B - p))
                    src = idx[0:CAP, e:e + 1, 2:3] if isinstance(e, int) else idx[0:CAP, bass.ds(e, 1), 2:3]
                    V.tensor_copy(ics[0:CAP, p:p + 1, :], src).then_inc(sem["isx"], 1)

                def take(e, p, wait):
                    dve.wait_ge(sem["trx"], e + (B + 1))
                    if wait:
                        dve.wait_ge(sem["up"], e + (B - 1))
                    V.tensor_copy(xgT[:, p, 4:8, :], ps[5][:, 0:4 * CAP].rearrange("p (k s) -> p k s", k=4))\
                        .then_inc(sem["xtb"], 1)

                def hidden_T(e, wait):
                    dve.wait_ge(sem["trh"], e + (B + 1))
                    if wait:
                        dve.wait_ge(sem["dn"], e + B)
                    V.tensor_copy(hidT, ps[3][:, 0:2 * CAP].rearrange("p (a s) -> p a s", a=2)).then_inc(sem["ht"], 1)

                def rows(e, p, wait):
                    copy_scatter(e, p, wait)
                    dve.wait_ge(sem["dn"], e + (B + 1))
                    V.tensor_copy(yb[0:CAP, p, 512:1024], ps[1][0:CAP, :]).then_inc(sem["yb_e"], 1)

                def step(e0, i=None):
                    e = e0 if i is None else i * 2 + e0
                    if e0:
                        hidden_T(e - 1, e0 >= 2)
                    if e0 + 1 < NE:
                        take(e + 1, (e0 + 1) % 2, e0 + 1 >= 2)
                    if e0 + 3 < NE:
                        copy_gather(e + 3, (e0 + 1) % 2, True)
                    dve.wait_ge(sem["sg"], e + (B + 1))
                    if e0:
                        dve.wait_ge(sem["trh"], e + B)
                    gate = idx[0:CAP, e, 1:2] if i is None else idx[0:CAP, bass.ds(e, 1), 1:2].rearrange("p a b -> p (a b)")
                    stt(hid[0:CAP], ps[2][0:CAP, DE:2 * DE], gate.bitcast(F32), silu_b[0:CAP], ALU.mult, ALU.mult)\
                        .then_inc(sem["hd"], 1)
                    if e0:
                        rows(e - 1, (e0 - 1) % 2, e0 >= 3)

                copy_gather(0, 0, False)
                copy_gather(1, 1, False)
                take(0, 0, False)
                copy_gather(2, 0, True)
                for e in range(3):
                    step(e)
                with dve.Fori(0, (NE - 6) // 2) as i:
                    step(3, i)
                    step(4, i)
                for e in range(NE - 3, NE):
                    step(e)
                hidden_T(NE - 1, True)
                rows(NE - 1, (NE - 1) % 2, True)

                dve.wait_ge(sem["flag"], l + 1)
                more = dve.value_load(flagi[0:1, 0:1], min_val=0, max_val=1)
                with dve.If(more > 0):
                    s = lambda n: sem[f"{n}{l}"]
                    for p in range(2):
                        dve.wait_ge(sem[f"ysc{p}"], 8 * (B + NE))
                    with dve.Fori(0, 2) as bb:
                        cnt = [0]

                        def chain(ins):
                            cnt[0] += 1
                            ins.then_inc(s("ovi"), 1)
                            dve.wait_ge(s("ovi"), bb * 11 + cnt[0])

                        dve.wait_ge(s("od"), bb * NE + 1)
                        dve.sem_inc(sem["passed"], 1)
                        chain(tt(rkb_flat, rk_flat, cst[:, bass.ds(bb * CAP + (CST["iota"][0] + CAP), 1)]
                                 .broadcast_to([128, 3 * NE]), ALU.subtract))
                        for g in range(8):
                            if g >= 2:
                                dve.wait_ge(s("osel_ps"), bb * 8 + (g - 1))
                            one_hots(g, s("osel"), None)
                        dve.wait_ge(s("osel_ps"), bb * 8 + 8)
                        chain(tables(chain, cst[0:CAP, bass.ds(bb * CAP + (CST["iota"][0] + CAP), 1)]
                                     .broadcast_to([CAP, NE])))
                        assert cnt[0] == 11, cnt
                        dve.sem_inc(sem["passed"], 1)
                        with dve.Fori(0, NE) as e:
                            J = bb * NE + e
                            dve.wait_ge(s("od"), J + 1)
                            V.tensor_copy(ico[0:CAP, :].unsqueeze(1), idx[0:CAP, bass.ds(e, 1), :]).then_inc(s("ovd"), 1)
                            dve.wait_ge(s("ova"), J * 4 + 2)
                            dve.wait_ge(s("ovd"), J * 2 + 1)
                            stt(hid[0:CAP], ps[2][0:CAP, DE:2 * DE], ico[0:CAP, 1:2].bitcast(F32), silu_b[0:CAP],
                                ALU.mult, ALU.mult)\
                                .then_inc(s("ovd"), 1)

                dve.wait_ge(sem["shd_sb"], 3 * (l + 1))
                for n in range(24):
                    j, k = n // 8, n % 8
                    P = TILES[j][1]
                    dve.wait_ge(sem[f"got{n % 4}"], 16 * ((24 * l + n) // 4 + 1))
                    L(tt(ysh[0:P, j, :], ysh[0:P, j, :], gb[0:P, n % 4, :], ALU.add), "cb")
                for j, (t0, P) in enumerate(TILES):
                    dve.wait_ge(sem["acc_ps"], 3 * l + j + 1)
                    for k in range(KC):
                        ins = stt(x[:, k, t0:t0 + P], ps[2 * j + k // 4][:, (k % 4) * 128:(k % 4) * 128 + P],
                                  mod[:, l, 40 + k, (1 if j == 2 else 0):(2 if j == 2 else 1)], x[:, k, t0:t0 + P],
                                  ALU.mult, ALU.add)
                        L(ins, "acc_x" if (j, k) == (2, KC - 1) else None)

            squares(1)
            apply_norm(1, 0, 1)
            moe(0)
            squares(2)
            apply_norm(2, 1, 0)
            L(V.memset(raw[:, :, :, 0:3], 0.0), "padc")
            L(V.memset(sst[:, 0, :, :], 0.0), "s0")
            cw1 = M("cconv").rearrange("p (c j) -> p c j", c=24)
            cs1 = M("cstate").rearrange("p (c j) -> p c j", c=24)
            for n in range(6):
                for c in range(4):
                    i = 4 * n + c
                    r = raw[:, n % 2, c, :]
                    dve.wait_ge(sem["proj_ev"], 16 + i + 1)
                    L(V.tensor_copy(r[:, SEG:SEG + 3], cs1[:, i, :]))
                    L(V.tensor_copy(cc3[:, i, 0, :], r[:, NP_:NP_ + 3]))
                    L(V.tensor_copy(cc3[:, i, 1, :], r[:, SEG + NS:SEG + NS + 3]), "cc" if i == 23 else None)
                    if n >= 2 and c == 0:
                        dve.wait_ge(sem["csilu"], n - 1)
                    o = cacc[:, n % 2, c, :]
                    L(ts(o, r[:, 0:XW], cw1[:, i, 0:1], None, ALU.mult))
                    for j in range(1, 4):
                        L(stt(o, r[:, j:j + XW], cw1[:, i, j:j + 1], o, ALU.mult, ALU.add), "cacc" if j == 3 else None)
            dve.wait_ge(sem["ab_ps"], 1)
            L(V.memset(spt, 0.0))
            L(V.memset(btm, 0.0))
            for j, (t0, P) in enumerate(TILES):
                L(tt(spt[0:P, j, :], ps[6][0:P, j * 16:j * 16 + 8], M("dtb", P), ALU.add))
            s3 = lambda v: v.rearrange("p (t h) -> p t h", t=3)
            L(ts(s3(spw[:, 2, :]), spt, -1.0, None, ALU.mult))
            L(tt(s3(spw[:, 0, :]), spt, s3(spw[:, 2, :]), ALU.min), "ab_e")
            L(ts(spt, spt, 0.0, None, ALU.max))
            dve.wait_ge(sem["ab_act"], 2)
            log1p(spw[:, 2, :], spw[:, 1, :], spw[:, 3, :], spw[:, 4, :])
            L(tt(spt, spt, s3(spw[:, 2, :]), ALU.add))
            L(stt(gtm, spt, -1.0, spw[:, 5, 0:8].unsqueeze(1).broadcast_to([128, 3, 8]), ALU.mult, ALU.mult), "ab_sb")
            dve.wait_ge(sem["gcum_ps"], 1)
            L(V.memset(gcol, 0.0))
            L(V.memset(glast, 0.0))
            for j, (t0, P) in enumerate(TILES):
                L(V.tensor_copy(gcol[0:P, j, :], ps[6][0:P, 64 + j * 8:72 + j * 8]))
                L(tt(glast[0:P, j, :], ps[6][0:P, 96 + j * 8:104 + j * 8], gcol[0:P, j, :], ALU.subtract),
                  "gcum_e" if j == 2 else None)
            dve.wait_ge(sem["ab_act"], 3)
            L(tt(begc, begc, btm, ALU.mult), "gdec")
            dve.wait_ge(sem["csilu"], 6)
            for n in range(4):
                src = (qf, kf)[n // 2][:, 4 * (n % 2):4 * (n % 2) + 4, :]
                L(tt(sqb[:, 4 * n:4 * n + 4, :], src, src, ALU.mult), "lsq")
            dve.wait_ge(sem["lrms"], 1)
            L(V.reciprocal(lbuf[0:16, 0, 0:T], lbuf[0:16, 0, 0:T]), "qk_n")
            for n in range(16):
                v = (qf, kf)[n // 8][:, n % 8, :]
                dve.wait_ge(sem["lss"], n + 2)
                L.go(tt(v, v, ps[1 + n % 4][:, 0:T], ALU.mult), "qk_n")
            dve.wait_ge(sem["qk_n"], 17)
            for j, (t0, P) in enumerate(TILES):
                f = lambda b: four(b, P)[0:P]
                pb = lambda b: ps[b][0:P, 0:4 * P].rearrange("p (h i) -> p h i", h=4)
                for g in range(2):
                    n = 2 * j + g
                    hsl = slice(4 * g, 4 * g + 4)
                    dve.wait_ge(sem["gb_e"], n + 1)
                    if j:
                        dve.wait_ge(sem["u_ps"], n - 1)
                    L(tt(f(lbuf[:, g, :]), pb(0), gcol[0:P, j, hsl].unsqueeze(2).broadcast_to([P, 4, P]), ALU.subtract))
                    L(ts(f(lbuf[:, g, :]), f(lbuf[:, g, :]), 0.0, None, ALU.min), "ldif")
                    L.go(V.tensor_copy(f(xbuf[:, g, :]), ident[0:P, 0:P].unsqueeze(1).broadcast_to([P, 4, P])))
                    L(V.tensor_copy(f(dbuf[:, g, :]), ident[0:P, 0:P].unsqueeze(1).broadcast_to([P, 4, P])), "xd")
                    dve.wait_ge(sem["lexp"], n + 1)
                    L(tt(f(lbuf[:, g, :]), f(lbuf[:, g, :]), C("tri")[0:P, 0:P].unsqueeze(1).broadcast_to([P, 4, P]),
                         ALU.mult))
                    dve.wait_ge(sem["kk_ps"], n + 1)
                    L(tt(f(nbuf[:, g, :]), pb(2), f(lbuf[:, g, :]), ALU.mult))
                    L(tt(f(nbuf[:, g, :]), f(nbuf[:, g, :]), pb(1), ALU.mult), "nmat")
                    L.go(tt(att(j)[0:P, hsl, :], pb(3), f(lbuf[:, g, :]), ALU.mult))
                    eg = four(egb[:, g, :], P)
                    L.go(tt(qf[:, hsl, t0:t0 + P], qf[:, hsl, t0:t0 + P], eg, ALU.mult))
                    for cc, col in ((2 * j, 63), (2 * j + 1, 127)) if j < 2 else ((4, 31),):
                        L.go(V.tensor_copy(sdec[:, cc, hsl].unsqueeze(2), eg[:, :, col:col + 1]))
                    dve.wait_ge(sem["tk_ps"], n + 1)
                    tk = lambda b: ps[b][0:P, :].rearrange("p (h d) -> p h d", h=4)
                    bc = lambda v: v[0:P, j, hsl].unsqueeze(2).broadcast_to([P, 4, 128])
                    L.go(tt(kbe[0:P, g, :].rearrange("p (h d) -> p h d", h=4), tk(4), bc(begc), ALU.mult))
                    L.go(tt(kdec[0:P, j, hsl, :], tk(4), bc(kdcol), ALU.mult))
                    L(tt(vbe[0:P, g, :].rearrange("p (h d) -> p h d", h=4), tk(5), bc(btm), ALU.mult), "tk_sb")
                for m in range(STEP0[j], STEP0[j] + 2 * LEV_N[j]):
                    g = m % 2
                    dve.wait_ge(sem["z_ps"], m + 1)
                    if m >= STEP0[j] + 2:
                        dve.wait_ge(sem["xd"], 2 * (j + 1) + m - 1)
                    L.go(tt(f(dbuf[:, g, :]), f(dbuf[:, g, :]), pb(2 * g), ALU.subtract))
                    L.go(tt(f(xbuf[:, g, :]), f(xbuf[:, g, :]), pb(2 * g + 1), ALU.subtract), "xd")
            dve.wait_ge(sem["batch"], 6)
            for n in range(10):
                c, g = n // 2, n % 2
                j = c // 2
                r0, R = (64 * (c % 2), 64) if c < 4 else (0, 32)
                hsl = slice(4 * g, 4 * g + 4)
                st = sst[:, 0 if c < 4 else 1, :, :]
                dve.wait_ge(sem["ws_ps"], n + 1)
                L(tt(uu[r0:r0 + R, j, hsl, :], uu[r0:r0 + R, j, hsl, :],
                     ps[3 * (n % 2)][r0:r0 + R, :].rearrange("p (h v) -> p h v", h=4), ALU.subtract), "vn")
                dve.wait_ge(sem["su_ps"], n + 1)
                for a in range(4):
                    hd = 4 * g + a
                    L(stt(st[:, hd, :], st[:, hd, :], sdec[:, c, hd:hd + 1], ps[2 + 3 * (n % 2)][:, a * 128:(a + 1) * 128],
                          ALU.mult, ALU.add), "s_new" if a == 3 else None)
            dve.wait_ge(sem["o_sb"], 10)
            L(tt(vf, ycat[:, :, :], ycat[:, :, :], ALU.mult), "osq")
            dve.wait_ge(sem["orms"], 1)
            L(V.reciprocal(lbuf[0:8, 0, 0:T], lbuf[0:8, 0, 0:T]), "on")
            for n in range(8):
                dve.wait_ge(sem["oss"], n + 2)
                L.go(tt(ycat[:, n, :], ycat[:, n, :], ps[n % 4][:, 0:T], ALU.mult), "on")
            dve.wait_ge(sem["on"], 9)
            L(stt(ycat[:, :, :], ycat[:, :, :], M("cnorm"), zf, ALU.mult, ALU.mult), "ozs")
            residual(8, 1)
            squares(3)
            apply_norm(3, 1, 1)
            moe(1)
            squares(4)
            apply_norm(4, None, None)

        @block.gpsimd
        def _(po):
            po.wait_ge(sem["conv"], 1)
            po.wait_ge(sem["hst"], 1)
            po.dma_start(t["aconv"], cst3[:, :, :, :]).then_inc(sem["st_small"], 16)
            po.dma_start(t["ah"], hst[:, :, :]).then_inc(sem["st_small"], 16)

            def gather(index, dst, src, bound):
                return po.indirect_dma_start(dst, None, src, bass.IndirectOffsetOnAxis(ap=index, axis=0),
                                             bounds_check=bound, oob_is_err=False)

            def scatter(index, dst, src, bound):
                return po.indirect_dma_start(dst, bass.IndirectOffsetOnAxis(ap=index, axis=0), src, None,
                                             bounds_check=bound, oob_is_err=False)

            def moe(l):
                B = NE * l
                for j, (t0, P) in enumerate(TILES):
                    po.wait_ge(sem["shu_sb"], 3 * l + j + 1)
                    po.tensor_tensor(shh_[0:P, j, :], shs[0:P, j, :], shu_[0:P, j, :], ALU.mult)\
                        .then_inc(sem["shh"], 1)
                po.wait_ge(sem["h2_st"], 48 * (l + 1))
                po.wait_ge(sem["xgz"], l + 1)

                def fetch(e, p, wait):
                    if wait:
                        po.wait_ge(sem["trx"], e + (B - 1))
                    po.wait_ge(sem["ig"], e + (B + 1))
                    po.sem_inc(sem["passed"], 1)
                    gather(icg[0:CAP, p, 0:1], xgb[0:CAP, p, :], H2, T - 1).then_inc(sem[f"xg{p}"], 16)

                def store(e, p):
                    po.wait_ge(sem["isx"], e + (B + 1))
                    po.wait_ge(sem["ya_e"], e + (B + 1))
                    po.wait_ge(sem["yb_e"], e + (B + 1))
                    po.sem_inc(sem["passed"], 1)
                    scatter(ics[0:CAP, p, 0:1], Y, yb[0:CAP, p, :], T * TOPK - 1).then_inc(sem[f"ysc{p}"], 16)

                def step(e0, i=None):
                    e = e0 if i is None else i * 2 + e0
                    if e0 + 3 < NE:
                        fetch(e + 3, (e0 + 1) % 2, True)
                    if e0:
                        store(e - 1, (e0 - 1) % 2)

                fetch(0, 0, False)
                fetch(1, 1, False)
                fetch(2, 0, True)
                for e in range(3):
                    step(e)
                with po.Fori(0, (NE - 6) // 2) as i:
                    step(3, i)
                    step(4, i)
                for e in range(NE - 3, NE):
                    step(e)
                store(NE - 1, (NE - 1) % 2)
                for p in range(2):
                    po.wait_ge(sem[f"ysc{p}"], 8 * (B + NE))

                po.wait_ge(sem["flag"], l + 1)
                more = po.value_load(flagi[0:1, 0:1], min_val=0, max_val=1)
                with po.If(more > 0):
                    s = lambda n: sem[f"{n}{l}"]
                    po.sem_inc(s("od"), 1)
                    with po.Fori(0, 2) as bb:
                        with po.Fori(0, NE) as e:
                            J = bb * NE + e
                            po.wait_ge(s("ovd"), J * 2 + 1)
                            po.sem_inc(sem["passed"], 1)
                            gather(ico[0:CAP, 0:1], xgb[0:CAP, 0, :], H2, T - 1).then_inc(s("og"), 16)
                            po.wait_ge(s("ova"), J * 4 + 4)
                            po.sem_inc(sem["passed"], 1)
                            scatter(ico[0:CAP, 2:3], Y, yb[0:CAP, 0, :], T * TOPK - 1).then_inc(s("osc"), 16)
                            po.wait_ge(s("osc"), J * 16 + 16)
                            po.sem_inc(s("od"), 1)
                po.wait_ge(sem["rowi"], l + 1)
                for n in range(24):
                    j, k = n // 8, n % 8
                    P = TILES[j][1]
                    if n >= 4:
                        po.wait_ge(sem["cb"], 24 * l + n - 3)
                    gather(rowi[0:P, j, k:k + 1], gb[0:P, n % 4, :], Y, T * TOPK - 1).then_inc(sem[f"got{n % 4}"], 16)

            moe(0)
            for j, (t0, P) in enumerate(TILES):
                f = lambda v: v[0:P, 0:4 * P].rearrange("p (h i) -> p h i", h=4)
                for lv in range(LEV_N[j]):
                    for g in range(2):
                        m = STEP0[j] + 2 * lv + g
                        if lv == 0:
                            po.wait_ge(sem["nmat"], 2 * j + g + 1)
                        if m >= 2:
                            po.wait_ge(sem["y_ps"], m - 1)
                        mk = C("mask")[0:P, lv * 128:lv * 128 + P].unsqueeze(1).broadcast_to([P, 4, P])
                        po.tensor_tensor(f(ubuf[:, g, :]), f(nbuf[:, g, :]), mk, ALU.mult).then_inc(sem["um"], 1)
            po.wait_ge(sem["cc"], 1)
            po.dma_start(t["cconv"], cc3[:, :, :, :]).then_inc(sem["st_small"], 16)
            po.wait_ge(sem["s_new"], 10)
            for g in range(2):
                po.dma_start(t["S"][g, :, :, :], sst[:, g, :, :]).then_inc(sem["st_small"], 16)
            po.wait_ge(sem["st_small"], 16 * 5)
            moe(1)


def constants():
    c = np.zeros((128, CST_N), np.float32)
    m, i = np.arange(128)[:, None], np.arange(128)[None, :]

    def put(name, v):
        c[:, CST[name][0]:CST[name][1]] = v

    put("ident", m == i)
    put("ones", 1)
    put("tri", (m <= i) & (m // CH == i // CH))
    put("same", m // CH == i // CH)
    put("mask", np.concatenate([(m // (2 * s) == i // (2 * s)) & (i // s % 2 == 1) & (m // s % 2 == 0)
                                for s in LEVELS], axis=1))
    put("before", m < i)
    g = np.arange(8)
    put("lower", (g[None, :] < g[:, None]).reshape(1, 64))
    put("iota", np.arange(T))
    put("slot", m)
    put("eps", np.array([EPS, 128 * EPS]))
    put("pick", np.arange(31) == 15)
    put("l2", np.where(m < HC, 128.0, 1.0) * np.array([1.0, EPS]))
    return c


def kernel(**inputs):
    import concourse.bacc as bacc
    from concourse.bass_utils import run_bass_kernel_spmd

    a = {k: np.asarray(v) for k, v in inputs.items()}

    def chunks(v):
        v = v.reshape(v.shape[:-1] + (-1, 128))
        return np.moveaxis(v, -1, 0).reshape(128, -1)

    def tiles(w):
        return np.ascontiguousarray(w.reshape(KC, 128, -1, 2, 128).transpose(2, 1, 3, 0, 4)).reshape(-1, 128, UNIT)

    def halves(w):
        return np.ascontiguousarray(w.reshape(2, 4, 128, 512).transpose(0, 2, 1, 3)).reshape(2, 128, UNIT)

    def expert_units(l):
        gu = np.concatenate([np.concatenate([a["e_w_gate"][l], a["s_w_gate"][l][None]]),
                             np.concatenate([a["e_w_up"][l], a["s_w_up"][l][None]])], axis=-1)
        dn = np.concatenate([a["e_w_down"][l], a["s_w_down"][l][None]])
        out = np.empty((NE + 1, 3, 128, UNIT), np.float32)
        out[:, 0:2] = gu.reshape(NE + 1, 2, 4, 128, 512).transpose(0, 1, 3, 2, 4).reshape(NE + 1, 2, 128, UNIT)
        out[:, 2] = dn.reshape(NE + 1, 2, 128, D).transpose(0, 2, 1, 3).reshape(NE + 1, 128, UNIT)
        return out.reshape(-1, 128, UNIT)

    small = np.zeros((128, SML_N), np.float32)

    def put(name, v):
        small[:, SML[name][0]:SML[name][1]] = v

    cond = np.stack([a["c_prompt"][0], a["c_sample"][0]])
    put("cond", cond.reshape(2, KC, 128).transpose(2, 1, 0).reshape(128, 16))
    norms = np.stack([a["norm1_g"][0], a["norm2_g"][0], a["norm1_g"][1], a["norm2_g"][1], a["final_g"]])
    put("norms", chunks(norms))
    put("bmod", chunks(a["b_mod"]))
    put("aconv", a["a_conv_w"][0].reshape(4, 4, 128).transpose(2, 1, 0).reshape(128, 16))
    put("aconvb", chunks(a["a_conv_b"][0]))
    put("abr", chunks(a["a_b_r"][0]))
    put("abi", chunks(a["a_b_i"][0]))
    put("alam", chunks(a["a_lambda"][0]))
    put("ah0", chunks(a["state_a_h"][0, 0]))
    put("astate", a["state_a_conv"][0, 0].reshape(3, 4, 128).transpose(2, 1, 0).reshape(128, 12))
    put("cconv", a["c_conv_w"][0].reshape(4, 24, 128).transpose(2, 1, 0).reshape(128, 96))
    put("cstate", a["state_c_conv"][0, 0].reshape(3, 24, 128).transpose(2, 1, 0).reshape(128, 72))
    put("cnorm", a["c_norm_g"][0][:, None])
    put("alog", a["c_A_log"][0][None])
    put("dtb", a["c_dt_bias"][0][None])
    put("rb", a["router_bias"].reshape(1, 128))
    put("router", a["router_w"].reshape(2, KC, 128, NE).transpose(2, 0, 1, 3).reshape(128, 1024))
    w1 = a["w_in1"][0]
    put("wab", w1[:, 4096:4112].reshape(KC, 128, 16).transpose(1, 0, 2).reshape(128, 128))

    table = a["b_rel_bias"][0]

    def band(q0, nq, nk):
        rel = np.clip((q0 + np.arange(nq))[:, None] - np.arange(nk)[None, :], -128, 128) + 128
        return np.ascontiguousarray(table[:, rel].transpose(1, 0, 2))

    x = np.concatenate([a["x_prompt"][0], a["x_sample"][0]])
    w0 = a["w_in0"][0]
    arrays = {
        "small": small, "const": constants(),
        "x": np.ascontiguousarray(x.reshape(T, KC, 128).transpose(2, 1, 0)),
        "biasP0": band(0, 128, 128), "biasP1": band(128, 128, 256), "biasS": band(256, NS, T),
        "kcache": np.ascontiguousarray(a["cache_b_k"][0, 0].reshape(NP_, 4, 128).transpose(2, 1, 0)),
        "vcache": np.ascontiguousarray(a["cache_b_v"][0, 0].reshape(2, 128, 512).transpose(1, 0, 2)),
        "wr": np.ascontiguousarray(a["a_w_r"][0].reshape(4, 2, 64, 64).transpose(2, 1, 0, 3)),
        "wi": np.ascontiguousarray(a["a_w_i"][0].reshape(4, 2, 64, 64).transpose(2, 1, 0, 3)),
        "S0": np.ascontiguousarray(a["state_c_S"][0, 0].transpose(1, 0, 2)),
        "wmod": np.ascontiguousarray(a["w_mod"].reshape(2, 2, 4, 128, MOD_B, 512).transpose(0, 4, 1, 3, 2, 5))
        .reshape(2 * MOD_U, 128, UNIT),
        "win0": np.concatenate([tiles(w0[:, 0:2048]), halves(w0[:, 2048:2560])]),
        "wout0": tiles(a["w_out0"][0]),
        "win1": tiles(w1[:, 0:4096]),
        "wout1": tiles(a["w_out1"][0]),
        "wexp": np.concatenate([expert_units(0), expert_units(1)]),
    }
    outs = {"y": (128, KC, T), "k": (128, 4, T), "v": (T, 512), "aconv": (128, 4, 2, 3), "ah": (128, 4, 2),
            "cconv": (128, 24, 2, 3), "S": (2, 128, HC, 128)}
    nc = bacc.Bacc("TRN2", target_bir_lowering=False, num_devices=1)
    t = {n: nc.dram_tensor(f"in_{n}", v.shape, F32, kind="ExternalInput").ap() for n, v in arrays.items()}
    t.update({n: nc.dram_tensor(f"out_{n}", s, F32, kind="ExternalOutput").ap() for n, s in outs.items()})
    t["H2"] = nc.dram_tensor("h_rows", (T, D), F32, kind="Internal").ap()
    t["Y"] = nc.dram_tensor("expert_rows", (T * TOPK, D), F32, kind="Internal").ap()
    build(nc, t)
    r = run_bass_kernel_spmd(nc, [{f"in_{n}": v for n, v in arrays.items()}], core_ids=[0]).results[0]
    r = {n: r[f"out_{n}"] for n in outs}

    y = r["y"].transpose(2, 1, 0).reshape(T, D)
    k = r["k"].transpose(2, 1, 0).reshape(T, HB, DHB)
    v = r["v"].reshape(T, HB, DHB)
    conv_a = r["aconv"].transpose(2, 3, 1, 0).reshape(2, 3, 512)
    h_a = r["ah"].transpose(2, 1, 0).reshape(2, 512)
    conv_c = r["cconv"].transpose(2, 3, 1, 0).reshape(2, 3, 3072)
    S = r["S"].transpose(0, 2, 1, 3)
    c = np.ascontiguousarray
    return (c(y[None, 0:NP_]), c(y[None, NP_:T]), c(k[None, None, 0:NP_]), c(k[None, None, NP_:T]),
            c(v[None, None, 0:NP_]), c(v[None, None, NP_:T]), c(conv_a[None, 0:1]), c(conv_a[None, 1:2]),
            c(h_a[None, 0:1]), c(h_a[None, 1:2]), c(conv_c[None, 0:1]), c(conv_c[None, 1:2]),
            c(S[None, 0:1]), c(S[None, 1:2]))
```

```python
import numpy as np
import concourse.bass as bass
from concourse import mybir

F32 = mybir.dt.float32
I32 = mybir.dt.int32
BF16 = mybir.dt.bfloat16
ALU = mybir.AluOpType
ACT = mybir.ActivationFunctionType
AX = mybir.AxisListType

D, NP_, NS, T = 1024, 256, 32, 288
KC = D // 128
GROUPS = [(0, NP_), (NP_, T)]
TILES = [(0, 128), (128, 128), (256, 32)]
CH, EPS = 64, 1e-6
HB, DHB, HC = 8, 64, 8
NE, EG, TOPK, DE = 64, 8, 8, 256
CAP = 96
LIM = 4096
XPAD = NP_ + NS + 6
SEG = NP_ + 3
XW = XPAD - 3
UNIT = 2048
NU = 6
LEVELS = [1, 2, 4, 8, 16, 32]
FIRST_BANKS = [(0, 1, 2, 3, 4, 5), (6, 7, 0, 1, 2, 3)]
LEV_N = [6, 6, 5]
STEP0 = [0, 12, 24]
PROD0 = [0, 10, 20]
COLLECT = [(k, j) for k in range(TOPK - 1, -1, -1) for j in range(3)]
MOD_AHEAD = 2
SEL_STEPS = [(3, 4), (5, 6), (7,)]
O_BANKS = [1, 4, 6]
assert T % CAP == 0 and T // CAP == 3

CST_W = dict(ident=128, ones=128, tri=128, same=128, mask=6 * 128, before=128, lower=64, iota=T,
             slot=1, eps=2, pick=31, l2=2, fold=2)
SML_W = dict(cond=16, norms=40, bmod=96, aconv=16, aconvb=4, abr=4, abi=4, alam=4, ah0=4, astate=12,
             cconv=96, cstate=72, cnorm=1, alog=8, dtb=8, rb=128, router=1024, wab=128)


def places(widths):
    at, out = 0, {}
    for name, w in widths.items():
        out[name] = (at, at + w)
        at += w
    return out, at


CST, CST_N = places(CST_W)
SML, SML_N = places(SML_W)

MOD_U, IN0_U, OUT0_U, MOE_U, IN1_U = 24, 10, 4, 3 + 3 * NE, 16
U_MOD0 = 0
U_IN0 = U_MOD0 + MOD_U
U_MOD1 = U_IN0 + IN0_U
U_OUT0 = U_MOD1 + MOD_U
MOD_B = MOD_U // 2
U_MOE0 = U_OUT0 + OUT0_U
U_IN1 = U_MOE0 + MOE_U
U_OUT1 = U_IN1 + IN1_U
U_MOE1 = U_OUT1 + 4
U_MODS = [U_MOD0, U_MOD1]
U_MOES = [U_MOE0, U_MOE1]

SEMS = """zero y_zero ld_small ld_rest ld_att ld_state st_mix st_small st_out w_used mod_row mod_t cond lamn lame lam sq ss rms h
 proj_ps proj_ev v_ps v_ev pad conv hst gate_ps gate_i lru_a lru_w lru_s lru_g ya
 s_ps s_sm p_exp p_nrm pt_ps pt_sb pv_ps pv_sb out_ps out_x
 tm_ps tm_sb h2_st lg_ps lgz xgz score mask rank_ps flag rowi sel sel_ps
 shu_ps shu_sb shh sht_ps sht_sb shd_ps shd_sb
 ig isx xg0 xg1 trx xta xtb up sg hd trh ht dn ya_e yb_e ysc0 ysc1 got0 got1 got2 got3 cb acc_ps acc_x
 ab_ps ab_act ab_sb ab_e gcum_ps gcum_e gdec
 padc cc cacc csilu lsq lss lrms qk_n gb_ps gb_e ldif lexp nmat kk_ps tk_ps tk_sb um
 y_ps y_sb z_ps xd u_ps batch s0 ws_ps vn o_ps su_ps s_new o_sb osq oss on
 dve act passed""".split()
OVF = """od ovi ovd ova ovp og osc ow osel osel_ps""".split()


def build(nc, t):
    sem = {n: nc.alloc_semaphore(n) for n in SEMS}
    for l in range(2):
        for n in OVF:
            sem[f"{n}{l}"] = nc.alloc_semaphore(f"{n}{l}")
    w_loaded = [nc.alloc_semaphore(f"w_loaded{u}") for u in range(NU)]

    def sb(name, shape, dt=F32):
        return nc.alloc_sbuf_tensor(name, shape, dt)

    ring = sb("ring", [128, NU, UNIT])
    cst = sb("cst", [128, CST_N])
    sml = sb("sml", [128, SML_N])
    x = sb("x", [128, KC, T])
    h = sb("h", [128, KC, T])
    ycat = sb("ycat", [128, KC, T])
    rms = sb("rms", [128, T])
    idle = sb("idle", [128, 1])
    condT = sb("condT", [128, KC, 32])
    mod = sb("mod", [128, 2, 48, 2])
    scale1 = sb("scale1", [128, 2, 2, KC, 2])
    hst = sb("hst", [128, 4, 2])
    cst3 = sb("cst3", [128, 4, 2, 3])
    cc3 = sb("cc3", [128, 24, 2, 3])
    arena = sb("arena", [128, 29400])
    ps = [nc.alloc_psum_tensor(f"ps{b}", [128, 512], F32) for b in range(8)]

    def C(name, p=128):
        return cst[0:p, CST[name][0]:CST[name][1]]

    def M(name, p=128):
        return sml[0:p, SML[name][0]:SML[name][1]]

    def carver(at):

        def carve(*dims):
            n = int(np.prod(dims))
            a = arena[:, at[0]:at[0] + n]
            at[0] += n
            assert at[0] <= 29400, at[0]
            if len(dims) == 2:
                a = a.rearrange("p (a b) -> p a b", a=dims[0])
            if len(dims) == 3:
                a = a.rearrange("p (a b c) -> p a b c", a=dims[0], b=dims[1])
            return a
        return carve

    ident, ones = C("ident"), C("ones")

    place = [0]
    cv = carver(place)
    xpad, gaT, qT, kT = cv(4, XPAD), cv(4, T), cv(4, T), cv(4, T)
    ksT = cv(4, T)
    vtm, vcache = cv(3, 512), cv(2, 512)
    biasP0, biasP1, biasS = cv(HB, 128), cv(HB, 256), cv(HB, T)
    bdr, bdi = cv(4, 128), cv(4, 128)
    xc, rg, ig_, aa, tt_ = (cv(4, XW) for _ in range(5))
    hh = cv(4, XW)
    lamw = cv(8, 4)
    s_sb, mx, rsum = cv(2, T), cv(2, 2), cv(2, 1)
    pT = cv(2, 3, 128)
    modrow = cv(2, 512)

    place = [0]
    cv = carver(place)
    qf, kf, vf, zf = (cv(HC, T) for _ in range(4))
    kdec = cv(3, HC, 128)
    share = cv(1, 5400)[:, 0, :]
    uu = share[:, 0:3072].rearrange("p (t h v) -> p t h v", t=3, h=HC)
    atm = share[:, 3072:3072 + 2304]
    raw = share[:, 0:2 * 4 * XPAD].rearrange("p (a c x) -> p a c x", a=2, c=4)
    cacc = share[:, 2400:2400 + 2 * 4 * XW].rearrange("p (a c x) -> p a c x", a=2, c=4)
    sst = cv(2, HC, 128)
    lbuf = cv(2, 512)
    SQ0 = place[0]
    nbuf, xbuf, dbuf, ybuf, ubuf, kbe, vbe, egb = (cv(2, 512) for _ in range(8))
    sqb = arena[:, SQ0:SQ0 + 16 * T].rearrange("p (c x) -> p c x", c=16)
    kdcol = cv(3, 8)
    gtm, btm, spt, gcol, glast, begc = (cv(3, 8) for _ in range(6))
    spw = cv(6, 24)
    sdec = cv(5, HC)

    def att(t):
        P = TILES[t][1]
        return atm[:, t * 1024:t * 1024 + HC * P].rearrange("p (h i) -> p h i", h=HC)

    def four(buf, P):
        return buf[:, 0:4 * P].rearrange("p (h i) -> p h i", h=4)

    place = [0]
    cv = carver(place)
    ysh = cv(3, D)
    xgb, yb = cv(2, D), cv(2, D)
    xgT = cv(2, KC, CAP)
    gb = cv(4, D)
    selb = cv(2, 3, 4 * CAP).bitcast(BF16)
    silu_b, hid = cv(1, DE)[:, 0, :], cv(1, DE)[:, 0, :]
    hidT = cv(2, CAP)
    shs, shu_, shh_, shT = cv(3, DE), cv(3, DE), cv(3, DE), cv(3, 2, 128)
    lg, score, selv, msk, gates, rk, tmp1, tmp2 = (cv(3, NE) for _ in range(8))
    top2, gsc, gcmp, geq, grk, top8, gsum = cv(3, 8, 8), cv(3, 8), cv(3, 8, 8), cv(3, 8, 8), cv(3, 8), cv(3, 8), cv(3, 1)
    tg = cv(3, NE, 3).bitcast(BF16)
    rkb, slots = cv(3, NE // 2).bitcast(BF16), cv(1, CAP // 2)[:, 0, :].bitcast(BF16)
    idxf = cv(2, NE)
    rowif = cv(3, 8)
    cntf, start, srow = cv(1, 66)[:, 0, :], cv(1, NE)[:, 0, :], cv(1, NE)[:, 0, :]
    rowi = cv(3, 8).bitcast(I32)
    idx = cv(NE, 3).bitcast(I32)
    icg = cv(2, 1).bitcast(I32)
    ics = cv(2, 1).bitcast(I32)
    ico = cv(1, 3)[:, 0, :].bitcast(I32)
    flagi = sb("flagi", [1, 1], I32)

    rk_flat, rkb_flat = rk.rearrange("p a b -> p (a b)"), rkb.rearrange("p a b -> p (a b)")
    H2, Y, SH = t["H2"], t["Y"], t["SH"]

    class Chain:

        def __init__(self, eng, own):
            self.eng, self.own, self.n = eng, own, {}

        def go(self, ins, name=None):
            name = name or self.own
            self.n[name] = self.n.get(name, 0) + 1
            ins.then_inc(sem[name], 1)
            self.last = name

        def __call__(self, ins, name=None):
            self.go(ins, name)
            self.eng.wait_ge(sem[self.last], self.n[self.last])

    def unit(n):
        return ring[:, n % NU, :]

    def wait_unit(eng, n):
        eng.wait_ge(w_loaded[n % NU], 16 * (n // NU + 1))

    with nc.Block() as block:
        @block.sync
        def _(sp):
            def used(n):
                if n < U_IN0:
                    return "w_used", n + 1
                if U_MOD1 <= n < U_OUT0:
                    return "w_used", MOD_U + (n - U_MOD1) + 1
                if n < U_MOD1:
                    q = n - U_IN0
                    return ("proj_ps", 2 * q + 2) if q < 8 else ("v_ps", q - 7)
                if n < U_MOE0:
                    return "out_ps", 2 * (n - U_OUT0) + 2
                if U_IN1 <= n < U_OUT1:
                    return "proj_ps", 16 + 2 * (n - U_IN1) + 2
                if U_OUT1 <= n < U_MOE1:
                    return "out_ps", 8 + 2 * (n - U_OUT1) + 2
                l = 0 if n < U_IN1 else 1
                m, B = n - U_MOES[l], NE * l
                if m < 2:
                    return "shu_ps", 2 * l + m + 1
                if m == 2:
                    return "shd_ps", 3 * l + 3
                if m < 5:
                    return "up", B + 1
                if m == MOE_U - 1:
                    return "dn", B + NE
                e, r = (m - 5) // 3 + 1, (m - 5) % 3
                return ("up", B + e + 1) if r < 2 else ("dn", B + e)

            def load(n, src, i=None, per=0):
                if n >= NU:
                    name, v = used(n - NU)
                    sp.wait_ge(sem[name], v if i is None else i * per + v)
                sp.dma_start(ring[:, n % NU, :], src).then_inc(w_loaded[n % NU], 16)

            def at(w, i, k, n):
                return w[bass.ds(i * k + n, 1), :, :].rearrange("a p n -> p (a n)")

            for n in range(NU):
                load(n, t["wmod"][n, :, :])
            with sp.Fori(0, MOD_U // NU - 1) as i:
                for u in range(NU):
                    load(NU + u, at(t["wmod"], i, NU, NU + u), i, NU)
            for n in range(IN0_U):
                load(U_IN0 + n, t["win0"][n, :, :])
            for n in range(NU):
                load(U_MOD1 + n, t["wmod"][MOD_U + n, :, :])
            with sp.Fori(0, MOD_U // NU - 1) as i:
                for u in range(NU):
                    load(U_MOD1 + NU + u, at(t["wmod"], i, NU, MOD_U + NU + u), i, NU)
            for n in range(4):
                load(U_OUT0 + n, t["wout0"][n, :, :])

            def moe_loads(l):
                b, w = U_MOES[l], t["wexp"]
                W0 = l * (NE + 1) * 3
                for n in range(3):
                    load(b + n, w[W0 + 3 * NE + n, :, :])
                for n in range(2):
                    load(b + 3 + n, w[W0 + n, :, :])

                def pair(e0, i=None):
                    for n, j in enumerate((3 * e0, 3 * e0 + 1, 3 * e0 - 1)):
                        m = b + 5 + 3 * (e0 - 1) + n
                        load(m, w[W0 + j, :, :] if i is None else at(w, i, 6, W0 + j), i, 2)

                pair(1)
                pair(2)
                with sp.Fori(0, (NE - 4) // 2) as i:
                    pair(3, i)
                    pair(4, i)
                pair(NE - 1)
                load(b + MOE_U - 1, w[W0 + 3 * NE - 1, :, :])
                sp.wait_ge(sem["flag"], l + 1)
                more = sp.value_load(flagi[0:1, 0:1], min_val=0, max_val=1)
                with sp.If(more > 0):
                    sp.wait_ge(sem["dn"], NE * (l + 1))
                    with sp.Fori(0, 2) as bb:
                        with sp.Fori(0, NE) as e:
                            sp.wait_ge(sem[f"od{l}"], bb * NE + e + 1)
                            for n in range(3):
                                sp.dma_start(ring[:, n, :], at(w, e, 3, W0 + n)).then_inc(sem[f"ow{l}"], 16)
                    sp.wait_ge(sem[f"od{l}"], 2 * NE + 1)

            moe_loads(0)
            for n in range(IN1_U):
                load(U_IN1 + n, t["win1"][n, :, :])
            for n in range(4):
                load(U_OUT1 + n, t["wout1"][n, :, :])
            moe_loads(1)
            for hf in range(2):
                sp.wait_ge(sem["h"], 9 + hf)
                sp.dma_start(t["y"][:, 4 * hf:4 * hf + 4, :], h[:, 4 * hf:4 * hf + 4, :]).then_inc(sem["st_out"], 16)
            sp.wait_ge(sem["st_out"], 32)
            sp.wait_ge(sem["st_mix"], 16 * 4)
            sp.wait_ge(sem["st_small"], 16 * 5)

        @block.tensor
        def _(pe):
            mm = nc.tensor.matmul
            tr = nc.tensor.transpose

            def mod_unit(l, n, bank):
                b, q = n // 2, n % 2
                wait_unit(pe, U_MODS[l] + n)
                for k in range(4):
                    last = mm(ps[bank][32 * k:32 * k + 32, :], condT[:, 4 * q + k, :],
                              unit(U_MODS[l] + n)[:, k * 512:(k + 1) * 512], start=(q == 0), stop=(q == 1),
                              tile_position=(0, 32 * k))
                last.then_inc(sem["w_used"], 1)

            def mod_turn(l, b, bank):
                pe.wait_ge(sem["mod_row"], MOD_B * l + b + 1)
                for q in range(4):
                    last = mm(ps[bank][:, (4 * b + q) * 2:(4 * b + q) * 2 + 2], modrow[:, b % 2, q * 128:(q + 1) * 128],
                              C("fold"), start=True, stop=True)
                last.then_inc(sem["mod_t"], 1)

            def sum_squares(k):
                for c in range(KC):
                    pe.wait_ge(sem["sq"], KC * k + c + 1)
                    last = mm(ps[7][:, 0:T], ones, h[:, c, :], start=(c == 0), stop=(c == KC - 1))
                last.then_inc(sem["ss"], 1)

            def halves(k, norm):
                if norm is not None and k % 4 == 0:
                    pe.wait_ge(sem["h"], 2 * norm + k // 4 + 1)

            def project(u0, tiles, base, rhs, rdy, norm=None):
                for i in range(tiles):
                    n = u0 + i // 2
                    if i % 2 == 0:
                        wait_unit(pe, n)
                    if base + i >= 4:
                        pe.wait_ge(sem[rdy], base + i - 3)
                    for k in range(KC):
                        if i == 0:
                            halves(k, norm)
                        a = (i % 2) * KC + k
                        last = mm(ps[i % 4][:, 0:T], unit(n)[:, a * 128:(a + 1) * 128], rhs[:, k, :],
                                  start=(k == 0), stop=(k == KC - 1))
                    last.then_inc(sem["proj_ps" if rdy == "proj_ev" else "out_ps"], 1)

            pe.wait_ge(sem["cond"], 1)
            for b in range(MOD_B):
                if b >= 2:
                    pe.wait_ge(sem["mod_row"], b - 1)
                mod_unit(0, 2 * b, b % 2)
                mod_unit(0, 2 * b + 1, b % 2)
                if b == 1:
                    pe.wait_ge(sem["ld_rest"], 32)
                    sum_squares(0)
                if b:
                    mod_turn(0, b - 1, 2)
            mod_turn(0, MOD_B - 1, 2)
            project(U_IN0, 16, 0, h, "proj_ev", 0)
            for kq in range(2):
                wait_unit(pe, U_IN0 + 8 + kq)
                for j, (t0, P) in enumerate(TILES):
                    for k in range(4):
                        last = mm(ps[4 + j][0:P, :], h[:, kq * 4 + k, t0:t0 + P],
                                  unit(U_IN0 + 8 + kq)[:, k * 512:(k + 1) * 512],
                                  start=(kq == 0 and k == 0), stop=(kq == 1 and k == 3))
                last.then_inc(sem["v_ps"], 1)
            pe.wait_ge(sem["ld_att"], 16 * 9)
            pe.wait_ge(sem["conv"], 1)
            pe.wait_ge(sem["proj_ev"], 16)
            for c in range(4):
                last = mm(ps[c][:, 0:XW], bdr[:, c, :], xc[:, c, :], start=True, stop=True)
            last.then_inc(sem["gate_ps"], 1)
            pe.wait_ge(sem["v_ev"], 1)
            for c in range(4):
                last = mm(ps[4 + c][:, 0:XW], bdi[:, c, :], xc[:, c, :], start=True, stop=True)
            last.then_inc(sem["gate_ps"], 1)
            units = [(j, hd) for j in range(3) for hd in range(HB)]

            def scores(n):
                j, hd = units[n]
                t0, P = TILES[j]
                b, c = DHB * (hd % 2), hd // 2
                nk = (128, 256, T)[j]
                keys = ksT if j == 2 else kT
                if n >= 2:
                    pe.wait_ge(sem["s_sm"], n - 1)
                mm(ps[n % 2][0:P, 0:nk], qT[b:b + DHB, c, t0:t0 + P], keys[b:b + DHB, c, 0:nk],
                   start=True, stop=True).then_inc(sem["s_ps"], 1)

            pe.wait_ge(sem["gate_i"], 1)
            scores(0)
            scores(1)

            def mod1(u):
                if u >= 2 and u % 2 == 0:
                    pe.wait_ge(sem["mod_row"], MOD_B + u // 2)
                mod_unit(1, u, 6)
                if u >= 2 and u % 2 == 0:
                    mod_turn(1, u // 2 - 1, 7)

            for u in range(MOD_AHEAD):
                mod1(u)
            for n, (j, hd) in enumerate(units):
                t0, P = TILES[j]
                if n + 2 < len(units):
                    scores(n + 2)
                kts = [(0, 128)] if j == 0 else [(0, 128), (1, 128)] if j == 1 else [(0, 128), (1, 128), (2, 32)]
                pe.wait_ge(sem["p_nrm"], n + 1)
                if n >= 2:
                    pe.wait_ge(sem["pt_sb"], n - 1)
                for kt, K in kts:
                    last = tr(ps[2 + n % 2][0:K, kt * 128:kt * 128 + P],
                              s_sb[0:P, n % 2, kt * 128:kt * 128 + K], ident[0:P, 0:P])
                last.then_inc(sem["pt_ps"], 1)
                if n + MOD_AHEAD < MOD_U:
                    mod1(n + MOD_AHEAD)
                pe.wait_ge(sem["pt_sb"], n + 1)
                if n >= 2:
                    pe.wait_ge(sem["pv_sb"], n - 1)
                c = hd // 2
                for kt, K in kts:
                    val = vcache if (j == 2 and kt < 2) else vtm
                    last = mm(ps[4 + n % 2][:, 0:P], val[0:K, kt, c * 128:(c + 1) * 128], pT[0:K, n % 2, kt, 0:P],
                              start=(kt == 0), stop=(kt == kts[-1][0]))
                last.then_inc(sem["pv_ps"], 1)
            mod_turn(1, MOD_B - 1, 7)
            pe.wait_ge(sem["ya"], 1)
            pe.wait_ge(sem["pv_sb"], len(units))
            project(U_OUT0, 8, 0, ycat, "out_x")

            def moe(l):
                B, u0 = NE * l, U_MOES[l]
                for j, (t0, P) in enumerate(TILES):
                    for k in range(KC):
                        if j == 0:
                            halves(k, 2 * l + 1)
                        rw = M("router")[:, l * 512 + k * 64:l * 512 + (k + 1) * 64]
                        last = mm(ps[6][0:P, j * 64:(j + 1) * 64], h[:, k, t0:t0 + P], rw,
                                  start=(k == 0), stop=(k == KC - 1))
                last.then_inc(sem["lg_ps"], 1)
                for j, (t0, P) in enumerate(TILES):
                    for k in range(KC):
                        last = tr(ps[2 * j + k // 4][0:P, (k % 4) * 128:(k % 4 + 1) * 128], h[:, k, t0:t0 + P], ident)
                    last.then_inc(sem["tm_ps"], 1)
                pe.wait_ge(sem["tm_sb"], 3 * (l + 1))
                for q in range(2):
                    wait_unit(pe, u0 + q)
                    for j, (t0, P) in enumerate(TILES):
                        for k in range(4):
                            last = mm(ps[j][0:P, :], h[:, 4 * q + k, t0:t0 + P],
                                      unit(u0 + q)[:, k * 512:(k + 1) * 512],
                                      start=(q == 0 and k == 0), stop=(q == 1 and k == 3))
                    last.then_inc(sem["shu_ps"], 1)
                pe.wait_ge(sem["mask"], l + 1)
                for j, (t0, P) in enumerate(TILES):
                    for jj in range(j + 1):
                        PP = TILES[jj][1]
                        w = C("before")[0:PP, 0:P] if jj == j else ones[0:PP, 0:P]
                        last = mm(ps[7][0:P, j * 64:(j + 1) * 64], w, msk[0:PP, jj, :], start=(jj == 0), stop=(jj == j))
                for jj, (t0, PP) in enumerate(TILES):
                    last = mm(ps[7][:, 192:256], ones[0:PP, :], msk[0:PP, jj, :], start=(jj == 0), stop=(jj == 2))
                last.then_inc(sem["rank_ps"], 1)

                def slot_table(g):
                    pe.wait_ge(sem["sel"], 8 * l + g + 1)
                    for e in range(8):
                        for j, (t0, P) in enumerate(TILES):
                            last = mm(ps[6][0:CAP, (8 * g + e) * 5:(8 * g + e) * 5 + 5],
                                      selb[0:P, g % 2, j, e * CAP:(e + 1) * CAP], tg[0:P, j, 8 * g + e, 0:5],
                                      start=(j == 0), stop=(j == 2))
                    last.then_inc(sem["sel_ps"], 1)

                for j, (t0, P) in enumerate(TILES):
                    pe.wait_ge(sem["shh"], 3 * l + j + 1)
                    for a in range(2):
                        last = tr(ps[3][:, a * 128:a * 128 + P], shh_[0:P, j, a * 128:(a + 1) * 128],
                                  ident[0:P, 0:P])
                    last.then_inc(sem["sht_ps"], 1)
                    pe.wait_ge(sem["sht_sb"], 3 * l + j + 1)
                for j, (t0, P) in enumerate(TILES):
                    if j == 0:
                        wait_unit(pe, u0 + 2)
                        pe.wait_ge(sem["shu_sb"], 3 * (l + 1))
                    b0, b1 = ((0, 1), (4, 5), (2, 3))[j]
                    for hf, bk in ((0, b0), (1, b1)):
                        for a in range(2):
                            last = mm(ps[bk][0:P, :], shT[:, j, a, 0:P],
                                      unit(u0 + 2)[:, a * D + hf * 512:a * D + (hf + 1) * 512],
                                      start=(a == 0), stop=(a == 1))
                    last.then_inc(sem["shd_ps"], 1)
                    if j == 0:
                        slot_table(0)
                slot_table(1)
                pe.wait_ge(sem["shd_sb"], 3 * (l + 1))

                def take(e, p):
                    pe.wait_ge(sem[f"xg{p}"], e * 8 + (8 * (B - p) + 16))
                    for k in range(KC):
                        last = tr(ps[4 + k // 4][:, (k % 4) * CAP:(k % 4 + 1) * CAP],
                                  xgb[0:CAP, p, k * 128:(k + 1) * 128], ident[0:CAP, 0:CAP])
                    last.then_inc(sem["trx"], 1)

                def up(e, p, n, i):
                    for q in range(2):
                        s = (n + q) % NU
                        v = 16 * ((n + q) // NU + 1)
                        pe.wait_ge(w_loaded[s], v if i is None else i * 16 + v)
                        for k in range(4):
                            last = mm(ps[2][0:CAP, :], xgT[:, p, 4 * q + k, :], ring[:, s, k * 512:(k + 1) * 512],
                                      start=(q == 0 and k == 0), stop=(q == 1 and k == 3))
                    last.then_inc(sem["up"], 1)

                def hidden(e):
                    pe.wait_ge(sem["hd"], e + (B + 1))
                    for a in range(2):
                        last = tr(ps[3][:, a * CAP:(a + 1) * CAP], hid[0:CAP, a * 128:(a + 1) * 128], ident[0:CAP, 0:CAP])
                    last.then_inc(sem["trh"], 1)

                def down(e, n, i, first=False):
                    pe.wait_ge(sem["ht"], e + (B + 1))
                    if not first:
                        pe.wait_ge(sem["ya_e"], e + B)
                        pe.wait_ge(sem["yb_e"], e + B)
                    s, v = n % NU, 16 * (n // NU + 1)
                    pe.wait_ge(w_loaded[s], v if i is None else i * 16 + v)
                    for a in range(2):
                        for hf in range(2):
                            last = mm(ps[hf][0:CAP, :], hidT[:, a, :], ring[:, s, a * D + hf * 512:a * D + (hf + 1) * 512],
                                      start=(a == 0), stop=(a == 1))
                    last.then_inc(sem["dn"], 1)

                take(0, 0)
                slot_table(2)

                def step(e0, i=None):
                    e = e0 if i is None else i * 2 + e0
                    n = u0 + 3 + (0 if e0 == 0 else 2 + 3 * (e0 - 1))
                    if e0 > 0:
                        hidden(e - 1)
                    if e0 + 1 < NE:
                        pe.wait_ge(sem["xta"], e + (B + 1))
                        pe.wait_ge(sem["xtb"], e + (B + 1))
                        take(e + 1, (e0 + 1) % 2)
                    else:
                        pe.wait_ge(sem["xta"], e + (B + 1))
                        pe.wait_ge(sem["xtb"], e + (B + 1))
                    up(e, e0 % 2, n, i)
                    for g in SEL_STEPS[e0] if e0 < 3 else ():
                        slot_table(g)
                    if e0 > 0:
                        down(e - 1, n + 2, i, first=(e0 == 1))

                for e in range(3):
                    step(e)
                with pe.Fori(0, (NE - 10) // 2) as i:
                    step(3, i)
                    step(4, i)
                for e in range(NE - 7, NE):
                    step(e)
                hidden(NE - 1)
                down(NE - 1, u0 + 3 + 2 + 3 * (NE - 1), None)

                pe.wait_ge(sem["flag"], l + 1)
                more = pe.value_load(flagi[0:1, 0:1], min_val=0, max_val=1)
                with pe.If(more > 0):
                    s = lambda n: sem[f"{n}{l}"]
                    pe.wait_ge(sem["ya_e"], B + NE)
                    pe.wait_ge(sem["yb_e"], B + NE)
                    with pe.Fori(0, 2) as bb:
                        for g in range(8):
                            pe.wait_ge(s("osel"), bb * 8 + (g + 1))
                            for e in range(8):
                                for j, (t0, P) in enumerate(TILES):
                                    last = mm(ps[6][0:CAP, (8 * g + e) * 5:(8 * g + e) * 5 + 5],
                                              selb[0:P, g % 2, j, e * CAP:(e + 1) * CAP], tg[0:P, j, 8 * g + e, 0:5],
                                              start=(j == 0), stop=(j == 2))
                            last.then_inc(s("osel_ps"), 1)
                        with pe.Fori(0, NE) as e:
                            J = bb * NE + e
                            pe.wait_ge(s("og"), J * 16 + 16)
                            for k in range(KC):
                                last = tr(ps[4 + k // 4][:, (k % 4) * CAP:(k % 4 + 1) * CAP],
                                          xgb[0:CAP, 0, k * 128:(k + 1) * 128], ident[0:CAP, 0:CAP])
                            last.then_inc(s("ovp"), 1)
                            pe.wait_ge(s("ova"), J * 4 + 1)
                            pe.wait_ge(s("ow"), J * 48 + 48)
                            for k in range(KC):
                                last = mm(ps[2][0:CAP, :], xgT[:, 0, k, :],
                                          ring[:, k // 4, (k % 4) * 512:(k % 4 + 1) * 512],
                                          start=(k == 0), stop=(k == KC - 1))
                            last.then_inc(s("ovp"), 1)
                            pe.wait_ge(s("ovd"), J * 2 + 2)
                            for a in range(2):
                                last = tr(ps[3][:, a * CAP:(a + 1) * CAP], hid[0:CAP, a * 128:(a + 1) * 128], ident[0:CAP, 0:CAP])
                            last.then_inc(s("ovp"), 1)
                            pe.wait_ge(s("ova"), J * 4 + 3)
                            for a in range(2):
                                for hf in range(2):
                                    last = mm(ps[hf][0:CAP, :], hidT[:, a, :],
                                              ring[:, 2, a * D + hf * 512:a * D + (hf + 1) * 512],
                                              start=(a == 0), stop=(a == 1))
                            last.then_inc(s("ovp"), 1)
                    pe.wait_ge(s("ova"), 8 * NE)
                    pe.wait_ge(s("ovd"), 4 * NE + 24)
                pe.wait_ge(sem["ya_e"], B + NE)
                pe.wait_ge(sem["yb_e"], B + NE)
                for j, (t0, P) in enumerate(TILES):
                    pe.wait_ge(sem["cb"], 24 * l + 21 + j + 1)
                    for k in range(KC):
                        last = tr(ps[2 * j + k // 4][:, (k % 4) * 128:(k % 4) * 128 + P],
                                  ysh[0:P, j, k * 128:(k + 1) * 128], ident[0:P, 0:P])
                    last.then_inc(sem["acc_ps"], 1)

            sum_squares(1)
            moe(0)

            sum_squares(2)
            for j, (t0, P) in enumerate(TILES):
                for k in range(KC):
                    if j == 0:
                        halves(k, 2)
                    last = mm(ps[6][0:P, j * 16:(j + 1) * 16], h[:, k, t0:t0 + P], M("wab")[:, k * 16:(k + 1) * 16],
                              start=(k == 0), stop=(k == KC - 1))
            last.then_inc(sem["ab_ps"], 1)
            pe.wait_ge(sem["acc_x"], 1)
            project(U_IN1, 32, 16, h, "proj_ev")
            pe.wait_ge(sem["ab_sb"], 1)
            for j, (t0, P) in enumerate(TILES):
                mm(ps[6][0:P, 64 + j * 8:72 + j * 8], C("tri")[0:P, 0:P], gtm[0:P, j, :], start=True, stop=True)
                last = mm(ps[6][0:P, 96 + j * 8:104 + j * 8], C("same")[0:P, 0:P], gtm[0:P, j, :],
                          start=True, stop=True)
            last.then_inc(sem["gcum_ps"], 1)
            pe.wait_ge(sem["proj_ev"], 48)
            for n in range(16):
                if n % 4 == 0:
                    pe.wait_ge(sem["lsq"], n // 4 + 1)
                last = mm(ps[0][0:16, 0:T], C("pick")[:, 15 - n:31 - n], sqb[:, n, :], start=(n == 0), stop=(n == 15))
            last.then_inc(sem["lss"], 1)
            for n in range(16):
                pe.wait_ge(sem["qk_n"], max(n - 2, 1))
                mm(ps[1 + n % 4][:, 0:T], ident[0:16, n:n + 1].broadcast_to([16, 128]), lbuf[0:16, 0, 0:T],
                   start=True, stop=True).then_inc(sem["lss"], 1)

            for j, (t0, P) in enumerate(TILES):
                blk = lambda b: ps[b][:, 0:4 * P].rearrange("p (h i) -> p h i", h=4)
                u_ = lambda buf: four(buf, P)[0:P]
                for g in range(2):
                    n = 2 * j + g
                    hs = range(4 * g, 4 * g + 4)
                    bg, bb, bk, bq, btk, btv = FIRST_BANKS[g]
                    if n == 0:
                        pe.wait_ge(sem["qk_n"], 17)
                        pe.wait_ge(sem["gdec"], 1)
                    elif g == 0:
                        pe.wait_ge(sem["batch"], n)
                    for a, hd in enumerate(hs):
                        last = mm(blk(bg)[:, a, :], gtm[0:P, j, hd:hd + 1].broadcast_to([P, 128]), C("tri")[0:P, 0:P],
                                  start=True, stop=True)
                    last.then_inc(sem["gb_ps"], 1)
                    for a, hd in enumerate(hs):
                        mm(blk(bb)[0:P, a, :], btm[0:P, j, hd:hd + 1].broadcast_to([P, P]), ident[0:P, 0:P],
                           start=True, stop=True)
                    if g:
                        pe.wait_ge(sem["ldif"], n)
                    for a, hd in enumerate(hs):
                        mm(blk(bk)[0:P, a, :], kf[:, hd, t0:t0 + P], kf[:, hd, t0:t0 + P], start=True, stop=True)
                    if g:
                        pe.wait_ge(sem["nmat"], 2 * n)
                    for a, hd in enumerate(hs):
                        last = mm(blk(bq)[0:P, a, :], kf[:, hd, t0:t0 + P], qf[:, hd, t0:t0 + P], start=True, stop=True)
                    last.then_inc(sem["kk_ps"], 1)
                    for a, hd in enumerate(hs):
                        tr(ps[btk][0:P, a * 128:(a + 1) * 128], kf[:, hd, t0:t0 + P], ident)
                        last = tr(ps[btv][0:P, a * 128:(a + 1) * 128], vf[:, hd, t0:t0 + P], ident)
                    last.then_inc(sem["tk_ps"], 1)
                pe.wait_ge(sem["ldif"], 2 * j + 2)
                for g in range(2):
                    pe.wait_ge(sem["um"], STEP0[j] + g + 1)
                    for a in range(4):
                        last = tr(blk(6 + g)[0:P, a, :], u_(ybuf[:, g, :])[:, a, :], ident[0:P, 0:P])
                    last.then_inc(sem["y_ps"], 1)
                for lv in range(1, LEV_N[j]):
                    for g in range(2):
                        m = STEP0[j] + 2 * lv + g
                        pe.wait_ge(sem["um"], m + 1)
                        pe.wait_ge(sem["xd"], m - 1)
                        for a in range(4):
                            last = mm(blk(6 + g)[0:P, a, :], u_(ubuf[:, g, :])[:, a, :], u_(dbuf[:, g, :])[:, a, :],
                                      start=True, stop=True)
                        last.then_inc(sem["y_ps"], 1)
                    for g in range(2):
                        pe.wait_ge(sem["y_sb"], PROD0[j] + 2 * (lv - 1) + g + 1)
                        if lv == 1:
                            pe.wait_ge(*(sem["tk_sb"], 2 * (j + 1)) if g else (sem["nmat"], 4 * (j + 1)))
                        for a in range(4):
                            mm(blk(2 * g)[0:P, a, :], u_(xbuf[:, g, :])[:, a, :], u_(ybuf[:, g, :])[:, a, :],
                               start=True, stop=True)
                        for a in range(4):
                            last = mm(blk(2 * g + 1)[0:P, a, :], u_(ybuf[:, g, :])[:, a, :], u_(xbuf[:, g, :])[:, a, :],
                                      start=True, stop=True)
                        last.then_inc(sem["z_ps"], 1)
                for g in range(2):
                    pe.wait_ge(sem["xd"], STEP0[j] + 2 * LEV_N[j] - 1 + g)
                    pe.wait_ge(sem["tk_sb"], 2 * (j + 1))
                    for a in range(4):
                        mm(ps[4 + 2 * g][0:P, a * 128:(a + 1) * 128], u_(xbuf[:, g, :])[:, a, :],
                           vbe[0:P, g, a * 128:(a + 1) * 128], start=True, stop=True)
                    for a in range(4):
                        last = mm(blk(5 + 2 * g)[:, a, :], kbe[0:P, g, a * 128:(a + 1) * 128], u_(xbuf[:, g, :])[:, a, :],
                                  start=True, stop=True)
                    last.then_inc(sem["u_ps"], 1)

            pe.wait_ge(sem["batch"], 6)
            pe.wait_ge(sem["s0"], 1)
            pe.wait_ge(sem["ld_state"], 16)
            def chunk(n):
                c = n // 2
                r0, R = (64 * (c % 2), 64) if c < 4 else (0, 32)
                ob = ps[O_BANKS[n % 3]][:, 0:4 * R].rearrange("p (h i) -> p h i", h=4)
                return c // 2, r0, R, sst[:, 0 if c < 4 else 1, :, :], ob, range(4 * (n % 2), 4 * (n % 2) + 4)

            def from_state(n):
                j, r0, R, st, ob, hs = chunk(n)
                t0, P = TILES[j]
                if n >= 2:
                    pe.wait_ge(sem["s_new"], n - 1)
                for a, hd in enumerate(hs):
                    last = mm(ps[3 * (n % 2)][0:P, a * 128:(a + 1) * 128], h[:, hd, t0:t0 + P], st[:, hd, :],
                              start=True, stop=True)
                last.then_inc(sem["ws_ps"], 1)
                if n >= 3:
                    pe.wait_ge(sem["o_sb"], n - 2)
                for a, hd in enumerate(hs):
                    mm(ob[:, a, :], st[:, hd, :], qf[:, hd, t0 + r0:t0 + r0 + R], start=(a == 0), stop=False)

            from_state(0)
            for n in range(10):
                j, r0, R, st, ob, hs = chunk(n)
                if n + 1 < 10:
                    from_state(n + 1)
                pe.wait_ge(sem["vn"], n + 1)
                for a, hd in enumerate(hs):
                    last = mm(ps[2 + 3 * (n % 2)][:, a * 128:(a + 1) * 128], kdec[r0:r0 + R, j, hd, :],
                              uu[r0:r0 + R, j, hd, :], start=True, stop=True)
                last.then_inc(sem["su_ps"], 1)
                for a, hd in enumerate(hs):
                    last = mm(ob[:, a, :], uu[r0:r0 + R, j, hd, :], att(j)[r0:r0 + R, hd, r0:r0 + R],
                              start=False, stop=(a == 3))
                last.then_inc(sem["o_ps"], 1)
            pe.wait_ge(sem["osq"], 1)
            for n in range(8):
                last = mm(ps[6][0:8, 0:T], C("pick")[:, 15 - n:23 - n], vf[:, n, :], start=(n == 0), stop=(n == 7))
            last.then_inc(sem["oss"], 1)
            for n in range(8):
                pe.wait_ge(sem["on"], max(n - 2, 1))
                mm(ps[n % 4][:, 0:T], ident[0:8, n:n + 1].broadcast_to([8, 128]), lbuf[0:8, 0, 0:T],
                   start=True, stop=True).then_inc(sem["oss"], 1)
            pe.wait_ge(sem["on"], 10)
            project(U_OUT1, 8, 8, ycat, "out_x")
            sum_squares(3)
            moe(1)
            sum_squares(4)

        @block.scalar
        def _(act):
            A = nc.scalar.activation
            L = Chain(act, "act")
            act.dma_start(sml[:, :], t["small"]).then_inc(sem["ld_small"], 16)
            for dst, src in ((cst[:, :], t["const"]), (x[:, :, :], t["x"])):
                act.dma_start(dst, src).then_inc(sem["ld_rest"], 16)
            act.wait_ge(sem["ld_small"], 16)
            act.wait_ge(sem["pad"], 1)
            L(A(condT[:, :, 0:2], M("cond").rearrange("p (k g) -> p k g", g=2), ACT.Silu), "cond")
            act.wait_ge(sem["lamn"], 1)
            L(A(lamw[:, 1, :], lamw[:, 0, :], ACT.Exp), "lame")

            def warm(func):
                A(idle[:, 0:1], C("eps")[:, 0:1], func)

            def norm_root(k):
                if k:
                    warm(ACT.Sqrt)
                act.wait_ge(sem["ss"], k + 1)
                if k:
                    act.wait_ge(sem["h"], 2 * k)
                L(A(rms[:, :], ps[7][:, 0:T], ACT.Sqrt, scale=1.0 / D, bias=C("eps")[:, 0:1]), "rms")

            def mod_rows(l, b, bank):
                act.wait_ge(sem["w_used"], MOD_U * l + 2 * (b + 1))
                if b >= 2:
                    act.wait_ge(sem["mod_t"], MOD_B * l + b - 1)
                A(modrow[:, b % 2, :], ps[bank][:, :], ACT.Copy).then_inc(sem["mod_row"], 1)

            for b in range(MOD_B):
                mod_rows(0, b, b % 2)
                if b == 0:
                    norm_root(0)
            act.dma_start(biasP0, t["biasP0"]).then_inc(sem["ld_att"], 16)
            act.dma_start(biasP1, t["biasP1"]).then_inc(sem["ld_att"], 16)
            act.dma_start(biasS[0:NS], t["biasS"]).then_inc(sem["ld_att"], 16)
            act.dma_start(ksT[:, :, 0:NP_], t["kcache"]).then_inc(sem["ld_att"], 16)
            act.dma_start(vcache, t["vcache"]).then_inc(sem["ld_att"], 16)
            act.wait_ge(sem["pad"], 2)
            for hf in range(2):
                for dst, src in ((bdr, t["wr"]), (bdi, t["wi"])):
                    act.dma_start(dst[64 * hf:64 * hf + 64, :, 64 * hf:64 * hf + 64],
                                  src[:, hf, :, :]).then_inc(sem["ld_att"], 16)
            for i in range(16):
                act.wait_ge(sem["proj_ps"], i + 1)
                src, c = ps[i % 4], i % 4
                if i < 4:
                    (A(xpad[:, c, 3:3 + NP_], src[:, 0:NP_], ACT.Copy))
                    A(xpad[:, c, SEG + 3:SEG + 3 + NS], src[:, NP_:T], ACT.Copy).then_inc(sem["proj_ev"], 1)
                elif i < 8:
                    A(gaT[:, c, :], src[:, 0:T], ACT.Copy).then_inc(sem["proj_ev"], 1)
                elif i < 12:
                    A(qT[:, c, :], src[:, 0:T], ACT.Copy).then_inc(sem["proj_ev"], 1)
                else:
                    (A(ksT[:, c, NP_:T], src[:, NP_:T], ACT.Copy))
                    A(kT[:, c, :], src[:, 0:T], ACT.Copy).then_inc(sem["proj_ev"], 1)
            act.wait_ge(sem["proj_ev"], 16)
            act.dma_start(t["k"], kT).then_inc(sem["st_mix"], 16)
            act.wait_ge(sem["v_ev"], 1)
            for j, (t0, P) in enumerate(TILES):
                act.dma_start(t["v"][t0:t0 + P, :], vtm[0:P, j, :]).then_inc(sem["st_mix"], 16)
            act.wait_ge(sem["gate_ps"], 1)
            for c in range(4):
                (A(rg[:, c, :], ps[c][:, 0:XW], ACT.Sigmoid, bias=M("abr")[:, c:c + 1]))
            act.wait_ge(sem["gate_ps"], 2)
            for c in range(3):
                (A(ig_[:, c, :], ps[4 + c][:, 0:XW], ACT.Sigmoid, bias=M("abi")[:, c:c + 1]))
            L(A(ig_[:, 3, :], ps[7][:, 0:XW], ACT.Sigmoid, bias=M("abi")[:, 3:4]), "gate_i")
            act.wait_ge(sem["lam"], 1)
            for c in range(4):
                (A(aa[:, c, :], rg[:, c, :], ACT.Exp, scale=lamw[:, 6, c:c + 1]))
            for c in range(4):
                ins = A(tt_[:, c, :], rg[:, c, :], ACT.Tanh, scale=lamw[:, 7, c:c + 1])
            L(ins, "lru_a")
            act.wait_ge(sem["lru_w"], 1)
            L(A(tt_[:, :, :], tt_[:, :, :], ACT.Sqrt), "lru_s")
            L(A(rg[:, :, 0:T], rg[:, :, 0:T], ACT.Tanh, scale=0.7978845608028654), "lru_g")
            for b in range(MOD_AHEAD // 2):
                mod_rows(1, b, 6)

            def softmax_exp(n):
                P, nk = TILES[n // 8][1], (128, 256, T)[n // 8]
                act.wait_ge(sem["s_sm"], n + 1)
                L.go(A(s_sb[0:P, n % 2, 0:nk], s_sb[0:P, n % 2, 0:nk], ACT.Exp, bias=mx[0:P, n % 2, 1:2],
                       accum_out=rsum[0:P, n % 2, :]), "p_exp")

            softmax_exp(0)
            for n in range(24):
                j, hd = n // 8, n % 8
                t0, P = TILES[j]
                if n + 1 < 24:
                    softmax_exp(n + 1)
                act.wait_ge(sem["pt_ps"], n + 1)
                if n >= 2:
                    act.wait_ge(sem["pv_ps"], n - 1)
                kts = [(0, 128)] if j == 0 else [(0, 128), (1, 128)] if j == 1 else [(0, 128), (1, 128), (2, 32)]
                for kt, K in kts:
                    ins = A(pT[0:K, n % 2, kt, 0:P], ps[2 + n % 2][0:K, kt * 128:kt * 128 + P], ACT.Copy)
                    if kt == kts[-1][0]:
                        ins.then_inc(sem["pt_sb"], 1)
                if n % 2 and n + MOD_AHEAD < MOD_U:
                    mod_rows(1, (n + MOD_AHEAD) // 2, 6)
                if n == 0:
                    act.wait_ge(sem["y_zero"], 16 * (T * TOPK // 128))
                act.wait_ge(sem["pv_ps"], n + 1)
                b = DHB * (hd % 2)
                A(ycat[b:b + DHB, 4 + hd // 2, t0:t0 + P], ps[4 + n % 2][b:b + DHB, 0:P], ACT.Copy)\
                    .then_inc(sem["pv_sb"], 1)

            def moe(l):
                B = NE * l
                warm(ACT.Sigmoid)
                act.wait_ge(sem["lg_ps"], l + 1)
                act.wait_ge(sem["lgz"], l + 1)
                act.wait_ge(sem["st_mix"], 16 * 4)
                if l:
                    act.wait_ge(sem["st_small"], 16 * 5)
                for j, (t0, P) in enumerate(TILES):
                    ins = A(lg[0:P, j, :], ps[6][0:P, j * 64:(j + 1) * 64], ACT.Copy)
                    L(ins, "act")
                L(A(score, lg, ACT.Sigmoid), "score")
                if l:
                    act.wait_ge(sem["h2_st"], 96 * l)
                for j, (t0, P) in enumerate(TILES):
                    act.wait_ge(sem["tm_ps"], 3 * l + j + 1)
                    for hf in range(2):
                        ins = A(gb[0:P, j, hf * 512:(hf + 1) * 512], ps[2 * j + hf][0:P, :], ACT.Copy)
                        L(ins, "tm_sb" if hf else None)
                        if hf:
                            act.dma_start(H2[t0:t0 + P, :], gb[0:P, j, :]).then_inc(sem["h2_st"], 16)
                act.wait_ge(sem["shu_ps"], 2 * l + 2)
                for j, (t0, P) in enumerate(TILES):
                    A(shs[0:P, j, :], ps[j][0:P, 0:DE], ACT.Silu)
                    L(A(shu_[0:P, j, :], ps[j][0:P, DE:2 * DE], ACT.Copy), "shu_sb")
                for j, (t0, P) in enumerate(TILES):
                    act.wait_ge(sem["sht_ps"], 3 * l + j + 1)
                    for a in range(2):
                        L(A(shT[:, j, a, 0:P], ps[3][:, a * 128:a * 128 + P], ACT.Copy),
                          "sht_sb" if a else None)
                for j, (t0, P) in enumerate(TILES):
                    act.wait_ge(sem["shd_ps"], 3 * l + j + 1)
                    for hf, bk in enumerate(((0, 1), (4, 5), (2, 3))[j]):
                        L(A(ysh[0:P, j, hf * 512:(hf + 1) * 512], ps[bk][0:P, :], ACT.Copy), "shd_sb" if hf else None)
                act.wait_ge(sem["h2_st"], 96 * l + 48)
                for j, (t0, P) in enumerate(TILES):
                    act.dma_start(SH[t0:t0 + P, :], ysh[0:P, j, :]).then_inc(sem["h2_st"], 16)

                def take(e, p, i):
                    act.wait_ge(sem["trx"], e + (B + 1))
                    if p[0]:
                        act.wait_ge(sem["up"], e + (B - 1))
                    A(xgT[:, p[1], 0:4, :], ps[4][:, 0:4 * CAP].rearrange("p (k s) -> p k s", k=4), ACT.Copy)\
                        .then_inc(sem["xta"], 1)

                def rows(e, p, old):
                    act.wait_ge(sem["dn"], e + (B + 1))
                    if old:
                        act.wait_ge(sem[f"ysc{p}"], e * 8 + 8 * (B - p))
                    A(yb[0:CAP, p, 0:512], ps[0][0:CAP, :], ACT.Copy).then_inc(sem["ya_e"], 1)

                def step(e0, i=None):
                    e = e0 if i is None else i * 2 + e0
                    if e0 + 1 < NE:
                        take(e + 1, (e0 + 1 >= 2, (e0 + 1) % 2), i)
                    act.wait_ge(sem["up"], e + (B + 1))
                    if e0:
                        act.wait_ge(sem["hd"], e + B)
                    A(silu_b[0:CAP], ps[2][0:CAP, 0:DE], ACT.Silu).then_inc(sem["sg"], 1)
                    if e0:
                        rows(e - 1, (e0 - 1) % 2, e0 >= 3)

                take(0, (False, 0), None)
                for e in range(3):
                    step(e)
                with act.Fori(0, (NE - 10) // 2) as i:
                    step(3, i)
                    step(4, i)
                for e in range(NE - 7, NE):
                    step(e)
                rows(NE - 1, (NE - 1) % 2, True)

                act.wait_ge(sem["flag"], l + 1)
                more = act.value_load(flagi[0:1, 0:1], min_val=0, max_val=1)
                with act.If(more > 0):
                    s = lambda n: sem[f"{n}{l}"]
                    with act.Fori(0, 2) as bb:
                        with act.Fori(0, NE) as e:
                            J = bb * NE + e
                            act.wait_ge(s("ovp"), J * 4 + 1)
                            for hf in range(2):
                                ins = A(xgT[:, 0, 4 * hf:4 * hf + 4, :],
                                        ps[4 + hf][:, 0:4 * CAP].rearrange("p (k s) -> p k s", k=4), ACT.Copy)
                            ins.then_inc(s("ova"), 1)
                            act.wait_ge(s("ovp"), J * 4 + 2)
                            A(silu_b[0:CAP], ps[2][0:CAP, 0:DE], ACT.Silu).then_inc(s("ova"), 1)
                            act.wait_ge(s("ovp"), J * 4 + 3)
                            A(hidT, ps[3][:, 0:2 * CAP].rearrange("p (a s) -> p a s", a=2), ACT.Copy).then_inc(s("ova"), 1)
                            act.wait_ge(s("ovp"), J * 4 + 4)
                            for hf in range(2):
                                ins = A(yb[0:CAP, 0, hf * 512:(hf + 1) * 512], ps[hf][0:CAP, :], ACT.Copy)
                            ins.then_inc(s("ova"), 1)

            norm_root(1)
            moe(0)
            norm_root(2)
            act.wait_ge(sem["padc"], 1)
            act.wait_ge(sem["acc_x"], 1)
            act.dma_start(sst[:, 1, :, :], t["S0"]).then_inc(sem["ld_state"], 16)
            def conv_silu(n):
                act.wait_ge(sem["cacc"], 4 * (n + 1))
                dst = (qf, kf, vf)[n // 2][:, 4 * (n % 2):4 * (n % 2) + 4, :]
                A(dst[:, :, 0:NP_], cacc[:, n % 2, :, 0:NP_], ACT.Silu)
                A(dst[:, :, NP_:T], cacc[:, n % 2, :, SEG:SEG + NS], ACT.Silu).then_inc(sem["csilu"], 1)

            act.wait_ge(sem["ab_e"], 1)
            L(A(spw[:, 1, :], spw[:, 0, :], ACT.Exp), "ab_act")
            L(A(spw[:, 5, 0:8], M("alog"), ACT.Exp), "ab_act")
            for j, (t0, P) in enumerate(TILES):
                ins = A(btm[0:P, j, :], ps[6][0:P, j * 16 + 8:j * 16 + 16], ACT.Sigmoid)
            L(ins, "ab_act")
            for i in range(32):
                n, c = i // 4, i % 4
                act.wait_ge(sem["proj_ps"], 16 + i + 1)
                src = ps[i % 4]
                if i < 24:
                    if n >= 2:
                        act.wait_ge(sem["cacc"], 4 * (n - 2) + c + 1)
                    A(raw[:, n % 2, c, 3:3 + NP_], src[:, 0:NP_], ACT.Copy)
                    A(raw[:, n % 2, c, SEG + 3:SEG + 3 + NS], src[:, NP_:T], ACT.Copy).then_inc(sem["proj_ev"], 1)
                else:
                    A(zf[:, i - 24, :], src[:, 0:T], ACT.Silu).then_inc(sem["proj_ev"], 1)
                if c == 3 and 1 <= n <= 6:
                    conv_silu(n - 1)
            act.wait_ge(sem["gcum_e"], 1)
            A(begc, gcol, ACT.Exp)
            L(A(kdcol, glast, ACT.Exp), "ab_act")
            act.wait_ge(sem["lss"], 1)
            L(A(lbuf[0:16, 0, 0:T], ps[0][0:16, 0:T], ACT.Sqrt, scale=C("l2", 16)[:, 0:1], bias=C("l2", 16)[:, 1:2]), "lrms")
            for j, (t0, P) in enumerate(TILES):
                blk = lambda b: ps[b][:, 0:4 * P].rearrange("p (h i) -> p h i", h=4)
                for g in range(2):
                    n = 2 * j + g
                    act.wait_ge(sem["gb_ps"], n + 1)
                    if n >= 2:
                        act.wait_ge(sem["tk_sb"], n - 1)
                    L(A(four(egb[:, g, :], P), blk(FIRST_BANKS[g][0]), ACT.Exp), "gb_e")
                    act.wait_ge(sem["ldif"], n + 1)
                    L(A(four(lbuf[:, g, :], P)[0:P], four(lbuf[:, g, :], P)[0:P], ACT.Exp), "lexp")
                for m in range(STEP0[j] + 2, STEP0[j] + 2 * LEV_N[j]):
                    act.wait_ge(sem["y_ps"], m + 1)
                    L.go(A(four(ybuf[:, m % 2, :], P)[0:P], blk(6 + m % 2)[0:P], ACT.Copy), "y_sb")
                for g in range(2):
                    act.wait_ge(sem["u_ps"], 2 * j + g + 1)
                    L(A(uu[0:P, j, 4 * g:4 * g + 4, :], ps[4 + 2 * g][0:P, :].rearrange("p (h v) -> p h v", h=4), ACT.Copy),
                      "act")
                    L(A(h[:, 4 * g:4 * g + 4, t0:t0 + P], blk(5 + 2 * g), ACT.Copy), "batch")
            for n in range(10):
                c, g = n // 2, n % 2
                t0 = TILES[c // 2][0]
                r0, R = (64 * (c % 2), 64) if c < 4 else (0, 32)
                act.wait_ge(sem["o_ps"], n + 1)
                L(A(ycat[:, 4 * g:4 * g + 4, t0 + r0:t0 + r0 + R],
                    ps[O_BANKS[n % 3]][:, 0:4 * R].rearrange("p (h i) -> p h i", h=4), ACT.Copy), "o_sb")
            act.wait_ge(sem["oss"], 1)
            L(A(lbuf[0:8, 0, 0:T], ps[6][0:8, 0:T], ACT.Sqrt, scale=1.0 / 128, bias=C("eps", 8)[:, 0:1]), "lrms")
            norm_root(3)
            moe(1)
            norm_root(4)

        @block.vector
        def _(dve):
            V = nc.vector
            L = Chain(dve, "dve")

            def tt(o, a, b, op):
                return V.tensor_tensor(o, a, b, op)

            def ts(o, a, s1, s2, op0, op1=None):
                return V.tensor_scalar(o, a, s1, s2, op0, op1) if op1 is not None else V.tensor_scalar(o, a, s1, None, op0)

            def stt(o, a, s, b, op0, op1):
                return V.scalar_tensor_tensor(out=o, in0=a, scalar=s, in1=b, op0=op0, op1=op1)

            def log1p(out, e, w1, w2):
                L(ts(w1, e, 2.0, None, ALU.add))
                L(V.reciprocal(w1, w1))
                L(tt(w1, w1, e, ALU.mult))
                L(tt(w2, w1, w1, ALU.mult))
                L(ts(out, w2, 1.0 / 17, None, ALU.mult))
                for k in (15, 13, 11, 9, 7, 5, 3):
                    L(stt(out, out, 1.0 / k, w2, ALU.add, ALU.mult))
                L(stt(out, out, 1.0, w1, ALU.add, ALU.mult))
                L(ts(out, out, 2.0, None, ALU.mult))

            L(V.memset(condT[:, :, :], 0.0), "pad")
            L(V.memset(bdr, 0.0))
            L(V.memset(bdi, 0.0), "pad")
            dve.wait_ge(sem["ld_small"], 16)
            dve.wait_ge(sem["ld_rest"], 32)
            L(V.memset(xpad[:, :, 0:3], 0.0))
            L(V.tensor_copy(xpad[:, :, SEG:SEG + 3], M("astate").rearrange("p (c j) -> p c j", c=4)))
            lam = M("alam")
            L(ts(lamw[:, 2, :], lam, -1.0, None, ALU.mult))
            L(tt(lamw[:, 0, :], lam, lamw[:, 2, :], ALU.min), "lamn")
            L(ts(lamw[:, 2, :], lamw[:, 2, :], 0.0, None, ALU.max))
            dve.wait_ge(sem["lame"], 1)
            log1p(lamw[:, 3, :], lamw[:, 1, :], lamw[:, 4, :], lamw[:, 5, :])
            L(tt(lamw[:, 3, :], lamw[:, 3, :], lamw[:, 2, :], ALU.add))
            L(ts(lamw[:, 7, :], lamw[:, 3, :], 8.0, None, ALU.mult))
            L(ts(lamw[:, 6, :], lamw[:, 3, :], -8.0, None, ALU.mult), "lam")

            def square(c):
                L.go(tt(h[:, c, :], x[:, c, :], x[:, c, :], ALU.mult), "sq")

            def vectors(l, bank):
                dve.wait_ge(sem["mod_t"], MOD_B * (l + 1))
                L(tt(mod[:, l, :, :], ps[bank][:, 0:96].rearrange("p (m g) -> p m g", g=2),
                     M("bmod")[:, l * 48:(l + 1) * 48].unsqueeze(2).broadcast_to([128, 48, 2]), ALU.add))
                for w in range(2):
                    g_ = M("norms")[:, (2 * l + w) * 8:(2 * l + w + 1) * 8].unsqueeze(2).broadcast_to([128, KC, 2])
                    L(stt(scale1[:, l, w, :, :], mod[:, l, 24 * w + 8:24 * w + 16, :], 1.0, g_, ALU.add, ALU.mult))

            def apply_norm(k, l, which):
                dve.wait_ge(sem["rms"], k + 1)
                L(V.reciprocal(rms[:, :], rms[:, :]))
                for hf in range(2):
                    cs = slice(4 * hf, 4 * hf + 4)
                    L(tt(h[:, cs, :], x[:, cs, :], rms[:, :].unsqueeze(1).broadcast_to([128, 4, T]), ALU.mult))
                    if k == 0 and hf == 0:
                        vectors(0, 2)
                    for c in range(4 * hf, 4 * hf + 4):
                        for g, (a, b) in enumerate(GROUPS):
                            if l is None:
                                ins = ts(h[:, c, a:b], h[:, c, a:b], M("norms")[:, 32 + c:33 + c], None, ALU.mult)
                            else:
                                ins = ts(h[:, c, a:b], h[:, c, a:b], scale1[:, l, which, c, g:g + 1],
                                         mod[:, l, 24 * which + c, g:g + 1], ALU.mult, ALU.add)
                            (L if c % 4 == 3 and g else L.go)(ins, "h" if c % 4 == 3 and g else None)

            for c in range(KC):
                square(c)
            apply_norm(0, 0, 0)
            cw = M("aconv").rearrange("p (c j) -> p c j", c=4)
            for c in range(4):
                dve.wait_ge(sem["proj_ev"], c + 1)
                L(ts(xc[:, c, :], xpad[:, c, 0:XW], cw[:, c, 0:1], M("aconvb")[:, c:c + 1], ALU.mult, ALU.add))
                for j in range(1, 4):
                    last = c == 3 and j == 3
                    L(stt(xc[:, c, :], xpad[:, c, j:j + XW], cw[:, c, j:j + 1], xc[:, c, :], ALU.mult, ALU.add),
                      "conv" if last else None)
            L(V.tensor_copy(cst3[:, :, 0, :], xpad[:, :, NP_:NP_ + 3]))
            L(V.tensor_copy(cst3[:, :, 1, :], xpad[:, :, SEG + NS:SEG + NS + 3]))
            dve.wait_ge(sem["proj_ev"], 8)
            L(tt(hh[:, :, 0:T], gaT, gaT, ALU.mult))
            L(ts(hh[:, :, 0:T], hh[:, :, 0:T], 0.044715, 1.0, ALU.mult, ALU.add))
            dve.wait_ge(sem["v_ps"], 2)
            for j, (t0, P) in enumerate(TILES):
                L(V.tensor_copy(vtm[0:P, j, :], ps[4 + j][0:P, :]), "v_ev" if j == 2 else None)
            dve.wait_ge(sem["ld_att"], 16 * 9)
            L(V.memset(biasP0[0:64, :, 64:128], -1e30))
            L(V.memset(biasP1[0:64, :, 192:256], -1e30))
            dve.wait_ge(sem["lru_a"], 1)
            L(tt(rg[:, :, 0:T], hh[:, :, 0:T], gaT, ALU.mult))
            L(tt(ig_, ig_, xc, ALU.mult))
            L(tt(xc, aa, aa, ALU.mult))
            L(stt(tt_, xc, 1.0, tt_, ALU.add, ALU.mult), "lru_w")
            dve.wait_ge(sem["lru_s"], 1)
            L(tt(tt_, tt_, ig_, ALU.mult))
            for c in range(4):
                L.go(V.tensor_tensor_scan(hh[:, c, 0:NP_], aa[:, c, 0:NP_], tt_[:, c, 0:NP_], 0.0, ALU.mult, ALU.add))
                L(V.tensor_tensor_scan(hh[:, c, SEG:SEG + NS], aa[:, c, SEG:SEG + NS], tt_[:, c, SEG:SEG + NS],
                                       M("ah0")[:, c:c + 1], ALU.mult, ALU.add))
            L(V.tensor_copy(hst[:, :, 0:1], hh[:, :, NP_ - 1:NP_]))
            L(V.tensor_copy(hst[:, :, 1:2], hh[:, :, SEG + NS - 1:SEG + NS]), "hst")
            dve.wait_ge(sem["lru_g"], 1)
            L(stt(gaT, rg[:, :, 0:T], 1.0, gaT, ALU.add, ALU.mult))
            dve.wait_ge(sem["y_zero"], 16 * (T * TOPK // 128))
            L(stt(ycat[:, 0:4, 0:NP_], hh[:, :, 0:NP_], 0.5, gaT[:, :, 0:NP_], ALU.mult, ALU.mult))
            L(stt(ycat[:, 0:4, NP_:T], hh[:, :, SEG:SEG + NS], 0.5, gaT[:, :, NP_:T], ALU.mult, ALU.mult), "ya")

            def softmax_max(n):
                j, hd = n // 8, n % 8
                P, nk = TILES[j][1], (128, 256, T)[j]
                bias = (biasP0, biasP1, biasS)[j]
                dve.wait_ge(sem["s_ps"], n + 1)
                if n >= 2:
                    dve.wait_ge(sem["pt_ps"], n - 1)
                L(stt(s_sb[0:P, n % 2, 0:nk], ps[n % 2][0:P, 0:nk], DHB ** -0.5, bias[0:P, hd, :], ALU.mult, ALU.add))
                L(V.reduce_max(mx[0:P, n % 2, 0:1], s_sb[0:P, n % 2, 0:nk], AX.X))
                L(ts(mx[0:P, n % 2, 1:2], mx[0:P, n % 2, 0:1], -1.0, None, ALU.mult), "s_sm")

            softmax_max(0)
            for n in range(24):
                P, nk = TILES[n // 8][1], (128, 256, T)[n // 8]
                if n + 1 < 24:
                    softmax_max(n + 1)
                dve.wait_ge(sem["p_exp"], n + 1)
                L(V.reciprocal(rsum[0:P, n % 2, :], rsum[0:P, n % 2, :]))
                L(ts(s_sb[0:P, n % 2, 0:nk], s_sb[0:P, n % 2, 0:nk], rsum[0:P, n % 2, :], None, ALU.mult), "p_nrm")

            def residual(base, l):
                for i in range(8):
                    dve.wait_ge(sem["out_ps"], base + i + 1)
                    for g, (a, b) in enumerate(GROUPS):
                        (L if g else L.go)(stt(x[:, i, a:b], ps[i % 4][:, a:b], mod[:, l, 16 + i, g:g + 1], x[:, i, a:b],
                                               ALU.mult, ALU.add), "out_x" if g else None)
                    square(i)

            vectors(1, 7)
            residual(0, 0)

            def moe(l):
                B = NE * l
                dve.wait_ge(sem["st_mix"], 16 * 4)
                if l:
                    dve.wait_ge(sem["st_small"], 16 * 5)
                L(V.memset(lg, 0.0), "lgz")
                L(V.memset(xgb, 0.0), "xgz")
                dve.wait_ge(sem["score"], l + 1)
                rb = M("rb")[:, l * 64:(l + 1) * 64].unsqueeze(1).broadcast_to([128, 3, NE])
                L(tt(selv, score, rb, ALU.add))
                for j in range(3):
                    for g in range(8):
                        ins = V.max(top2[:, j, g, :], selv[:, j, g * 8:(g + 1) * 8])
                        (L if (j, g) == (2, 7) else L.go)(ins)
                L(tt(gsc.unsqueeze(3), top2[:, :, :, 0:1], top2[:, :, :, 1:2], ALU.add))
                for j in range(3):
                    other = gsc[:, j, :].unsqueeze(1).broadcast_to([128, 8, 8])
                    own = gsc[:, j, :].unsqueeze(2).broadcast_to([128, 8, 8])
                    L(tt(gcmp[:, j], other, own, ALU.is_gt))
                    L(tt(geq[:, j], other, own, ALU.is_equal))
                    L(tt(geq[:, j], geq[:, j], C("lower").rearrange("p (a b) -> p a b", a=8), ALU.mult))
                    L(tt(gcmp[:, j], gcmp[:, j], geq[:, j], ALU.add))
                    L(V.reduce_sum(grk[:, j, :], gcmp[:, j], AX.X))
                L(ts(grk, grk, 4.0, None, ALU.is_lt))
                L(ts(gsc, grk, 1.0, 1e30, ALU.subtract, ALU.mult))
                for j in range(3):
                    e8 = lambda v: v[:, j, :].rearrange("p (g e) -> p g e", g=8)
                    L(tt(e8(tmp1), e8(selv), grk[:, j, :].unsqueeze(2).broadcast_to([128, 8, 8]), ALU.mult))
                    L(tt(e8(tmp1), e8(tmp1), gsc[:, j, :].unsqueeze(2).broadcast_to([128, 8, 8]), ALU.add))
                for j in range(3):
                    L(V.max(top8[:, j, :], tmp1[:, j, :]))
                    L(V.match_replace(out=tmp2[:, j, :], in_to_replace=top8[:, j, :], in_values=tmp1[:, j, :],
                                      imm_value=-3e30))
                L(tt(msk, tmp2, tmp1, ALU.is_lt), "mask")
                L(tt(gates, score, msk, ALU.mult))
                L(V.reduce_sum(gsum[:, :, :], gates, AX.X))
                L(V.reciprocal(gsum[:, :, :], gsum[:, :, :]))
                L(tt(gates, gates, gsum.broadcast_to([128, 3, NE]), ALU.mult))
                L(ts(gates, gates, 2.5, None, ALU.mult))
                L(V.tensor_copy(tg[:, :, :, 2:3], gates.unsqueeze(3)))
                for c in (3, 4):
                    L(tt(gates.unsqueeze(3), gates.unsqueeze(3), tg[:, :, :, c - 1:c], ALU.subtract))
                    L(V.tensor_copy(tg[:, :, :, c:c + 1], gates.unsqueeze(3)))
                for j in range(3):
                    L(V.tensor_copy(tg[:, j, :, 0:1], C("slot").unsqueeze(2).broadcast_to([128, NE, 1])))
                    L(V.memset(tg[:, j, :, 1:2], float(128 * j - LIM)))
                L(V.tensor_copy(slots, C("iota")[:, 0:CAP]))
                dve.wait_ge(sem["rank_ps"], l + 1)
                L(V.tensor_copy(cntf[:, 0:NE], ps[7][:, 192:256]))
                L(V.reduce_max(cntf[0:1, 64:65], cntf[0:1, 0:NE], AX.X))
                L(ts(flagi[0:1, 0:1], cntf[0:1, 64:65], float(CAP), None, ALU.is_gt), "flag")
                L(V.memset(rk, 0.0))
                for j, (t0, P) in enumerate(TILES):
                    L(V.tensor_copy(rk[0:P, j, :], ps[7][0:P, j * 64:(j + 1) * 64]))
                L(V.tensor_tensor_scan(start, ones[:, 0:NE], cntf[:, 0:NE], 0.0, ALU.mult, ALU.add))
                L(tt(start, start, cntf[:, 0:NE], ALU.subtract))
                L(ts(srow, start, C("slot"), None, ALU.add))
                L(ts(start, start, 1.0, None, ALU.add))
                base_ = start.unsqueeze(1).broadcast_to([128, 3, NE])
                L(tt(tmp1, rk, base_, ALU.add))
                L(stt(rk, rk, 1.0, msk, ALU.add, ALU.mult))
                L(ts(rk, rk, -1.0, None, ALU.add))
                L(V.tensor_copy(rkb_flat, rk_flat))

                def one_hots(g, sem_, wait):
                    if wait is not None:
                        dve.wait_ge(*wait)
                    for j, (t0, P) in enumerate(TILES):
                        o = selb[0:P, g % 2, j, :].rearrange("p (e s) -> p e s", e=8)
                        ins = tt(o, slots[0:P].unsqueeze(1).broadcast_to([P, 8, CAP]),
                                 rkb[0:P, j, 8 * g:8 * g + 8].unsqueeze(2).broadcast_to([P, 8, CAP]), ALU.is_equal)
                    ins.then_inc(sem_, 1)

                def sel_group(g):
                    one_hots(g, sem["sel"], (sem["sel_ps"], 8 * l + g - 1) if 8 * l + g >= 2 else None)

                def tables(chain, shift, e0, e1):
                    tabs = ps[6][0:CAP, 5 * e0:5 * e1].rearrange("p (e c) -> p e c", c=5)
                    f, ix = idxf[0:CAP, 0, e0:e1], idx[0:CAP, e0:e1]
                    chain(ts(f.unsqueeze(2), tabs[:, :, 0:1], float(LIM), None, ALU.add))
                    chain(tt(f.unsqueeze(2), f.unsqueeze(2), tabs[:, :, 1:2], ALU.add))
                    chain(V.tensor_copy(ix[:, :, 0:1], f.unsqueeze(2)))
                    gate = ix[:, :, 1:2].bitcast(F32)
                    chain(V.tensor_copy(gate, tabs[:, :, 2:3]))
                    chain(tt(gate, gate, tabs[:, :, 3:4], ALU.add))
                    chain(tt(gate, gate, tabs[:, :, 4:5], ALU.add))
                    chain(ts(f, f, float(LIM), 65536.0, ALU.is_ge, ALU.mult))
                    chain(tt(f, f, srow[0:CAP, e0:e1], ALU.add))
                    if shift is not None:
                        chain(tt(f, f, shift, ALU.add))
                    return V.tensor_copy(ix[:, :, 2:3], f.unsqueeze(2))

                sel_group(0)
                dve.wait_ge(sem["sel_ps"], 8 * l + 1)
                L(tables(L, None, 0, 8))

                def copy_gather(e, p, wait):
                    if wait:
                        dve.wait_ge(sem[f"xg{p}"], e * 8 + 8 * (B - p))
                    src = idx[0:CAP, e:e + 1, 0:1] if isinstance(e, int) else idx[0:CAP, bass.ds(e, 1), 0:1]
                    V.tensor_copy(icg[0:CAP, p:p + 1, :], src).then_inc(sem["ig"], 1)

                def copy_scatter(e, p, wait):
                    if wait:
                        dve.wait_ge(sem[f"ysc{p}"], e * 8 + 8 * (B - p))
                    src = idx[0:CAP, e:e + 1, 2:3] if isinstance(e, int) else idx[0:CAP, bass.ds(e, 1), 2:3]
                    V.tensor_copy(ics[0:CAP, p:p + 1, :], src).then_inc(sem["isx"], 1)

                def take(e, p, wait):
                    dve.wait_ge(sem["trx"], e + (B + 1))
                    if wait:
                        dve.wait_ge(sem["up"], e + (B - 1))
                    V.tensor_copy(xgT[:, p, 4:8, :], ps[5][:, 0:4 * CAP].rearrange("p (k s) -> p k s", k=4))\
                        .then_inc(sem["xtb"], 1)

                def hidden_T(e, wait):
                    dve.wait_ge(sem["trh"], e + (B + 1))
                    if wait:
                        dve.wait_ge(sem["dn"], e + B)
                    V.tensor_copy(hidT, ps[3][:, 0:2 * CAP].rearrange("p (a s) -> p a s", a=2)).then_inc(sem["ht"], 1)

                def rows(e, p, wait):
                    copy_scatter(e, p, wait)
                    dve.wait_ge(sem["dn"], e + (B + 1))
                    V.tensor_copy(yb[0:CAP, p, 512:1024], ps[1][0:CAP, :]).then_inc(sem["yb_e"], 1)

                def step(e0, i=None):
                    e = e0 if i is None else i * 2 + e0
                    if e0:
                        hidden_T(e - 1, e0 >= 2)
                    if e0 + 1 < NE:
                        take(e + 1, (e0 + 1) % 2, e0 + 1 >= 2)
                    if e0 + 3 < NE:
                        copy_gather(e + 3, (e0 + 1) % 2, True)
                    for g in SEL_STEPS[e0] if e0 < 3 else ():
                        sel_group(g)
                    if e0 >= NE - 5:
                        add_rows(e0 - (NE - 5))
                    dve.wait_ge(sem["sg"], e + (B + 1))
                    if e0:
                        dve.wait_ge(sem["trh"], e + B)
                    gate = idx[0:CAP, e, 1:2] if i is None else idx[0:CAP, bass.ds(e, 1), 1:2].rearrange("p a b -> p (a b)")
                    stt(hid[0:CAP], ps[2][0:CAP, DE:2 * DE], gate.bitcast(F32), silu_b[0:CAP], ALU.mult, ALU.mult)\
                        .then_inc(sem["hd"], 1)
                    if e0:
                        rows(e - 1, (e0 - 1) % 2, e0 >= 3)

                def add_rows(m):
                    if m == 0:
                        dve.wait_ge(sem["shd_sb"], 3 * (l + 1))
                        dve.wait_ge(sem["h2_st"], 96 * (l + 1))
                    for q in range(3 * m, 3 * m + 3):
                        j = COLLECT[q][1]
                        P = TILES[j][1]
                        dve.wait_ge(sem[f"got{q % 4}"], 16 * ((24 * l + q) // 4 + 1))
                        L(tt(ysh[0:P, j, :], ysh[0:P, j, :], gb[0:P, q % 4, :], ALU.add), "cb")

                copy_gather(0, 0, False)
                copy_gather(1, 1, False)
                sel_group(1)
                sel_group(2)
                take(0, 0, False)
                copy_gather(2, 0, True)
                for e in range(3):
                    step(e)
                dve.wait_ge(sem["sel_ps"], 8 * l + 8)
                L(tables(L, None, 8, NE))
                L(tt(tmp1, tmp1, msk, ALU.mult))
                for j in range(3):
                    L(V.max(rowif[:, j, :], tmp1[:, j, :]))
                L(ts(rowi[:, :, :], rowif, -1.0, None, ALU.add), "rowi")
                with dve.Fori(0, (NE - 10) // 2) as i:
                    step(3, i)
                    step(4, i)
                for e in range(NE - 7, NE):
                    step(e)
                hidden_T(NE - 1, True)
                rows(NE - 1, (NE - 1) % 2, True)
                for m in range(5, 8):
                    add_rows(m)

                dve.wait_ge(sem["flag"], l + 1)
                more = dve.value_load(flagi[0:1, 0:1], min_val=0, max_val=1)
                with dve.If(more > 0):
                    s = lambda n: sem[f"{n}{l}"]
                    for p in range(2):
                        dve.wait_ge(sem[f"ysc{p}"], 8 * (B + NE))
                    with dve.Fori(0, 2) as bb:
                        cnt = [0]

                        def chain(ins):
                            cnt[0] += 1
                            ins.then_inc(s("ovi"), 1)
                            dve.wait_ge(s("ovi"), bb * 11 + cnt[0])

                        dve.wait_ge(s("od"), bb * NE + 1)
                        dve.sem_inc(sem["passed"], 1)
                        chain(tt(rkb_flat, rk_flat, cst[:, bass.ds(bb * CAP + (CST["iota"][0] + CAP), 1)]
                                 .broadcast_to([128, 3 * NE]), ALU.subtract))
                        for g in range(8):
                            if g >= 2:
                                dve.wait_ge(s("osel_ps"), bb * 8 + (g - 1))
                            one_hots(g, s("osel"), None)
                        dve.wait_ge(s("osel_ps"), bb * 8 + 8)
                        chain(tables(chain, cst[0:CAP, bass.ds(bb * CAP + (CST["iota"][0] + CAP), 1)]
                                     .broadcast_to([CAP, NE]), 0, NE))
                        assert cnt[0] == 11, cnt
                        dve.sem_inc(sem["passed"], 1)
                        with dve.Fori(0, NE) as e:
                            J = bb * NE + e
                            dve.wait_ge(s("od"), J + 1)
                            V.tensor_copy(ico[0:CAP, :].unsqueeze(1), idx[0:CAP, bass.ds(e, 1), :]).then_inc(s("ovd"), 1)
                            dve.wait_ge(s("ova"), J * 4 + 2)
                            dve.wait_ge(s("ovd"), J * 2 + 1)
                            stt(hid[0:CAP], ps[2][0:CAP, DE:2 * DE], ico[0:CAP, 1:2].bitcast(F32), silu_b[0:CAP],
                                ALU.mult, ALU.mult)\
                                .then_inc(s("ovd"), 1)

                    for q, (k, j) in enumerate(COLLECT):
                        P = TILES[j][1]
                        dve.wait_ge(s("og"), 16 * (2 * NE + q + 1))
                        if q >= 3:
                            dve.wait_ge(s("ovd"), 4 * NE + q - 2)
                        tt(ysh[0:P, j, :], ysh[0:P, j, :], gb[0:P, 0, :], ALU.add).then_inc(s("ovd"), 1)

                for j, (t0, P) in enumerate(TILES):
                    dve.wait_ge(sem["acc_ps"], 3 * l + j + 1)
                    for k in range(KC):
                        ins = stt(x[:, k, t0:t0 + P], ps[2 * j + k // 4][:, (k % 4) * 128:(k % 4) * 128 + P],
                                  mod[:, l, 40 + k, (1 if j == 2 else 0):(2 if j == 2 else 1)], x[:, k, t0:t0 + P],
                                  ALU.mult, ALU.add)
                        (L if j == 2 else L.go)(ins, "acc_x" if (j, k) == (2, KC - 1) else None)
                        if j == 2:
                            square(k)

            apply_norm(1, 0, 1)
            moe(0)
            apply_norm(2, 1, 0)
            L(V.memset(raw[:, :, :, 0:3], 0.0), "padc")
            L(V.memset(sst[:, 0, :, :], 0.0), "s0")
            dve.wait_ge(sem["ab_ps"], 1)
            L(V.memset(spt, 0.0))
            L(V.memset(btm, 0.0))
            for j, (t0, P) in enumerate(TILES):
                L(tt(spt[0:P, j, :], ps[6][0:P, j * 16:j * 16 + 8], M("dtb", P), ALU.add))
            s3 = lambda v: v.rearrange("p (t h) -> p t h", t=3)
            L(ts(s3(spw[:, 2, :]), spt, -1.0, None, ALU.mult))
            L(tt(s3(spw[:, 0, :]), spt, s3(spw[:, 2, :]), ALU.min), "ab_e")
            L(ts(spt, spt, 0.0, None, ALU.max))
            dve.wait_ge(sem["ab_act"], 2)
            log1p(spw[:, 2, :], spw[:, 1, :], spw[:, 3, :], spw[:, 4, :])
            L(tt(spt, spt, s3(spw[:, 2, :]), ALU.add))
            L(stt(gtm, spt, -1.0, spw[:, 5, 0:8].unsqueeze(1).broadcast_to([128, 3, 8]), ALU.mult, ALU.mult), "ab_sb")
            cw1 = M("cconv").rearrange("p (c j) -> p c j", c=24)
            cs1 = M("cstate").rearrange("p (c j) -> p c j", c=24)
            for n in range(6):
                for c in range(4):
                    i = 4 * n + c
                    r = raw[:, n % 2, c, :]
                    dve.wait_ge(sem["proj_ev"], 16 + i + 1)
                    L(V.tensor_copy(r[:, SEG:SEG + 3], cs1[:, i, :]))
                    L(V.tensor_copy(cc3[:, i, 0, :], r[:, NP_:NP_ + 3]))
                    L(V.tensor_copy(cc3[:, i, 1, :], r[:, SEG + NS:SEG + NS + 3]), "cc" if i == 23 else None)
                    if n >= 2 and c == 0:
                        dve.wait_ge(sem["csilu"], n - 1)
                    o = cacc[:, n % 2, c, :]
                    L(ts(o, r[:, 0:XW], cw1[:, i, 0:1], None, ALU.mult))
                    for j in range(1, 4):
                        L(stt(o, r[:, j:j + XW], cw1[:, i, j:j + 1], o, ALU.mult, ALU.add), "cacc" if j == 3 else None)
            dve.wait_ge(sem["csilu"], 4)
            for n in range(4):
                src = (qf, kf)[n // 2][:, 4 * (n % 2):4 * (n % 2) + 4, :]
                L.go(tt(sqb[:, 4 * n:4 * n + 4, :], src, src, ALU.mult), "lsq")
            dve.wait_ge(sem["gcum_ps"], 1)
            L(V.memset(gcol, 0.0))
            L(V.memset(glast, 0.0))
            for j, (t0, P) in enumerate(TILES):
                L(V.tensor_copy(gcol[0:P, j, :], ps[6][0:P, 64 + j * 8:72 + j * 8]))
                L(tt(glast[0:P, j, :], ps[6][0:P, 96 + j * 8:104 + j * 8], gcol[0:P, j, :], ALU.subtract),
                  "gcum_e" if j == 2 else None)
            dve.wait_ge(sem["ab_act"], 4)
            L(tt(begc, begc, btm, ALU.mult), "gdec")
            dve.wait_ge(sem["csilu"], 6)
            dve.wait_ge(sem["lrms"], 1)
            L(V.reciprocal(lbuf[0:16, 0, 0:T], lbuf[0:16, 0, 0:T]), "qk_n")
            for n in range(16):
                v = (qf, kf)[n // 8][:, n % 8, :]
                dve.wait_ge(sem["lss"], n + 2)
                L.go(tt(v, v, ps[1 + n % 4][:, 0:T], ALU.mult), "qk_n")
            dve.wait_ge(sem["qk_n"], 17)
            for j, (t0, P) in enumerate(TILES):
                f = lambda b: four(b, P)[0:P]
                pb = lambda b: ps[b][0:P, 0:4 * P].rearrange("p (h i) -> p h i", h=4)
                for g in range(2):
                    n = 2 * j + g
                    hsl = slice(4 * g, 4 * g + 4)
                    bg, bb, bk, bq = FIRST_BANKS[g][0:4]
                    dve.wait_ge(sem["gb_e"], n + 1)
                    if j:
                        dve.wait_ge(sem["u_ps"], n - 1)
                    L(tt(f(lbuf[:, g, :]), pb(bg), gcol[0:P, j, hsl].unsqueeze(2).broadcast_to([P, 4, P]), ALU.subtract))
                    L(ts(f(lbuf[:, g, :]), f(lbuf[:, g, :]), 0.0, None, ALU.min), "ldif")
                    dve.wait_ge(sem["lexp"], n + 1)
                    L(tt(f(lbuf[:, g, :]), f(lbuf[:, g, :]), C("tri")[0:P, 0:P].unsqueeze(1).broadcast_to([P, 4, P]),
                         ALU.mult))
                    dve.wait_ge(sem["kk_ps"], n + 1)
                    L(tt(f(nbuf[:, g, :]), pb(bk), f(lbuf[:, g, :]), ALU.mult))
                    L(tt(f(nbuf[:, g, :]), f(nbuf[:, g, :]), pb(bb), ALU.mult), "nmat")
                    L.go(tt(att(j)[0:P, hsl, :], pb(bq), f(lbuf[:, g, :]), ALU.mult), "nmat")
                for g in range(2):
                    dve.wait_ge(sem["y_ps"], STEP0[j] + g + 1)
                    one = ident[0:P, 0:P].unsqueeze(1).broadcast_to([P, 4, P])
                    L.go(tt(f(dbuf[:, g, :]), one, pb(6 + g), ALU.subtract))
                    L.go(tt(f(xbuf[:, g, :]), one, f(ybuf[:, g, :]), ALU.subtract), "xd")
                for g in range(2):
                    n, hsl, (btk, btv) = 2 * j + g, slice(4 * g, 4 * g + 4), FIRST_BANKS[g][4:6]
                    eg = four(egb[:, g, :], P)
                    L.go(tt(qf[:, hsl, t0:t0 + P], qf[:, hsl, t0:t0 + P], eg, ALU.mult))
                    for cc, col in ((2 * j, 63), (2 * j + 1, 127)) if j < 2 else ((4, 31),):
                        L.go(V.tensor_copy(sdec[:, cc, hsl].unsqueeze(2), eg[:, :, col:col + 1]))
                    dve.wait_ge(sem["tk_ps"], n + 1)
                    tk = lambda b: ps[b][0:P, :].rearrange("p (h d) -> p h d", h=4)
                    bc = lambda v: v[0:P, j, hsl].unsqueeze(2).broadcast_to([P, 4, 128])
                    L.go(tt(kbe[0:P, g, :].rearrange("p (h d) -> p h d", h=4), tk(btk), bc(begc), ALU.mult))
                    L.go(tt(kdec[0:P, j, hsl, :], tk(btk), bc(kdcol), ALU.mult))
                    L(tt(vbe[0:P, g, :].rearrange("p (h d) -> p h d", h=4), tk(btv), bc(btm), ALU.mult), "tk_sb")
                for m in range(STEP0[j] + 2, STEP0[j] + 2 * LEV_N[j]):
                    g = m % 2
                    dve.wait_ge(sem["z_ps"], PROD0[j] + m - STEP0[j] - 1)
                    dve.wait_ge(sem["xd"], m - 1)
                    L.go(tt(f(dbuf[:, g, :]), f(dbuf[:, g, :]), pb(2 * g), ALU.subtract))
                    L.go(tt(f(xbuf[:, g, :]), f(xbuf[:, g, :]), pb(2 * g + 1), ALU.subtract), "xd")
            dve.wait_ge(sem["batch"], 6)
            for n in range(10):
                c, g = n // 2, n % 2
                j = c // 2
                r0, R = (64 * (c % 2), 64) if c < 4 else (0, 32)
                hsl = slice(4 * g, 4 * g + 4)
                st = sst[:, 0 if c < 4 else 1, :, :]
                dve.wait_ge(sem["ws_ps"], n + 1)
                L(tt(uu[r0:r0 + R, j, hsl, :], uu[r0:r0 + R, j, hsl, :],
                     ps[3 * (n % 2)][r0:r0 + R, :].rearrange("p (h v) -> p h v", h=4), ALU.subtract), "vn")
                dve.wait_ge(sem["su_ps"], n + 1)
                for a in range(4):
                    hd = 4 * g + a
                    (L if a == 3 else L.go)(stt(st[:, hd, :], st[:, hd, :], sdec[:, c, hd:hd + 1], ps[2 + 3 * (n % 2)][:, a * 128:(a + 1) * 128],
                          ALU.mult, ALU.add), "s_new" if a == 3 else None)
            dve.wait_ge(sem["o_sb"], 10)
            L(tt(vf, ycat[:, :, :], ycat[:, :, :], ALU.mult), "osq")
            dve.wait_ge(sem["lrms"], 2)
            L(V.reciprocal(lbuf[0:8, 0, 0:T], lbuf[0:8, 0, 0:T]), "on")
            for n in range(8):
                dve.wait_ge(sem["oss"], n + 2)
                L.go(tt(ycat[:, n, :], ycat[:, n, :], ps[n % 4][:, 0:T], ALU.mult), "on")
            dve.wait_ge(sem["on"], 9)
            L(stt(ycat[:, :, :], ycat[:, :, :], M("cnorm"), zf, ALU.mult, ALU.mult), "on")
            residual(8, 1)
            apply_norm(3, 1, 1)
            moe(1)
            apply_norm(4, None, None)

        @block.gpsimd
        def _(po):
            po.memset(ycat[:, 0:4, 0:256], 0.0).then_inc(sem["zero"], 1)
            po.wait_ge(sem["zero"], 1)
            po.wait_ge(sem["proj_ev"], 1)
            for n in range(T * TOPK // 128):
                po.dma_start(Y[n * 128:(n + 1) * 128, :].rearrange("p (a b) -> p a b", a=4), ycat[:, 0:4, 0:256])\
                    .then_inc(sem["y_zero"], 16)
            po.wait_ge(sem["conv"], 1)
            po.wait_ge(sem["hst"], 1)
            po.dma_start(t["aconv"], cst3[:, :, :, :]).then_inc(sem["st_small"], 16)
            po.dma_start(t["ah"], hst[:, :, :]).then_inc(sem["st_small"], 16)

            def gather(index, dst, src, bound):
                return po.indirect_dma_start(dst, None, src, bass.IndirectOffsetOnAxis(ap=index, axis=0),
                                             bounds_check=bound, oob_is_err=False)

            def scatter(index, dst, src, bound):
                return po.indirect_dma_start(dst, bass.IndirectOffsetOnAxis(ap=index, axis=0), src, None,
                                             bounds_check=bound, oob_is_err=False)

            def moe(l):
                B = NE * l
                for j, (t0, P) in enumerate(TILES):
                    po.wait_ge(sem["shu_sb"], 3 * l + j + 1)
                    po.tensor_tensor(shh_[0:P, j, :], shs[0:P, j, :], shu_[0:P, j, :], ALU.mult)\
                        .then_inc(sem["shh"], 1)
                po.wait_ge(sem["h2_st"], 96 * l + 48)
                po.wait_ge(sem["xgz"], l + 1)

                def fetch(e, p, wait):
                    if wait:
                        po.wait_ge(sem["trx"], e + (B - 1))
                    po.wait_ge(sem["ig"], e + (B + 1))
                    po.sem_inc(sem["passed"], 1)
                    gather(icg[0:CAP, p, 0:1], xgb[0:CAP, p, :], H2, T - 1).then_inc(sem[f"xg{p}"], 16)

                def store(e, p):
                    po.wait_ge(sem["isx"], e + (B + 1))
                    po.wait_ge(sem["ya_e"], e + (B + 1))
                    po.wait_ge(sem["yb_e"], e + (B + 1))
                    po.sem_inc(sem["passed"], 1)
                    scatter(ics[0:CAP, p, 0:1], Y, yb[0:CAP, p, :], T * TOPK - 1).then_inc(sem[f"ysc{p}"], 16)

                def step(e0, i=None):
                    e = e0 if i is None else i * 2 + e0
                    if e0 + 3 < NE:
                        fetch(e + 3, (e0 + 1) % 2, True)
                    if e0:
                        store(e - 1, (e0 - 1) % 2)
                    if e0 >= NE - 6:
                        collect(e0 - (NE - 6))

                def collect(m):
                    for p in range(2):
                        po.wait_ge(sem[f"ysc{p}"], 8 * B + 16 * ((NE - TOPK + m - p) // 2 + 1))
                    if m == 0:
                        po.wait_ge(sem["rowi"], l + 1)
                    for q in range(3 * m, 3 * m + 3):
                        k, j = COLLECT[q]
                        P = TILES[j][1]
                        if q >= 4:
                            po.wait_ge(sem["cb"], 24 * l + q - 3)
                        gather(rowi[0:P, j, k:k + 1], gb[0:P, q % 4, :], Y, T * TOPK - 1).then_inc(sem[f"got{q % 4}"], 16)

                fetch(0, 0, False)
                fetch(1, 1, False)
                fetch(2, 0, True)
                for e in range(3):
                    step(e)
                with po.Fori(0, (NE - 10) // 2) as i:
                    step(3, i)
                    step(4, i)
                for e in range(NE - 7, NE):
                    step(e)
                store(NE - 1, (NE - 1) % 2)
                collect(6)
                collect(7)

                po.wait_ge(sem["flag"], l + 1)
                more = po.value_load(flagi[0:1, 0:1], min_val=0, max_val=1)
                with po.If(more > 0):
                    s = lambda n: sem[f"{n}{l}"]
                    po.sem_inc(s("od"), 1)
                    with po.Fori(0, 2) as bb:
                        with po.Fori(0, NE) as e:
                            J = bb * NE + e
                            po.wait_ge(s("ovd"), J * 2 + 1)
                            po.sem_inc(sem["passed"], 1)
                            gather(ico[0:CAP, 0:1], xgb[0:CAP, 0, :], H2, T - 1).then_inc(s("og"), 16)
                            po.wait_ge(s("ova"), J * 4 + 4)
                            po.sem_inc(sem["passed"], 1)
                            scatter(ico[0:CAP, 2:3], Y, yb[0:CAP, 0, :], T * TOPK - 1).then_inc(s("osc"), 16)
                            po.wait_ge(s("osc"), J * 16 + 16)
                            po.sem_inc(s("od"), 1)
                    po.wait_ge(sem["cb"], 24 * (l + 1))
                    for j, (t0, P) in enumerate(TILES):
                        po.dma_start(ysh[0:P, j, :], SH[t0:t0 + P, :]).then_inc(s("osc"), 16)
                        po.wait_ge(s("osc"), 16 * (2 * NE + j + 1))
                    for q, (k, j) in enumerate(COLLECT):
                        P = TILES[j][1]
                        if q:
                            po.wait_ge(s("ovd"), 4 * NE + q)
                        gather(rowi[0:P, j, k:k + 1], gb[0:P, 0, :], Y, T * TOPK - 1).then_inc(s("og"), 16)

            moe(0)
            for j, (t0, P) in enumerate(TILES):
                f = lambda v: v[0:P, 0:4 * P].rearrange("p (h i) -> p h i", h=4)
                for lv in range(LEV_N[j]):
                    for g in range(2):
                        m = STEP0[j] + 2 * lv + g
                        if lv == 0:
                            po.wait_ge(sem["nmat"], 2 * (2 * j + g) + 1)
                        if lv == 0 and j:
                            po.wait_ge(sem["u_ps"], 2 * j)
                        elif lv >= 2:
                            po.wait_ge(sem["y_ps"], m - 1)
                        mk = C("mask")[0:P, lv * 128:lv * 128 + P].unsqueeze(1).broadcast_to([P, 4, P])
                        dst = ybuf if lv == 0 else ubuf
                        po.tensor_tensor(f(dst[:, g, :]), f(nbuf[:, g, :]), mk, ALU.mult).then_inc(sem["um"], 1)
            po.wait_ge(sem["cc"], 1)
            po.dma_start(t["cconv"], cc3[:, :, :, :]).then_inc(sem["st_small"], 16)
            po.wait_ge(sem["s_new"], 10)
            for g in range(2):
                po.dma_start(t["S"][g, :, :, :], sst[:, g, :, :]).then_inc(sem["st_small"], 16)
            po.wait_ge(sem["st_small"], 16 * 5)
            moe(1)


def constants():
    c = np.zeros((128, CST_N), np.float32)
    m, i = np.arange(128)[:, None], np.arange(128)[None, :]

    def put(name, v):
        c[:, CST[name][0]:CST[name][1]] = v

    put("ident", m == i)
    put("ones", 1)
    put("tri", (m <= i) & (m // CH == i // CH))
    put("same", m // CH == i // CH)
    put("mask", np.concatenate([(m // (2 * s) == i // (2 * s)) & (i // s % 2 == 1) & (m // s % 2 == 0)
                                for s in LEVELS], axis=1))
    put("before", m < i)
    g = np.arange(8)
    put("lower", (g[None, :] < g[:, None]).reshape(1, 64))
    put("iota", np.arange(T))
    put("slot", m)
    put("fold", m % 32 == np.arange(2))
    put("eps", np.array([EPS, 128 * EPS]))
    put("pick", np.arange(31) == 15)
    put("l2", np.where(m < HC, 128.0, 1.0) * np.array([1.0, EPS]))
    return c


def kernel(**inputs):
    import concourse.bacc as bacc
    from concourse.bass_utils import run_bass_kernel_spmd

    a = {k: np.asarray(v) for k, v in inputs.items()}

    def chunks(v):
        v = v.reshape(v.shape[:-1] + (-1, 128))
        return np.moveaxis(v, -1, 0).reshape(128, -1)

    def tiles(w):
        return np.ascontiguousarray(w.reshape(KC, 128, -1, 2, 128).transpose(2, 1, 3, 0, 4)).reshape(-1, 128, UNIT)

    def halves(w):
        return np.ascontiguousarray(w.reshape(2, 4, 128, 512).transpose(0, 2, 1, 3)).reshape(2, 128, UNIT)

    def expert_units(l):
        gu = np.concatenate([np.concatenate([a["e_w_gate"][l], a["s_w_gate"][l][None]]),
                             np.concatenate([a["e_w_up"][l], a["s_w_up"][l][None]])], axis=-1)
        dn = np.concatenate([a["e_w_down"][l], a["s_w_down"][l][None]])
        out = np.empty((NE + 1, 3, 128, UNIT), np.float32)
        out[:, 0:2] = gu.reshape(NE + 1, 2, 4, 128, 512).transpose(0, 1, 3, 2, 4).reshape(NE + 1, 2, 128, UNIT)
        out[:, 2] = dn.reshape(NE + 1, 2, 128, D).transpose(0, 2, 1, 3).reshape(NE + 1, 128, UNIT)
        return out.reshape(-1, 128, UNIT)

    small = np.zeros((128, SML_N), np.float32)

    def put(name, v):
        small[:, SML[name][0]:SML[name][1]] = v

    cond = np.stack([a["c_prompt"][0], a["c_sample"][0]])
    put("cond", cond.reshape(2, KC, 128).transpose(2, 1, 0).reshape(128, 16))
    norms = np.stack([a["norm1_g"][0], a["norm2_g"][0], a["norm1_g"][1], a["norm2_g"][1], a["final_g"]])
    put("norms", chunks(norms))
    put("bmod", chunks(a["b_mod"]))
    put("aconv", a["a_conv_w"][0].reshape(4, 4, 128).transpose(2, 1, 0).reshape(128, 16))
    put("aconvb", chunks(a["a_conv_b"][0]))
    put("abr", chunks(a["a_b_r"][0]))
    put("abi", chunks(a["a_b_i"][0]))
    put("alam", chunks(a["a_lambda"][0]))
    put("ah0", chunks(a["state_a_h"][0, 0]))
    put("astate", a["state_a_conv"][0, 0].reshape(3, 4, 128).transpose(2, 1, 0).reshape(128, 12))
    put("cconv", a["c_conv_w"][0].reshape(4, 24, 128).transpose(2, 1, 0).reshape(128, 96))
    put("cstate", a["state_c_conv"][0, 0].reshape(3, 24, 128).transpose(2, 1, 0).reshape(128, 72))
    put("cnorm", a["c_norm_g"][0][:, None])
    put("alog", a["c_A_log"][0][None])
    put("dtb", a["c_dt_bias"][0][None])
    put("rb", a["router_bias"].reshape(1, 128))
    put("router", a["router_w"].reshape(2, KC, 128, NE).transpose(2, 0, 1, 3).reshape(128, 1024))
    w1 = a["w_in1"][0]
    put("wab", w1[:, 4096:4112].reshape(KC, 128, 16).transpose(1, 0, 2).reshape(128, 128))

    table = a["b_rel_bias"][0]

    def band(q0, nq, nk):
        rel = np.clip((q0 + np.arange(nq))[:, None] - np.arange(nk)[None, :], -128, 128) + 128
        return np.ascontiguousarray(table[:, rel].transpose(1, 0, 2))

    x = np.concatenate([a["x_prompt"][0], a["x_sample"][0]])
    w0 = a["w_in0"][0]
    arrays = {
        "small": small, "const": constants(),
        "x": np.ascontiguousarray(x.reshape(T, KC, 128).transpose(2, 1, 0)),
        "biasP0": band(0, 128, 128), "biasP1": band(128, 128, 256), "biasS": band(256, NS, T),
        "kcache": np.ascontiguousarray(a["cache_b_k"][0, 0].reshape(NP_, 4, 128).transpose(2, 1, 0)),
        "vcache": np.ascontiguousarray(a["cache_b_v"][0, 0].reshape(2, 128, 512).transpose(1, 0, 2)),
        "wr": np.ascontiguousarray(a["a_w_r"][0].reshape(4, 2, 64, 64).transpose(2, 1, 0, 3)),
        "wi": np.ascontiguousarray(a["a_w_i"][0].reshape(4, 2, 64, 64).transpose(2, 1, 0, 3)),
        "S0": np.ascontiguousarray(a["state_c_S"][0, 0].transpose(1, 0, 2)),
        "wmod": np.ascontiguousarray(a["w_mod"].reshape(2, 2, 4, 128, MOD_B, 512).transpose(0, 4, 1, 3, 2, 5))
        .reshape(2 * MOD_U, 128, UNIT),
        "win0": np.concatenate([tiles(w0[:, 0:2048]), halves(w0[:, 2048:2560])]),
        "wout0": tiles(a["w_out0"][0]),
        "win1": tiles(w1[:, 0:4096]),
        "wout1": tiles(a["w_out1"][0]),
        "wexp": np.concatenate([expert_units(0), expert_units(1)]),
    }
    outs = {"y": (128, KC, T), "k": (128, 4, T), "v": (T, 512), "aconv": (128, 4, 2, 3), "ah": (128, 4, 2),
            "cconv": (128, 24, 2, 3), "S": (2, 128, HC, 128)}
    nc = bacc.Bacc("TRN2", target_bir_lowering=False, num_devices=1)
    t = {n: nc.dram_tensor(f"in_{n}", v.shape, F32, kind="ExternalInput").ap() for n, v in arrays.items()}
    t.update({n: nc.dram_tensor(f"out_{n}", s, F32, kind="ExternalOutput").ap() for n, s in outs.items()})
    t["H2"] = nc.dram_tensor("h_rows", (T, D), F32, kind="Internal").ap()
    t["SH"] = nc.dram_tensor("shared_rows", (T, D), F32, kind="Internal").ap()
    t["Y"] = nc.dram_tensor("expert_rows", (T * TOPK, D), F32, kind="Internal").ap()
    build(nc, t)
    r = run_bass_kernel_spmd(nc, [{f"in_{n}": v for n, v in arrays.items()}], core_ids=[0]).results[0]
    r = {n: r[f"out_{n}"] for n in outs}

    y = r["y"].transpose(2, 1, 0).reshape(T, D)
    k = r["k"].transpose(2, 1, 0).reshape(T, HB, DHB)
    v = r["v"].reshape(T, HB, DHB)
    conv_a = r["aconv"].transpose(2, 3, 1, 0).reshape(2, 3, 512)
    h_a = r["ah"].transpose(2, 1, 0).reshape(2, 512)
    conv_c = r["cconv"].transpose(2, 3, 1, 0).reshape(2, 3, 3072)
    S = r["S"].transpose(0, 2, 1, 3)
    c = np.ascontiguousarray
    return (c(y[None, 0:NP_]), c(y[None, NP_:T]), c(k[None, None, 0:NP_]), c(k[None, None, NP_:T]),
            c(v[None, None, 0:NP_]), c(v[None, None, NP_:T]), c(conv_a[None, 0:1]), c(conv_a[None, 1:2]),
            c(h_a[None, 0:1]), c(h_a[None, 1:2]), c(conv_c[None, 0:1]), c(conv_c[None, 1:2]),
            c(S[None, 0:1]), c(S[None, 1:2]))
```
